# Optimizing a Trainium2 kernel written in Bass

```python
import math
import jax
import jax.numpy as jnp
from jax import lax
import numpy as np

D_MODEL = 1024
BATCH = 1
SEQ = 1024
DEPTH = 1
DEC_BATCH = 8
DEC_SEQ = 16
PAST_LEN = 1024

CHUNK = 64
A_PAST_CHUNKS = 8
A_BAND = A_PAST_CHUNKS + 1
A_REACH = A_PAST_CHUNKS * CHUNK
N_HEADS_A = 8
HEAD_DIM_A = 64
WIDTH_A = N_HEADS_A * HEAD_DIM_A
REL_CLIP = 128
N_HEADS_B = 4
HEAD_DIM_B = 128
WIDTH_B = N_HEADS_B * HEAD_DIM_B
CONV_W = 4
B_CONV_DIM = 3 * WIDTH_B
N_HEADS_X = 4
HEAD_DIM_X = D_MODEL // N_HEADS_X
N_MEM = 256
D_FF = 2816
EPS = 1e-6
OFF_A = 0
OFF_B = OFF_A + 3 * WIDTH_A
OFF_Z = OFF_B + B_CONV_DIM
OFF_BETA = OFF_Z + WIDTH_B
OFF_DECAY = OFF_BETA + N_HEADS_B
OFF_GATE = OFF_DECAY + N_HEADS_B
N_IN = OFF_GATE + 2 * D_MODEL

kernel_name = 'hybrid_stream_band_attn_gated_delta_step'

def rmsnorm(x, g):
    xf = x.astype(jnp.float32)
    y = xf * lax.rsqrt(jnp.mean(xf * xf, axis=-1, keepdims=True) + EPS)
    return (y * g.astype(jnp.float32)).astype(x.dtype)

def l2norm(x):
    xf = x.astype(jnp.float32)
    return (xf * lax.rsqrt(jnp.sum(xf * xf, axis=-1, keepdims=True) + EPS)).astype(x.dtype)

def swiglu_ffn(x, g, w_gate, w_up, w_down):
    h = rmsnorm(x, g)
    return (jax.nn.silu(h @ w_gate) * (h @ w_up)) @ w_down

def rel_bias(table, d):
    idx = jnp.clip(d, -REL_CLIP, REL_CLIP) + REL_CLIP
    return table[:, idx].astype(jnp.float32)

def band_attention_prompt(q, k, v, table):
    bsz, s, h, dh = q.shape
    nc = s // CHUNK
    pad = ((0, 0), (A_REACH, 0), (0, 0), (0, 0))
    kp = jnp.pad(k, pad)
    vp = jnp.pad(v, pad)
    krel = jnp.arange(A_BAND * CHUNK) - A_REACH
    qrel = jnp.arange(CHUNK)
    bias = rel_bias(table, qrel[:, None] - krel[None, :])
    scale = HEAD_DIM_A ** -0.5

    def one_chunk(c):
        start = c * CHUNK
        qc = lax.dynamic_slice_in_dim(q, start, CHUNK, axis=1)
        kb = lax.dynamic_slice_in_dim(kp, start, A_BAND * CHUNK, axis=1)
        vb = lax.dynamic_slice_in_dim(vp, start, A_BAND * CHUNK, axis=1)
        sc = jnp.einsum('bqhd,bkhd->bhqk', qc, kb).astype(jnp.float32) * scale + bias
        valid = (start + krel) >= 0
        sc = jnp.where(valid[None, None, None, :], sc, -jnp.inf)
        p = jax.nn.softmax(sc, axis=-1).astype(v.dtype)
        return jnp.einsum('bhqk,bkhd->bqhd', p, vb)

    out = lax.map(one_chunk, jnp.arange(nc))
    return out.transpose(1, 0, 2, 3, 4).reshape(bsz, s, h, dh)

def band_attention_sample(q, k_new, v_new, k_cache, v_cache, table):
    t = q.shape[1]
    p_len = k_cache.shape[1]
    kk = jnp.concatenate([k_cache, k_new], axis=1)
    vv = jnp.concatenate([v_cache, v_new], axis=1)
    kpos = jnp.concatenate([jnp.arange(-p_len, 0), jnp.arange(t)])
    bias = rel_bias(table, jnp.arange(t)[:, None] - kpos[None, :])
    sc = jnp.einsum('bqhd,bkhd->bhqk', q, kk).astype(jnp.float32) * (HEAD_DIM_A ** -0.5) + bias
    p = jax.nn.softmax(sc, axis=-1).astype(vv.dtype)
    return jnp.einsum('bhqk,bkhd->bqhd', p, vv)

def causal_conv(x, prev, w):
    t = x.shape[1]
    xp = jnp.concatenate([prev, x], axis=1)
    y = xp[:, 0:t] * w[0]
    for j in range(1, CONV_W):
        y = y + xp[:, j:j + t] * w[j]
    return jax.nn.silu(y), xp[:, -(CONV_W - 1):]

def gated_delta_rule(q, k, v, g, beta, s0, blk):
    bsz, t, h, dk = q.shape
    dv = v.shape[-1]
    n = t // blk
    f32 = jnp.float32

    def blocks(a):
        return a.astype(f32).reshape(bsz, n, blk, h, -1).transpose(1, 0, 3, 2, 4)

    qc, kc, vc = blocks(q), blocks(k), blocks(v)
    gc = jnp.cumsum(blocks(g[..., None])[..., 0], axis=-1)
    bc = blocks(beta[..., None])[..., 0]
    incl = jnp.tril(jnp.ones((blk, blk), bool))
    strict = jnp.tril(jnp.ones((blk, blk), bool), -1)
    decay = jnp.exp(jnp.where(incl, gc[..., :, None] - gc[..., None, :], -jnp.inf))
    kbeta = kc * bc[..., None]
    a_mat = jnp.where(strict, jnp.einsum('nbhid,nbhjd->nbhij', kbeta, kc) * decay, 0.0) + jnp.eye(blk, dtype=f32)
    rhs = jnp.concatenate([vc * bc[..., None], kbeta * jnp.exp(gc)[..., None]], axis=-1)
    sol = lax.linalg.triangular_solve(a_mat, rhs, left_side=True, lower=True, unit_diagonal=True)
    u, w = sol[..., :dv], sol[..., dv:]
    intra = jnp.einsum('nbhid,nbhjd->nbhij', qc, kc) * decay
    qg = qc * jnp.exp(gc)[..., None]
    kdec = kc * jnp.exp(gc[..., -1:] - gc)[..., None]
    glast = jnp.exp(gc[..., -1])

    def step(s, xs):
        u_n, w_n, qg_n, intra_n, kdec_n, gl_n = xs
        v_n = u_n - jnp.einsum('bhlk,bhkv->bhlv', w_n, s)
        o = jnp.einsum('bhlk,bhkv->bhlv', qg_n, s) + jnp.einsum('bhij,bhjv->bhiv', intra_n, v_n)
        s = s * gl_n[..., None, None] + jnp.einsum('bhlk,bhlv->bhkv', kdec_n, v_n)
        return s, o

    s_fin, o = lax.scan(step, s0.astype(f32), (u, w, qg, intra, kdec, glast))
    o = o.transpose(1, 0, 3, 2, 4).reshape(bsz, t, h, dv)
    return o.astype(v.dtype), s_fin.astype(s0.dtype)

def token_mixers(h, lp, a_k_cache, a_v_cache, conv_prev, s0):
    bsz, t, _ = h.shape
    proj = h @ lp['w_in']

    def heads(cols, nh, hd):
        return cols.reshape(bsz, t, nh, hd)

    qa = heads(proj[..., OFF_A:OFF_A + WIDTH_A], N_HEADS_A, HEAD_DIM_A)
    ka = heads(proj[..., OFF_A + WIDTH_A:OFF_A + 2 * WIDTH_A], N_HEADS_A, HEAD_DIM_A)
    va = heads(proj[..., OFF_A + 2 * WIDTH_A:OFF_B], N_HEADS_A, HEAD_DIM_A)
    if a_k_cache is None:
        ya = band_attention_prompt(qa, ka, va, lp['a_rel_bias'])
        keep = min(A_REACH, t)
        new_k, new_v = ka[:, t - keep:], va[:, t - keep:]
    else:
        ya = band_attention_sample(qa, ka, va, a_k_cache, a_v_cache, lp['a_rel_bias'])
        new_k, new_v = ka, va
    xb, new_conv = causal_conv(proj[..., OFF_B:OFF_Z], conv_prev, lp['b_conv_w'])
    qb = l2norm(heads(xb[..., :WIDTH_B], N_HEADS_B, HEAD_DIM_B)) * (HEAD_DIM_B ** -0.5)
    kb = l2norm(heads(xb[..., WIDTH_B:2 * WIDTH_B], N_HEADS_B, HEAD_DIM_B))
    vb = heads(xb[..., 2 * WIDTH_B:], N_HEADS_B, HEAD_DIM_B)
    zb = heads(proj[..., OFF_Z:OFF_BETA], N_HEADS_B, HEAD_DIM_B)
    beta = jax.nn.sigmoid(proj[..., OFF_BETA:OFF_DECAY].astype(jnp.float32))
    decay_in = proj[..., OFF_DECAY:OFF_GATE].astype(jnp.float32) + lp['b_dt_bias'].astype(jnp.float32)
    g = -jnp.exp(lp['b_a_log'].astype(jnp.float32)) * jax.nn.softplus(decay_in)
    ob, new_s = gated_delta_rule(qb, kb, vb, g, beta, s0, min(CHUNK, t))
    ob = rmsnorm(ob, lp['b_out_norm']) * jax.nn.silu(zb)
    gate = jax.nn.sigmoid(proj[..., OFF_GATE:])
    merged = (gate[..., :D_MODEL] * (ya.reshape(bsz, t, WIDTH_A) @ lp['w_branch_a'])
              + gate[..., D_MODEL:] * (ob.reshape(bsz, t, WIDTH_B) @ lp['w_branch_b']))
    return merged @ lp['w_mix_out'], new_k, new_v, new_conv, new_s

def memory_kv(mem, g, wk, wv):
    m = rmsnorm(mem, g)
    bsz = mem.shape[0]
    mk = (m @ wk).reshape(bsz, N_MEM, N_HEADS_X, HEAD_DIM_X)
    mv = (m @ wv).reshape(bsz, N_MEM, N_HEADS_X, HEAD_DIM_X)
    return mk, mv

def cross_attention(x, g, wq, wo, mk, mv):
    bsz, t, _ = x.shape
    q = (rmsnorm(x, g) @ wq).reshape(bsz, t, N_HEADS_X, HEAD_DIM_X)
    sc = jnp.einsum('bqhd,bkhd->bhqk', q, mk).astype(jnp.float32) * (HEAD_DIM_X ** -0.5)
    p = jax.nn.softmax(sc, axis=-1).astype(mv.dtype)
    o = jnp.einsum('bhqk,bkhd->bqhd', p, mv).reshape(bsz, t, D_MODEL)
    return o @ wo

def trunk_layer(x, lp, mem_k, mem_v, a_k_cache, a_v_cache, conv_prev, s0):
    x = x + 0.5 * swiglu_ffn(x, lp['ffn1_norm'], lp['ffn1_w_gate'], lp['ffn1_w_up'], lp['ffn1_w_down'])
    mix, new_k, new_v, new_conv, new_s = token_mixers(rmsnorm(x, lp['mix_norm']), lp, a_k_cache, a_v_cache, conv_prev, s0)
    x = x + mix
    x = x + cross_attention(x, lp['xattn_norm'], lp['xattn_wq'], lp['xattn_wo'], mem_k, mem_v)
    x = x + 0.5 * swiglu_ffn(x, lp['ffn2_norm'], lp['ffn2_w_gate'], lp['ffn2_w_up'], lp['ffn2_w_down'])
    return x, new_k, new_v, new_conv, new_s

def setup_inputs(seed: int = 0) -> dict:
    key = jax.random.key(seed)
    keys = list(jax.random.split(key, 40))

    def nrm(shape, scale=1.0):
        return scale * jax.random.normal(keys.pop(), shape, jnp.float32)

    def gain(shape):
        return 1.0 + nrm(shape, 0.05)

    L = DEPTH
    a_len = min(A_REACH, PAST_LEN)
    dt = jnp.exp(jax.random.uniform(keys.pop(), (L, N_HEADS_B), jnp.float32, math.log(1e-3), math.log(1e-1)))
    a_init = jax.random.uniform(keys.pop(), (L, N_HEADS_B), jnp.float32, 1.0, 16.0)
    return {
        'x_prompt': nrm((BATCH, SEQ, D_MODEL)),
        'x_sample': nrm((DEC_BATCH, DEC_SEQ, D_MODEL)),
        'cache_a_k': nrm((L, DEC_BATCH, a_len, N_HEADS_A, HEAD_DIM_A)),
        'cache_a_v': nrm((L, DEC_BATCH, a_len, N_HEADS_A, HEAD_DIM_A)),
        'state_b_conv': nrm((L, DEC_BATCH, CONV_W - 1, B_CONV_DIM)),
        'state_b_s': nrm((L, DEC_BATCH, N_HEADS_B, HEAD_DIM_B, HEAD_DIM_B), 0.1),
        'cache_mem_k': nrm((L, DEC_BATCH, N_MEM, N_HEADS_X, HEAD_DIM_X)),
        'cache_mem_v': nrm((L, DEC_BATCH, N_MEM, N_HEADS_X, HEAD_DIM_X)),
        'mem_prompt': nrm((BATCH, N_MEM, D_MODEL)),
        'ffn1_norm': gain((L, D_MODEL)),
        'ffn1_w_gate': nrm((L, D_MODEL, D_FF), D_MODEL ** -0.5),
        'ffn1_w_up': nrm((L, D_MODEL, D_FF), D_MODEL ** -0.5),
        'ffn1_w_down': nrm((L, D_FF, D_MODEL), D_FF ** -0.5),
        'mix_norm': gain((L, D_MODEL)),
        'w_in': nrm((L, D_MODEL, N_IN), D_MODEL ** -0.5),
        'a_rel_bias': nrm((L, N_HEADS_A, 2 * REL_CLIP + 1), 0.5),
        'b_conv_w': nrm((L, CONV_W, B_CONV_DIM), CONV_W ** -0.5),
        'b_a_log': jnp.log(a_init),
        'b_dt_bias': dt + jnp.log(-jnp.expm1(-dt)),
        'b_out_norm': gain((L, HEAD_DIM_B)),
        'w_branch_a': nrm((L, WIDTH_A, D_MODEL), WIDTH_A ** -0.5),
        'w_branch_b': nrm((L, WIDTH_B, D_MODEL), WIDTH_B ** -0.5),
        'w_mix_out': nrm((L, D_MODEL, D_MODEL), D_MODEL ** -0.5),
        'xattn_norm': gain((L, D_MODEL)),
        'mem_norm': gain((L, D_MODEL)),
        'xattn_wq': nrm((L, D_MODEL, D_MODEL), D_MODEL ** -0.5),
        'xattn_wk': nrm((L, D_MODEL, D_MODEL), D_MODEL ** -0.5),
        'xattn_wv': nrm((L, D_MODEL, D_MODEL), D_MODEL ** -0.5),
        'xattn_wo': nrm((L, D_MODEL, D_MODEL), D_MODEL ** -0.5),
        'ffn2_norm': gain((L, D_MODEL)),
        'ffn2_w_gate': nrm((L, D_MODEL, D_FF), D_MODEL ** -0.5),
        'ffn2_w_up': nrm((L, D_MODEL, D_FF), D_MODEL ** -0.5),
        'ffn2_w_down': nrm((L, D_FF, D_MODEL), D_FF ** -0.5),
        'final_norm': gain((D_MODEL,)),
    }

def reference(x_prompt, x_sample, cache_a_k, cache_a_v, state_b_conv, state_b_s, cache_mem_k, cache_mem_v,
              mem_prompt, ffn1_norm, ffn1_w_gate, ffn1_w_up, ffn1_w_down, mix_norm, w_in, a_rel_bias,
              b_conv_w, b_a_log, b_dt_bias, b_out_norm, w_branch_a, w_branch_b, w_mix_out, xattn_norm,
              mem_norm, xattn_wq, xattn_wk, xattn_wv, xattn_wo, ffn2_norm, ffn2_w_gate, ffn2_w_up,
              ffn2_w_down, final_norm):
    xp, xs = x_prompt, x_sample
    bp = x_prompt.shape[0]
    p_a_k, p_a_v, p_b_conv, p_b_s, p_mem_k, p_mem_v = [], [], [], [], [], []
    s_a_k, s_a_v, s_b_conv, s_b_s = [], [], [], []
    for l in range(DEPTH):
        lp = {
            'ffn1_norm': ffn1_norm[l], 'ffn1_w_gate': ffn1_w_gate[l], 'ffn1_w_up': ffn1_w_up[l],
            'ffn1_w_down': ffn1_w_down[l], 'mix_norm': mix_norm[l], 'w_in': w_in[l],
            'a_rel_bias': a_rel_bias[l], 'b_conv_w': b_conv_w[l], 'b_a_log': b_a_log[l],
            'b_dt_bias': b_dt_bias[l], 'b_out_norm': b_out_norm[l], 'w_branch_a': w_branch_a[l],
            'w_branch_b': w_branch_b[l], 'w_mix_out': w_mix_out[l], 'xattn_norm': xattn_norm[l],
            'xattn_wq': xattn_wq[l], 'xattn_wo': xattn_wo[l], 'ffn2_norm': ffn2_norm[l],
            'ffn2_w_gate': ffn2_w_gate[l], 'ffn2_w_up': ffn2_w_up[l], 'ffn2_w_down': ffn2_w_down[l],
        }
        mk_p, mv_p = memory_kv(mem_prompt, mem_norm[l], xattn_wk[l], xattn_wv[l])
        conv0 = jnp.zeros((bp, CONV_W - 1, B_CONV_DIM), x_prompt.dtype)
        s_zero = jnp.zeros((bp, N_HEADS_B, HEAD_DIM_B, HEAD_DIM_B), x_prompt.dtype)
        xp, ak, av, cv, sb = trunk_layer(xp, lp, mk_p, mv_p, None, None, conv0, s_zero)
        p_a_k.append(ak)
        p_a_v.append(av)
        p_b_conv.append(cv)
        p_b_s.append(sb)
        p_mem_k.append(mk_p)
        p_mem_v.append(mv_p)
        xs, ak, av, cv, sb = trunk_layer(xs, lp, cache_mem_k[l], cache_mem_v[l], cache_a_k[l], cache_a_v[l],
                                         state_b_conv[l], state_b_s[l])
        s_a_k.append(ak)
        s_a_v.append(av)
        s_b_conv.append(cv)
        s_b_s.append(sb)
    y_prompt = rmsnorm(xp, final_norm)
    y_sample = rmsnorm(xs, final_norm)
    return (y_prompt, y_sample,
            jnp.stack(p_a_k), jnp.stack(p_a_v), jnp.stack(p_b_conv), jnp.stack(p_b_s),
            jnp.stack(p_mem_k), jnp.stack(p_mem_v),
            jnp.stack(s_a_k), jnp.stack(s_a_v), jnp.stack(s_b_conv), jnp.stack(s_b_s))


_drawn_inputs = setup_inputs


def setup_inputs(seed=0):
    import zlib

    import numpy as np

    out = dict(_drawn_inputs(seed))
    spreads = {}
    factors = {'b_out_norm': 3.638, 'xattn_norm': 8.0, 'ffn2_norm': 3.088}
    for name, (base, spread) in spreads.items():
        noise = np.random.default_rng([zlib.crc32(name.encode()), seed]).standard_normal(out[name].shape)
        drawn = base * np.exp(spread * noise) if base else spread * noise
        out[name] = jnp.asarray(drawn.astype(out[name].dtype))
    for name, factor in factors.items():
        out[name] = (out[name] * factor).astype(out[name].dtype)
    return out
```

```python
from contextlib import ExitStack

import numpy as np

import concourse.bass as bass
from concourse import mybir

F32 = mybir.dt.float32
F32R = mybir.dt.float32r
ALU = mybir.AluOpType
ACT = mybir.ActivationFunctionType
AX_X = mybir.AxisListType.X

P = 128
D = 1024
KD = D // P
SEQ = 1024
DB, DS = 8, 16
T = SEQ + DB * DS
NT_TILES = T // P
THIRD = T // 3
FF = 2816
NFF = FF // P
HA, DHA, REACH, REL = 8, 64, 512, 128
HB, DHB, CW = 4, 128, 4
HX, DHX, NMEM = 4, 256, 256
WIN = REACH + P
NBIAS = WIN + P
PADP, PADS = SEQ + CW - 1, DS + CW - 1
PADDED = PADP + DB * PADS
NEG = -1e30
EPS = 1e-6
RING = 3
NPS = 4


class Counter:

    def __init__(self, nc, ctx, name):
        self.sem = ctx.enter_context(nc.semaphore(name))
        self.base = 0

    def at(self, k):
        return self.base + k



def last_use(j, turn):
    same = [u for u in range(turn) if u % RING == j % RING]
    at = same.index(j)
    return (0, same[at - 1]) if at else (1, same[-1])


def load_units(sp, k, first, turns, turn, at_turn=None):
    def one(i, j):
        back, last = last_use(j, turn)
        if not (isinstance(i, int) and i < back):
            sp.wait_ge(k.unit_split.sem, k.unit_split.at(turn * i + (last + 1 - turn * back)))
        sp.dma_start(k.w_raw[j % RING][:, :], k.units[turn * i + (first + j)])\
            .then_inc(k.raw_landed[j % RING].sem, 16)
    if at_turn:
        at_turn(0)
    for j in range(turn):
        one(0, j)
    if turns > 1:
        with sp.Fori(1, turns) as i:
            if at_turn:
                at_turn(i)
            for j in range(turn):
                one(i, j)


def split_units(pool, k, turns, jobs):
    turn = len(jobs)

    def one(i, j):
        s = j % RING
        back, last = last_use(j, turn)
        landed = len(range(s, turn, RING))
        if not (isinstance(i, int) and i < back):
            pool.wait_ge(k.dense_done.sem, k.dense_done.at(jobs[-1] * i + (jobs[last] - jobs[-1] * back)))
        pool.wait_ge(k.raw_landed[s].sem, k.raw_landed[s].at(16 * landed * i + 16 * (j // RING + 1)))
        pool.tensor_tensor(k.w_hi[s][:, :], k.w_raw[s][:, :], k.zero[:, 0:1].to_broadcast([P, D]), ALU.add)\
            .then_inc(k.unit_hi.sem, 1)
        pool.wait_ge(k.unit_hi.sem, k.unit_hi.at(turn * i + (j + 1)))
        pool.tensor_tensor(k.w_lo[s][:, :], k.w_raw[s][:, :], k.w_hi[s][:, :].bitcast(F32),
                           ALU.subtract).then_inc(k.unit_split.sem, 1)

    for j in range(turn):
        one(0, j)
    if turns > 1:
        with pool.Fori(1, turns) as i:
            for j in range(turn):
                one(i, j)


def product(pe, out, tiles, n0, n1):
    last = len(tiles) - 1
    for part in range(3):
        for i, (wh, wl, xh, xl) in enumerate(tiles):
            mm = pe.matmul(out, wl if part == 2 else wh, (xl if part == 1 else xh)[:, n0:n1],
                           start=(part == 0 and i == 0), stop=(part == 2 and i == last))
    return mm


def units_done(k, turns, turn):
    for s in range(RING):
        k.raw_landed[s].base += 16 * turns * len(range(s, turn, RING))
    for sig in (k.unit_hi, k.unit_split):
        sig.base += turns * turn


class Filler:
    UNITS, PRODUCTS, PIECES = 4, 12, 24

    def __init__(self, main, plan):
        self.main, self.plan = main, plan
        assert sum(plan) == self.PRODUCTS * self.PIECES, sum(plan)

    def jobs(self):
        return tuple(3 * (u + 1) for u in range(self.main + self.UNITS))

    def products(self, k, pe, i, place, xh, xl):
        turn, per_turn = self.main + self.UNITS, 3 * (self.main + self.UNITS)
        first = sum(self.plan[:place])
        for m in range(first, first + self.plan[place]):
            g, r = 3 * self.main + m // self.PIECES, m % self.PIECES
            u, n, part, c = g // 3, g % 3, r // KD, r % KD
            if r == 0:
                if n == 0:
                    pe.wait_ge(k.unit_split.sem, k.unit_split.at(turn * i + (u + 1)))
                pe.wait_ge(k.evacuated.sem, k.evacuated.at(per_turn * i + (g + 1)))
            w = (k.w_lo if part == 2 else k.w_hi)[self.slot(u)]
            mm = pe.matmul(k.ps[g % 2][:, 0:THIRD], w[:, c * P:(c + 1) * P],
                           (xl if part == 1 else xh)[:, c, n * THIRD:(n + 1) * THIRD], start=(r == 0),
                           stop=(r == self.PIECES - 1))
            if r == self.PIECES - 1:
                mm.then_inc(k.dense_done.sem, 1)

    def slot(self, u):
        return u % RING

    def finished(self, place):
        a = sum(self.plan[:place])
        b = a + self.plan[place]
        return [3 * self.main + g for g in range(self.PRODUCTS) if a < (g + 1) * self.PIECES <= b]


def ffn_phase(nc, k, name, x, xh, xl, work, first_unit):
    turns = NFF // 2
    h_hi = nc.alloc_sbuf_tensor_at(name + "_h_hi", [P, 2, T], F32R, offset=work)
    h_lo = nc.alloc_sbuf_tensor_at(name + "_h_lo", [P, 2, T], F32R, offset=work + 8 * T)
    gate = nc.alloc_sbuf_tensor_at(name + "_gate", [P, 3, THIRD], F32, offset=work + 16 * T)
    hid = nc.alloc_sbuf_tensor_at(name + "_hid", [P, 2, THIRD], F32, offset=work + 20 * T)
    JOBS = 36

    with nc.Block() as block:
        @block.sync
        def _(sp):
            load_units(sp, k, first_unit, turns, 6)

        @block.gpsimd
        def _(pool):
            split_units(pool, k, turns, (3, 6, 9, 12, 36, 36))

        @block.tensor
        def _(pe):
            with pe.Fori(0, turns) as i:
                g = 0
                for u in range(4):
                    pe.wait_ge(k.unit_split.sem, k.unit_split.at(6 * i + (u + 1)))
                    for n in range(3):
                        if g < NPS:
                            pe.wait_ge(k.x_added.sem, k.x_added.at(24 * i + (g + 1)))
                        elif (g - NPS) % 6 < 3:
                            pe.wait_ge(k.gate_ready.sem, k.gate_ready.at(6 * i + ((g - NPS) // 6 * 3 + (g - NPS) % 6 + 1)))
                        else:
                            pe.wait_ge(k.gate_used.sem, k.gate_used.at(6 * i + ((g - NPS) // 6 * 3 + (g - NPS) % 6 - 3 + 1 + 3)))
                        tiles = [(k.w_hi[u % RING][:, c * P:(c + 1) * P], k.w_lo[u % RING][:, c * P:(c + 1) * P],
                                  xh[:, c, :], xl[:, c, :]) for c in range(KD)]
                        mm = product(pe, k.ps[g % NPS][:, 0:THIRD], tiles, n * THIRD, (n + 1) * THIRD)
                        mm.then_inc(k.dense_done.sem, 1)
                        g += 1
                pe.wait_ge(k.unit_split.sem, k.unit_split.at(6 * i + 6))
                for n in range(3):
                    pe.wait_ge(k.h_ready.sem, k.h_ready.at(6 * i + (3 + n + 1)))
                    for d in range(KD):
                        if g >= 12 + NPS:
                            pe.wait_ge(k.x_added.sem, k.x_added.at(24 * i + (g - 12 + 1)))
                        elif g == 12:
                            pe.wait_ge(k.gate_ready.sem, k.gate_ready.at(6 * i + 6))
                        else:
                            pe.wait_ge(k.gate_used.sem, k.gate_used.at(6 * i + (g - 13 + 4 + 3)))
                        tiles = [(k.w_hi[1 + c][:, d * P:(d + 1) * P], k.w_lo[1 + c][:, d * P:(d + 1) * P],
                                  h_hi[:, c, :], h_lo[:, c, :]) for c in range(2)]
                        mm = product(pe, k.ps[g % NPS][:, 0:THIRD], tiles, n * THIRD, (n + 1) * THIRD)
                        mm.then_inc(k.dense_done.sem, 1)
                        g += 1

        @block.scalar
        def _(act):
            with act.Fori(0, turns) as i:
                for c in range(2):
                    for n in range(3):
                        g = 6 * c + n
                        act.wait_ge(k.dense_done.sem, k.dense_done.at(JOBS * i + (g + 1)))
                        act.wait_ge(k.gate_used.sem, k.gate_used.at(6 * i + (3 * c + n + 1)))
                        act.activation(gate[:, n, :], k.ps[g % NPS][:, 0:THIRD], ACT.Silu)\
                            .then_inc(k.gate_ready.sem, 1)

        @block.vector
        def _(dve):
            with dve.Fori(0, turns) as i:
                for c in range(2):
                    for n in range(3):
                        g = 6 * c + 3 + n
                        j = 3 * c + n
                        cols = slice(n * THIRD, (n + 1) * THIRD)
                        dve.wait_ge(k.dense_done.sem, k.dense_done.at(JOBS * i + (g + 1)))
                        dve.wait_ge(k.gate_ready.sem, k.gate_ready.at(6 * i + (j + 1)))
                        up = k.ps[g % NPS][:, 0:THIRD]
                        dve.tensor_tensor(hid[:, j % 2, :], up, gate[:, n, :], ALU.mult).then_inc(k.hid_made.sem, 1)
                        dve.tensor_tensor(h_hi[:, c, cols], up, gate[:, n, :], ALU.mult)\
                            .then_inc(k.gate_used.sem, 1)
                        dve.wait_ge(k.hid_made.sem, k.hid_made.at(6 * i + (j + 1)))
                        dve.wait_ge(k.gate_used.sem, k.gate_used.at(6 * i + (j + 1 + 3)))
                        dve.tensor_tensor(h_lo[:, c, cols], hid[:, j % 2, :], h_hi[:, c, cols].bitcast(F32),
                                          ALU.subtract).then_inc(k.h_ready.sem, 1)
                g = 12
                for n in range(3):
                    for d in range(KD):
                        dve.wait_ge(k.dense_done.sem, k.dense_done.at(JOBS * i + (g + 1)))
                        xs = x[:, d, n * THIRD:(n + 1) * THIRD]
                        dve.scalar_tensor_tensor(out=xs, in0=k.ps[g % NPS][:, 0:THIRD], scalar=0.5, in1=xs,
                                                 op0=ALU.mult, op1=ALU.add).then_inc(k.x_added.sem, 1)
                        g += 1

    units_done(k, turns, 6)
    k.dense_done.base += JOBS * turns
    k.x_added.base += 24 * turns
    for sig in (k.gate_used, k.gate_ready, k.hid_made, k.h_ready):
        sig.base += 6 * turns


def norm_phase(nc, k, name, x, gains, hi, lo, work, width, block_cols, out=None):
    nb = width // block_cols
    tmp = nc.alloc_sbuf_tensor_at(name + "_tmp", [P, 2, KD, block_cols], F32, offset=work)
    work += 8 * KD * block_cols
    ssq = nc.alloc_sbuf_tensor_at(name + "_ssq", [P, 2, block_cols], F32, offset=work)
    rinv = nc.alloc_sbuf_tensor_at(name + "_rinv", [P, 2, block_cols], F32, offset=work + 8 * block_cols)

    def cols(n):
        return slice(n * block_cols, (n + 1) * block_cols)

    with nc.Block() as block:
        @block.tensor
        def _(pe):
            for n in range(nb):
                pe.wait_ge(k.nsum.sem, k.nsum.at(n + 1))
                pe.matmul(k.ps[n][:, 0:block_cols], k.ones[:, :], ssq[:, n % 2, :], start=True, stop=True)\
                    .then_inc(k.ntotal.sem, 1)

        @block.scalar
        def _(act):
            def finish(n):
                b = n % 2
                act.wait_ge(k.ntotal.sem, k.ntotal.at(n + 1))
                if n >= 2:
                    act.wait_ge(k.nscaled.sem, k.nscaled.at(n - 1))
                act.activation(rinv[:, b, :], k.ps[n][:, 0:block_cols], ACT.Ln, bias=k.eps[:, 0:1], scale=1.0 / D)\
                    .then_inc(k.nln.sem, 1)
                act.wait_ge(k.nln.sem, k.nln.at(n + 1))
                act.activation(rinv[:, b, :], rinv[:, b, :], ACT.Exp, scale=-0.5).then_inc(k.nrinv.sem, 1)
                if out is None:
                    act.wait_ge(k.nscaled.sem, k.nscaled.at(n + 1))
                    act.activation(hi[:, :, cols(n)], tmp[:, b], ACT.Copy).then_inc(k.nhi.sem, 1)

            for n in range(nb):
                if n >= 2 and out is None:
                    act.wait_ge(k.nsplit.sem, k.nsplit.at(n - 1))
                elif n >= 2:
                    act.wait_ge(k.nout[n % 2].sem, k.nout[n % 2].at(16 * (n // 2)))
                act.activation(tmp[:, n % 2], x[:, :, cols(n)], ACT.Square).then_inc(k.nsq.sem, 1)
                if n >= 1:
                    finish(n - 1)
            finish(nb - 1)

        def finish(dve, n):
            b = n % 2
            dve.wait_ge(k.nrinv.sem, k.nrinv.at(n + 1))
            dve.wait_ge(k.nsum.sem, k.nsum.at(n + 1))
            for c in range(KD):
                mm = dve.scalar_tensor_tensor(out=tmp[:, b, c, :], in0=x[:, c, cols(n)], scalar=gains[:, c:c + 1],
                                              in1=rinv[:, b, :], op0=ALU.mult, op1=ALU.mult)
            mm.then_inc(k.nscaled.sem, 1)
            if out is None:
                dve.wait_ge(k.nhi.sem, k.nhi.at(n + 1))
                dve.tensor_tensor(lo[:, :, cols(n)], tmp[:, b], hi[:, :, cols(n)].bitcast(F32), ALU.subtract)\
                    .then_inc(k.nsplit.sem, 1)

        @block.vector
        def _(dve):
            for n in range(nb):
                dve.wait_ge(k.nsq.sem, k.nsq.at(n + 1))
                if n >= 2:
                    dve.wait_ge(k.ntotal.sem, k.ntotal.at(n - 1))
                dve.tensor_reduce(ssq[:, n % 2, :], tmp[:, n % 2].rearrange("p c t -> p t c"), AX_X, ALU.add)\
                    .then_inc(k.nsum.sem, 1)
                if n < 1:
                    continue
                finish(dve, n - 1)
            finish(dve, nb - 1)

        @block.sync
        def _(sp):
            if out is not None:
                for n in range(nb):
                    sp.wait_ge(k.nscaled.sem, k.nscaled.at(n + 1))
                    sp.dma_start(out[:, :, cols(n)], tmp[:, n % 2]).then_inc(k.nout[n % 2].sem, 16)
                for b in range(min(2, nb)):
                    sp.wait_ge(k.nout[b].sem, k.nout[b].at(16 * len(range(b, nb, 2))))

    for sig in (k.nsum, k.ntotal, k.nsq, k.nln, k.nrinv, k.nscaled):
        sig.base += nb
    if out is None:
        k.nhi.base += nb
        k.nsplit.base += nb
    else:
        for b in range(2):
            k.nout[b].base += 16 * len(range(b, nb, 2))


class Core:

    def __init__(self, nc, ctx):
        self.nc, self.ctx, self.tokens = nc, ctx, []
        at = (nc.sbuf_base + 63) // 64 * 64
        self.ones = nc.alloc_sbuf_tensor_at("ones", [P, P], F32, offset=at)
        self.ident = nc.alloc_sbuf_tensor_at("ident", [P, P], F32, offset=at + 512)
        self.eps = nc.alloc_sbuf_tensor_at("eps", [P, 1], F32, offset=at + 1024)
        self.zero = nc.alloc_sbuf_tensor_at("zero", [P, 1], F32, offset=at + 1056)
        self.gains = nc.alloc_sbuf_tensor_at("gains", [P, 6 * KD], F32, offset=at + 1088)
        at += 1088 + 6 * KD * 4
        self.w_raw = [nc.alloc_sbuf_tensor_at(f"w_raw{s}", [P, D], F32, offset=at + 4096 * s) for s in range(RING)]
        self.w_hi = [nc.alloc_sbuf_tensor_at(f"w_hi{s}", [P, D], F32R, offset=at + 4096 * (RING + s))
                     for s in range(RING)]
        self.w_lo = [nc.alloc_sbuf_tensor_at(f"w_lo{s}", [P, D], F32R, offset=at + 4096 * (2 * RING + s))
                     for s in range(RING)]
        self.arena = at + 4096 * 3 * RING
        self.psum = ctx.enter_context(nc.psum_tensor("psum", [P, 8, 512], F32))
        self.ps = [self.psum[:, b, :] for b in range(8)]
        self.raw_landed = [self.counter(f"raw_landed{s}") for s in range(RING)]
        self.unit_hi, self.unit_split = self.counter("unit_hi"), self.counter("unit_split")
        self.dense_done, self.evacuated = self.counter("dense_done"), self.counter("evacuated", 2)
        self.gate_ready, self.gate_used = self.counter("gate_ready"), self.counter("gate_used", 3)
        self.hid_made, self.h_ready = self.counter("hid_made"), self.counter("h_ready")
        self.x_added = self.counter("x_added", NPS)
        self.nsq, self.nsum, self.ntotal = self.counter("nsq"), self.counter("nsum"), self.counter("ntotal")
        self.nln, self.nrinv, self.nscaled = self.counter("nln"), self.counter("nrinv"), self.counter("nscaled")
        self.nhi, self.nsplit = self.counter("nhi"), self.counter("nsplit")
        self.nout = [self.counter(f"normed_stored{b}") for b in range(2)]
        self.loaded = self.counter("loaded")
        self.table_loaded, self.rows_made = self.counter("table_loaded"), self.counter("rows_made")
        self.rows_stored = self.counter("rows_stored")
        self.v_turned, self.vn_ready = self.counter("v_turned"), self.counter("vn_ready")
        self.qbd_zero, self.qbd_ready, self.masked = self.counter("qbd_zero"), self.counter("qbd_ready"), self.counter("masked")
        self.scored, self.biased, self.maxed = self.counter("scored"), self.counter("biased"), self.counter("maxed")
        self.exped, self.inverted, self.normed = self.counter("exped"), self.counter("inverted"), self.counter("normed")
        self.turned, self.pt_ready = self.counter("turned"), self.counter("pt_ready")
        self.valued, self.o_read = self.counter("valued", 1), self.counter("o_read")
        self.a_loaded, self.kv_stored = self.counter("a_loaded"), self.counter("kv_stored", 32)
        self.ya_stored = self.counter("ya_stored", 16)

        self.kv_slot = [self.counter(f"slot_stored{b}", 32) for b in range(2)]
        self.score_read = self.counter("score_read", 2)
        self.merged, self.gated = self.counter("merged", 2), self.counter("gated")
        self.squared = self.counter("squared")
        self.lned = self.counter("lned")
        self.sq_summed = self.counter("sq_summed")
        self.rooted = self.counter("rooted")
        self.per_ready = self.counter("per_ready")
        self.decayed = self.counter("decayed")
        self.scaled = self.counter("scaled")
        self.rows_spread = self.counter("rows_spread")
        self.l2_done = self.counter("l2_done")
        self.grams = self.counter("grams")
        self.kv_turned = self.counter("kv_turned")
        self.y_started = self.counter("y_started")
        self.y_turned = self.counter("y_turned")
        self.x_started = self.counter("x_started")
        self.masked_level = self.counter("masked_level")
        self.p1_ready = self.counter("p1_ready")
        self.p1_done = self.counter("p1_done")
        self.level_done = self.counter("level_done")
        self.corrected = self.counter("corrected")
        self.w_ready = self.counter("w_ready")
        self.u_ready = self.counter("u_ready")
        self.wu_done = self.counter("wu_done")
        self.s_ready = self.counter("s_ready")
        self.ws_done = self.counter("ws_done")
        self.o_copied = self.counter("o_copied")
        self.qg_ready = self.counter("qg_ready")
        self.vw_ready = self.counter("vw_ready")
        self.o_done = self.counter("o_done")
        self.s_loaded = self.counter("s_loaded")
        self.wz_ready = self.counter("wz_ready")
        self.v8_ready = self.counter("v8_ready")
        self.pad_ready = self.counter("pad_ready")
        self.silued = self.counter("silued")
        self.convolved = self.counter("convolved")
        self.eg_ready = self.counter("eg_ready")
        self.dt_args = self.counter("dt_args")
        self.dt_ready = self.counter("dt_ready")
        self.s_final = self.counter("s_final")
        self.o_scaled = self.counter("o_scaled")
        self.o_normed = self.counter("o_normed")
        self.pad_landed = [self.counter(f"pad_landed{c}") for c in range(3)]
        self.z_landed, self.stash_clear = self.counter("z_landed"), self.counter("stash_clear")
        self.gate_sigmoid = self.counter("gate_sigmoid")
        self.tap = self.counter("tap")
        self.nt_made = self.counter("nt_made")
        self.first_mask = self.counter("first_mask")
        self.s_decayed = self.counter("s_decayed")
        self.pre = self.counter("pre")
        self.pre_pe = self.counter("pre_pe")
        self.pre_act = self.counter("pre_act")
        self.b_loaded = self.counter("b_loaded")
        self.kv_done, self.s_out, self.yb_stored = (self.counter("kv_done", 1), self.counter("s_out", 48),
                                                    self.counter("yb_stored", 16))

    def counter(self, name, tokens=0):
        s = Counter(self.nc, self.ctx, name)
        if tokens:
            self.tokens.append((s, tokens))
        return s



def make_bias_rows(nc, k, work):
    rows = nc.alloc_sbuf_tensor_at("bias_rows", [P, HA, NBIAS], F32, offset=work)
    far = NBIAS - (2 * REL + 1)
    with nc.Block() as block:
        @block.sync
        def _(sp):
            sp.dma_start(rows[:, :, far:], k.table.partition_broadcast(P)).then_inc(k.table_loaded.sem, 16)
            sp.wait_ge(k.rows_made.sem, k.rows_made.at(1))
            sp.dma_start(k.bias_dram[:, 0:HA * NBIAS], rows[:].rearrange("p h m -> p (h m)")).then_inc(k.rows_stored.sem, 16)
            sp.wait_ge(k.rows_stored.sem, k.rows_stored.at(16))

        @block.vector
        def _(dve):
            dve.wait_ge(k.table_loaded.sem, k.table_loaded.at(16))
            dve.tensor_copy(rows[:, :, 0:far], rows[:, :, far:far + 1].to_broadcast([P, HA, far]))\
                .then_inc(k.rows_made.sem, 1)


def attention_phase(nc, k, xh, xl, work, first_unit):
    at = [work]

    def sb(name, shape):
        t = nc.alloc_sbuf_tensor_at(name, shape, F32, offset=at[0])
        at[0] += (4 * int(np.prod(shape[1:])) + 31) // 32 * 32
        return t

    q, kt, vt = sb("a_q", [P, T]), sb("a_k", [P, T]), sb("a_v", [P, T])
    vn, vns = sb("a_vn", [P, 8, P]), sb("a_vns", [DS, DB, P])
    qbd = sb("a_qbd", [P, DB, 32])
    kc, vc = sb("a_kc", [P, DB, REACH]), sb("a_vc", [P, DB, 4, P])
    bias, bias_s = sb("a_bias", [P, 2, WIN]), sb("a_bias_s", [P, REACH + DS])
    sc, pt = sb("a_sc", [P, 2, WIN]), sb("a_pt", [P, 2, 5, P])
    ya = sb("a_y", [P, T])
    nmax, rsum, rinv = sb("a_nmax", [P, 2]), sb("a_rsum", [P, 2]), sb("a_rinv", [P, 2])
    PAIRS, STEPS, ND = HA // 2, 18, 2
    stash = sb("a_stash", [P, 2, PADDED])
    filler = Filler(3, [15] * 8 + [14] * 12)
    DONE = 9 + filler.PRODUCTS
    psS, psT = k.psum[:, 3:5, :].rearrange("p b c -> p (b c)"), k.psum[:, 5:7, :].rearrange("p b c -> p (b c)")
    obank = (7, 2)
    shifted = k.bias_dram_flat[P - 1:P - 1 + P * (k.bias_pitch - 1)].rearrange("(q m) -> q m", q=P)[:, 0:HA * NBIAS]\
        .rearrange("q (h m) -> h q m", h=HA)

    def window(t):
        n = min(5, t + 1)
        return t + 1 - n, n

    with nc.Block() as block:
        @block.sync
        def _(sp):
            load_units(sp, k, first_unit, PAIRS, 7)

        @block.gpsimd
        def _(pool):
            split_units(pool, k, PAIRS, filler.jobs())

        @block.tensor
        def _(pe):
            def scores(i, s):
                if s >= 1:
                    pe.wait_ge(k.biased.sem, k.biased.at(STEPS * i + s))
                if s < 16:
                    t, h = s // 2, s % 2
                    k0, n = window(t)
                    hp = slice(64 * h, 64 * h + 64)
                    for a, b in ((0, min(4, n)), (4, n)):
                        if b > a:
                            mm = pe.matmul(psS[:, a * P:b * P], q[hp, t * P:(t + 1) * P],
                                           kt[hp, (k0 + a) * P:(k0 + b) * P], start=True, stop=True)
                    mm.then_inc(k.scored.sem, 1)
                    return
                for b in range(4):
                    st = 4 * (s - 16) + b
                    pe.matmul(psS[32 * b:32 * b + 32, 0:REACH], qbd[:, st, :], kc[:, st, :], start=True, stop=True,
                              tile_position=(0, 32 * b))
                    mm = pe.matmul(psS[32 * b:32 * b + 32, REACH:REACH + DS], qbd[:, st, :],
                                   kt[:, SEQ + DS * st:SEQ + DS * (st + 1)], start=True, stop=True,
                                   tile_position=(0, 32 * b))
                mm.then_inc(k.scored.sem, 1)

            def turn_probs(i, s):
                pe.wait_ge(k.normed.sem, k.normed.at(STEPS * i + (s + 1)))
                if s >= 1:
                    pe.wait_ge(k.pt_ready.sem, k.pt_ready.at(STEPS * i + s))
                b = s % 2
                n = window(s // 2)[1] if s < 16 else 4
                for j in range(n):
                    mm = pe.transpose(psT[:, j * P:(j + 1) * P], sc[:, b, j * P:(j + 1) * P], k.ident[:, :])
                if s >= 16:
                    mm = pe.transpose(psT[0:DS, 4 * P:5 * P], sc[:, b, REACH:REACH + DS], k.ident[:, :])
                mm.then_inc(k.turned.sem, 1)

            def values(i, s):
                pe.wait_ge(k.pt_ready.sem, k.pt_ready.at(STEPS * i + (s + 1)))
                o = k.ps[obank[(s // 2) % 2 if s < 16 else s % 2]]
                b = s % 2
                if s < 16:
                    t, h = s // 2, s % 2
                    k0, n = window(t)
                    if h == 0 and t >= 2:
                        pe.wait_ge(k.o_read.sem, k.o_read.at(10 * i + (t - 1)))
                    for j in range(n):
                        mm = pe.matmul(o[64 * h:64 * h + 64, 0:P], vn[:, k0 + j, 64 * h:64 * h + 64], pt[:, b, j, :],
                                       start=(j == 0), stop=(j == n - 1), tile_position=(0, 64 * h))
                    mm.then_inc(k.valued.sem, 1)
                    return
                pe.wait_ge(k.o_read.sem, k.o_read.at(10 * i + (8 + (s - 16) - 1)))
                for c in range(4):
                    st = 4 * (s - 16) + c
                    out = o[:, 32 * c:32 * c + 32]
                    for j in range(4):
                        pe.matmul(out, vc[:, st, j, :], pt[:, b, j, 32 * c:32 * c + 32], start=(j == 0), stop=False)
                    mm = pe.matmul(out, vns[0:DS, st, :], pt[0:DS, b, 4, 32 * c:32 * c + 32], start=False, stop=True)
                mm.then_inc(k.valued.sem, 1)

            with pe.Fori(0, PAIRS) as i:
                for u in range(3):
                    pe.wait_ge(k.unit_split.sem, k.unit_split.at(7 * i + (u + 1)))
                    for n in range(3):
                        g = 3 * u + n
                        pe.wait_ge(k.evacuated.sem, k.evacuated.at(DONE * i + max(g + 1, 2)))
                        tiles = [(k.w_hi[u][:, c * P:(c + 1) * P], k.w_lo[u][:, c * P:(c + 1) * P],
                                  xh[:, c, :], xl[:, c, :]) for c in range(KD)]
                        product(pe, k.ps[g % ND][:, 0:THIRD], tiles, n * THIRD, (n + 1) * THIRD)\
                            .then_inc(k.dense_done.sem, 1)
                pe.wait_ge(k.evacuated.sem, k.evacuated.at(DONE * i + (9 + ND)))
                for t in range(8):
                    mm = pe.transpose(psT[:, t * P:(t + 1) * P], vt[:, t * P:(t + 1) * P], k.ident[:, :])
                mm.then_inc(k.v_turned.sem, 1)
                for b in range(DB):
                    mm = pe.transpose(psS[0:DS, b * P:(b + 1) * P], vt[:, SEQ + DS * b:SEQ + DS * (b + 1)], k.ident[:, :])
                mm.then_inc(k.v_turned.sem, 1)
                pe.wait_ge(k.vn_ready.sem, k.vn_ready.at(2 * i + 2))
                for s in range(STEPS + 2):
                    if s == 16:
                        pe.wait_ge(k.a_loaded.sem, k.a_loaded.at(192 * i + 192))
                        pe.wait_ge(k.qbd_ready.sem, k.qbd_ready.at(2 * i + 2))
                    if s < STEPS:
                        scores(i, s)
                    if s >= 2:
                        values(i, s - 2)
                    filler.products(k, pe, i, s, xh, xl)
                    if 1 <= s <= STEPS:
                        turn_probs(i, s - 1)

        @block.scalar
        def _(act):
            def evacuate(i, g):
                act.wait_ge(k.dense_done.sem, k.dense_done.at(DONE * i + (g + 1)))
                u, n = g // 3 - 3, g % 3
                row, src = stash[:, u % 2, :], k.ps[g % ND]
                if n == 0:
                    act.wait_ge(k.kv_slot[u % 2].sem, k.kv_slot[u % 2].at(32 * i + (16 * (u // 2) + 32)))
                if u == 3:
                    act.activation(row[:, n * THIRD:(n + 1) * THIRD], src[:, 0:THIRD], ACT.Copy)\
                        .then_inc(k.evacuated.sem, 1)
                elif n < 2:
                    act.activation(row[:, CW - 1 + n * THIRD:CW - 1 + (n + 1) * THIRD], src[:, 0:THIRD], ACT.Copy)\
                        .then_inc(k.evacuated.sem, 1)
                else:
                    act.activation(row[:, CW - 1 + 2 * THIRD:PADP], src[:, 0:THIRD - P], ACT.Copy)
                    act.activation(row[:, PADP:].rearrange("p (b c) -> p b c", c=PADS)[:, :, CW - 1:],
                                   src[:, THIRD - P:THIRD].rearrange("p (b c) -> p b c", c=DS), ACT.Copy)\
                        .then_inc(k.evacuated.sem, 1)
                if n == 2:
                    act.wait_ge(k.evacuated.sem, k.evacuated.at(DONE * i + (g + 1 + ND)))
                    act.dma_start(k.proj_dram[4 * i + u], row).then_inc(k.kv_slot[u % 2].sem, 16)

            act.wait_ge(k.stash_clear.sem, k.stash_clear.at(1))
            with act.Fori(0, PAIRS) as i:
                act.wait_ge(k.valued.sem, k.valued.at(STEPS * i + 1))
                loads = [(kc[:], k.k_cache[i]), (vc[:], k.v_cache[i])]
                for h in range(2):
                    loads.append((bias[:, h, :], shifted[2 * i + h][:, 0:WIN]))
                    for b in range(4):
                        r = 32 * b + 16 * h
                        loads.append((bias_s[r:r + 16, :], shifted[2 * i + h][0:16, 0:REACH + DS]))
                for dst, src in loads:
                    act.dma_start(dst, src).then_inc(k.a_loaded.sem, 16)
                for g in range(9):
                    if g == 3:
                        act.wait_ge(k.kv_stored.sem, k.kv_stored.at(32 * i + 32))
                    act.wait_ge(k.dense_done.sem, k.dense_done.at(DONE * i + (g + 1)))
                    dst = (q, kt, vt)[g // 3][:, (g % 3) * THIRD:(g % 3 + 1) * THIRD]
                    act.activation(dst, k.ps[g % ND][:, 0:THIRD], ACT.Copy,
                                   scale=DHA ** -0.5 if g < 3 else 1.0).then_inc(k.evacuated.sem, 1)
                act.wait_ge(k.evacuated.sem, k.evacuated.at(DONE * i + (9 + ND)))
                act.dma_start(k.a_k_out[i], kt[:, :]).then_inc(k.kv_stored.sem, 16)
                act.dma_start(k.a_v_out[i], vt[:, :]).then_inc(k.kv_stored.sem, 16)
                act.wait_ge(k.v_turned.sem, k.v_turned.at(2 * i + 1))
                act.activation(vn[:].rearrange("p t c -> p (t c)"), psT[:, :], ACT.Copy).then_inc(k.vn_ready.sem, 1)
                act.wait_ge(k.v_turned.sem, k.v_turned.at(2 * i + 2))
                act.activation(vns[:].rearrange("p t c -> p (t c)"), psS[0:DS, :], ACT.Copy).then_inc(k.vn_ready.sem, 1)

                def exps(s):
                    act.wait_ge(k.maxed.sem, k.maxed.at(STEPS * i + (s + 1)))
                    n = window(s // 2)[1] * P if s < 16 else REACH + DS
                    b = s % 2
                    act.activation(sc[:, b, 0:n], sc[:, b, 0:n], ACT.Exp, bias=nmax[:, b:b + 1],
                                   accum_out=rsum[:, b:b + 1]).then_inc(k.exped.sem, 1)

                def copy_turned(s):
                    act.wait_ge(k.turned.sem, k.turned.at(STEPS * i + (s + 1)))
                    if s >= 2:
                        act.wait_ge(k.valued.sem, k.valued.at(STEPS * i + (s - 1 + 1)))
                    n = window(s // 2)[1] if s < 16 else 4
                    b = s % 2
                    if s >= 16:
                        act.activation(pt[0:DS, b, 4, :], psT[0:DS, 4 * P:5 * P], ACT.Copy)
                    act.activation(pt[:, b, 0:n, :].rearrange("p t c -> p (t c)"), psT[:, 0:n * P], ACT.Copy)\
                        .then_inc(k.pt_ready.sem, 1)

                def copy_o(s):
                    act.wait_ge(k.valued.sem, k.valued.at(STEPS * i + (s + 1 + 1)))
                    if s == 1:
                        act.wait_ge(k.ya_stored.sem, k.ya_stored.at(16 * i + 16))
                    if s < 16:
                        t = s // 2
                        act.activation(ya[:, t * P:(t + 1) * P], k.ps[obank[t % 2]][:, 0:P], ACT.Copy)\
                            .then_inc(k.o_read.sem, 1)
                        return
                    o = k.ps[obank[s % 2]]
                    for h in range(2):
                        hp = slice(64 * h, 64 * h + 64)
                        c0 = SEQ + 64 * (s - 16)
                        a = act.activation(ya[hp, c0:c0 + 64].rearrange("p (b c) -> p b c", c=16),
                                           o[hp, 0:P].rearrange("p (b c) -> p b c", c=32)[:, :, 16 * h:16 * h + 16],
                                           ACT.Copy)
                    a.then_inc(k.o_read.sem, 1)

                for s in range(STEPS + 3):
                    if s >= 1:
                        for g in filler.finished(s - 1):
                            evacuate(i, g)
                    if s < STEPS:
                        exps(s)
                    if 1 <= s <= STEPS:
                        copy_turned(s - 1)
                    if s >= 3 and ((s - 3) % 2 == 1 or s - 3 >= 16):
                        copy_o(s - 3)
                act.wait_ge(k.o_read.sem, k.o_read.at(10 * i + 10))
                act.dma_start(k.ya_dram[i], ya[:, :]).then_inc(k.ya_stored.sem, 16)
            act.wait_ge(k.ya_stored.sem, k.ya_stored.at(16 * PAIRS + 16))
            act.wait_ge(k.kv_stored.sem, k.kv_stored.at(32 * PAIRS + 32))
            for b in range(2):
                act.wait_ge(k.kv_slot[b].sem, k.kv_slot[b].at(32 * PAIRS + 32))

        @block.vector
        def _(dve):
            dve.memset(stash[:], 0.0).then_inc(k.stash_clear.sem, 1)
            dve.memset(qbd[:], 0.0).then_inc(k.qbd_zero.sem, 1)
            dve.wait_ge(k.qbd_zero.sem, k.qbd_zero.at(1))
            with dve.Fori(0, PAIRS) as i:
                dve.wait_ge(k.evacuated.sem, k.evacuated.at(DONE * i + (3 + ND)))
                for h in range(2):
                    hp = slice(64 * h, 64 * h + 64)
                    dve.tensor_copy(qbd[hp, :, 16 * h:16 * h + 16], q[hp, SEQ:T].rearrange("p (b c) -> p b c", c=DS))\
                        .then_inc(k.qbd_ready.sem, 1)
                dve.wait_ge(k.a_loaded.sem, k.a_loaded.at(192 * i + 192))
                for h in range(2):
                    dve.memset(bias[0:64, h, WIN - 64:WIN], NEG)
                    m = dve.memset(bias[64:P, h, 0:64], NEG)
                m.then_inc(k.masked.sem, 1)
                dve.wait_ge(k.masked.sem, k.masked.at(i + 1))

                def logits(s):
                    dve.wait_ge(k.scored.sem, k.scored.at(STEPS * i + (s + 1)))
                    if s >= 2:
                        dve.wait_ge(k.turned.sem, k.turned.at(STEPS * i + (s - 1)))
                    b = s % 2
                    if s < 16:
                        n = window(s // 2)[1] * P
                        add = bias[:, s % 2, WIN - n:WIN]
                    else:
                        n, add = REACH + DS, bias_s[:, :]
                    dve.tensor_tensor(sc[:, b, 0:n], psS[:, 0:n], add, ALU.add).then_inc(k.biased.sem, 1)
                    dve.wait_ge(k.biased.sem, k.biased.at(STEPS * i + (s + 1)))
                    dve.tensor_reduce(nmax[:, b:b + 1], sc[:, b, 0:n], AX_X, ALU.max, negate=True)\
                        .then_inc(k.maxed.sem, 1)

                def normalise(s):
                    b = s % 2
                    n = window(s // 2)[1] * P if s < 16 else REACH + DS
                    dve.wait_ge(k.exped.sem, k.exped.at(STEPS * i + (s + 1)))
                    dve.reciprocal(rinv[:, b:b + 1], rsum[:, b:b + 1]).then_inc(k.inverted.sem, 1)
                    dve.wait_ge(k.inverted.sem, k.inverted.at(STEPS * i + (s + 1)))
                    dve.tensor_scalar(sc[:, b, 0:n], sc[:, b, 0:n], rinv[:, b:b + 1], None, ALU.mult)\
                        .then_inc(k.normed.sem, 1)

                for s in range(STEPS + 1):
                    if s < STEPS:
                        logits(s)
                    if s >= 1:
                        normalise(s - 1)

    units_done(k, PAIRS, 7)
    k.qbd_zero.base += 1
    k.stash_clear.base += 1
    for b in range(2):
        k.kv_slot[b].base += 32 * PAIRS
    for s_, n in ((k.dense_done, DONE), (k.evacuated, DONE), (k.v_turned, 2), (k.vn_ready, 2), (k.scored, STEPS),
                  (k.biased, STEPS), (k.maxed, STEPS), (k.exped, STEPS), (k.inverted, STEPS), (k.normed, STEPS),
                  (k.turned, STEPS), (k.pt_ready, STEPS), (k.valued, STEPS), (k.o_read, 10), (k.a_loaded, 192),
                  (k.kv_stored, 32), (k.ya_stored, 16), (k.masked, 1), (k.qbd_ready, 2)):
        s_.base += n * PAIRS



MASKS = ("upto", "upto16", "future", "future16", "same16")


def delta_constants():
    j, i = np.arange(P)[:, None], np.arange(P)[None, :]
    same = j // DS == i // DS
    out = [j <= i, (j <= i) & same, np.where(j <= i, 0, NEG), np.where((j <= i) & same, 0, NEG), same]
    for level in range(7):
        half = 1 << level
        out.append((i // (2 * half) == j // (2 * half)) & (i % (2 * half) >= half) & (j % (2 * half) < half))
    streams = (j // DS) == np.arange(DB)[None, :]
    return np.concatenate([np.asarray(m, np.float32) for m in out + [streams]], axis=1)


PLAN_START, PLAN_NORM, PLAN_GROUP, PLAN_BEFORE, PLAN_LEVEL, PLAN_STEP = 96, 6, 8, 8, 4, 6


def delta_phase(nc, k, xh, xl, work, first_unit):
    at = [work]

    def sb(name, shape, dt=F32):
        t = nc.alloc_sbuf_tensor_at(name, shape, dt, offset=at[0])
        at[0] += (4 * int(np.prod(shape[1:])) + 31) // 32 * 32
        return t

    def alias(name, shape, offset):
        return nc.alloc_sbuf_tensor_at(name, shape, F32, offset=offset)

    NM = 12
    consts = sb("b_consts", [P, NM * P + DB])

    def const(n):
        return consts[:, n * P:(n + 1) * P]

    upto, upto16, future, future16, same16 = (const(n) for n in range(5))
    level_mask = [const(5 + n) for n in range(7)]
    streams = consts[:, NM * P:NM * P + DB]
    pad_at = at[0]
    pad = sb("b_pad", [P, 3, PADDED])
    X, Y, P1 = (alias(n, [P, T], pad_at + 4 * T * m) for m, n in enumerate(("b_X", "b_Y", "b_P1")))
    yq_at = at[0]
    y = sb("b_y", [P, 3, T])
    yq, yk, yv = y[:, 0, :], y[:, 1, :], y[:, 2, :]
    oT, MT = alias("b_oT", [P, T], yq_at + 4 * T), alias("b_MT", [P, T], yq_at + 8 * T)
    z = sb("b_z", [P, T])
    kbe, kd, vb = sb("b_kbe", [P, T]), sb("b_kd", [P, T]), sb("b_vb", [P, T])
    eg = sb("b_eg", [P, T])
    DT = sb("b_DT", [P, T])
    wT = alias("b_wT", [P, T], at[0] - 4 * T)
    NT = sb("b_NT", [P, T])
    u = alias("b_u", [P, T], at[0] - 4 * T)
    intra = sb("b_intra", [P, T])
    S = sb("b_S", [P, 2, P])
    Sb, v8 = sb("b_Sb", [P, DB, P]), sb("b_v8", [P, DB, P])
    wz = sb("b_wz", [P, DB * (P + DS)])[:]
    vw = sb("b_vw", [P, 2, P])
    sq = sb("b_sq", [P, 2, THIRD])
    rr = sb("b_rr", [P, 2, THIRD])
    cst, cout = sb("b_cst", [P, 3, DB, CW - 1]), sb("b_cout", [P, 3, (DB + 1) * (CW - 1)])
    cw = sb("b_cw", [P, 3, CW])
    gn = sb("b_gn", [P, 1])
    w8, w8h, w8l = sb("b_w8", [P, KD, 8]), sb("b_w8h", [P, KD, 8], F32R), sb("b_w8l", [P, KD, 8], F32R)
    rate, dtb = sb("b_rate", [P, HB]), sb("b_dtb", [P, HB])
    stash = sb("b_stash", [P, 2, THIRD])
    per = sb("b_per", [P, HB, 5, NT_TILES])
    sh = sb("b_sh", [P, 5, NT_TILES])
    t1, t2, t3 = sb("b_t1", [P, HB, NT_TILES]), sb("b_t2", [P, HB, NT_TILES]), sb("b_t3", [P, HB, NT_TILES])
    ND = 2
    LV = 18
    PLAN = [PLAN_START] + [PLAN_NORM] * 6 + [PLAN_GROUP] * 3 + [PLAN_BEFORE] + [PLAN_LEVEL] * LV + [PLAN_STEP] * 8
    filler = Filler(0, PLAN + [12 * 24 - sum(PLAN)])

    with nc.Block() as block:
        @block.sync
        def _(sp):
            for dst, src in ((consts[:], k.b_consts), (w8[:], k.w_beta_decay), (rate[:], k.a_log.partition_broadcast(P)),
                             (dtb[:], k.dt_bias.partition_broadcast(P)), (gn[:], k.b_gain)):
                sp.dma_start(dst, src).then_inc(k.b_loaded.sem, 16)
            sp.wait_ge(k.b_loaded.sem, k.b_loaded.at(80))

        @block.tensor
        def _(pe):
            pe.wait_ge(k.pre.sem, k.pre.at(2))
            for t in range(NT_TILES):
                for part in range(3):
                    for c in range(KD):
                        mm = pe.matmul(k.ps[0][:, 8 * t:8 * t + 8], (xl if part == 1 else xh)[:, c, t * P:(t + 1) * P],
                                       (w8l if part == 2 else w8h)[:, c, :], start=(part == 0 and c == 0),
                                       stop=(part == 2 and c == KD - 1))
            mm.then_inc(k.pre_pe.sem, 1)
            pe.wait_ge(k.pre.sem, k.pre.at(10))
            for dst, m16, m in ((0, upto16, upto), (64, same16, k.ones[:, :])):
                pe.matmul(k.ps[1][:, dst:dst + 32], m, t1[:, :, 0:8], start=True, stop=True)
                mm = pe.matmul(k.ps[1][:, dst + 32:dst + 36], m16, t1[:, :, 8:9], start=True, stop=True)
            mm.then_inc(k.pre_pe.sem, 1)

        @block.scalar
        def _(act):
            act.wait_ge(k.b_loaded.sem, k.b_loaded.at(80))
            act.activation(rate[:, :], rate[:, :], ACT.Exp).then_inc(k.pre_act.sem, 1)
            act.wait_ge(k.pre.sem, k.pre.at(3))
            act.activation(t2[:], t2[:], ACT.Exp).then_inc(k.pre_act.sem, 1)
            act.wait_ge(k.pre.sem, k.pre.at(6))
            act.activation(t3[:], t3[:], ACT.Exp).then_inc(k.pre_act.sem, 1)
            act.wait_ge(k.pre_act.sem, k.pre_act.at(3))
            act.activation(t3[:], t3[:], ACT.Ln, bias=1.0).then_inc(k.pre_act.sem, 1)
            act.wait_ge(k.pre.sem, k.pre.at(12))
            act.activation(t2[:], t2[:], ACT.Exp).then_inc(k.pre_act.sem, 1)
            act.wait_ge(k.pre_act.sem, k.pre_act.at(5))
            act.wait_ge(k.pre.sem, k.pre.at(14))
            act.activation(per[:, :, 2, :], t3[:], ACT.Exp).then_inc(k.pre_act.sem, 1)

        @block.vector
        def _(dve):
            n = [0]

            def then(ins):
                ins.then_inc(k.pre.sem, 1)
                n[0] += 1
                dve.wait_ge(k.pre.sem, k.pre.at(n[0]))

            def both(off):
                return k.ps[0][:, 0:8 * NT_TILES].rearrange("p (t c) -> p c t", c=8)[:, off:off + HB, :]

            dve.memset(wz, 0.0)
            dve.wait_ge(k.b_loaded.sem, k.b_loaded.at(80))
            then(dve.tensor_copy(w8h[:], w8[:]))
            then(dve.tensor_tensor(w8l[:], w8[:], w8h[:].bitcast(F32), ALU.subtract))
            dve.wait_ge(k.pre_pe.sem, k.pre_pe.at(1))
            then(dve.tensor_scalar(t2[:], both(0), -1.0, None, ALU.mult))
            then(dve.tensor_tensor(t1[:], both(HB), dtb[:, :].unsqueeze(2).to_broadcast([P, HB, NT_TILES]), ALU.add))
            then(dve.tensor_scalar(t3[:], t1[:], -1.0, None, ALU.mult))
            then(dve.tensor_tensor(t3[:], t1[:], t3[:], ALU.min))
            dve.wait_ge(k.pre_act.sem, k.pre_act.at(2))
            then(dve.tensor_scalar(t2[:], t2[:], 1.0, None, ALU.add))
            then(dve.reciprocal(per[:, :, 0, :], t2[:]))
            dve.wait_ge(k.pre_act.sem, k.pre_act.at(4))
            then(dve.scalar_tensor_tensor(out=t1[:], in0=t1[:], scalar=0.0, in1=t3[:], op0=ALU.max, op1=ALU.add))
            then(dve.scalar_tensor_tensor(out=t1[:], in0=t1[:], scalar=-1.0,
                                          in1=rate[:, :].unsqueeze(2).to_broadcast([P, HB, NT_TILES]),
                                          op0=ALU.mult, op1=ALU.mult))
            dve.wait_ge(k.pre_pe.sem, k.pre_pe.at(2))
            gc8, gc1 = k.ps[1][:, 0:32].rearrange("p (h t) -> p h t", h=HB), k.ps[1][:, 32:36].unsqueeze(2)
            gl8, gl1 = k.ps[1][:, 64:96].rearrange("p (h t) -> p h t", h=HB), k.ps[1][:, 96:100].unsqueeze(2)
            then(dve.tensor_copy(t2[:, :, 0:8], gc8))
            then(dve.tensor_copy(t2[:, :, 8:9], gc1))
            dve.tensor_scalar(per[:, :, 3, 0:8], gc8, -1.0, None, ALU.mult)
            then(dve.tensor_scalar(per[:, :, 3, 8:9], gc1, -1.0, None, ALU.mult))
            dve.tensor_tensor(t3[:, :, 0:8], gl8, per[:, :, 3, 0:8], ALU.add)
            then(dve.tensor_tensor(t3[:, :, 8:9], gl1, per[:, :, 3, 8:9], ALU.add))
            dve.wait_ge(k.pre_act.sem, k.pre_act.at(6))
            dve.tensor_tensor(per[:, :, 1, :], per[:, :, 0, :], t2[:], ALU.mult)
            then(dve.tensor_copy(per[:, :, 4, :], t1[:]))

    k.pre.base += 15
    k.pre_pe.base += 2
    k.pre_act.base += 6
    k.b_loaded.base += 80

    def third(g):
        return slice(g * THIRD, (g + 1) * THIRD)

    def tile(t):
        return slice(t * P, (t + 1) * P)

    def by_tile(a):
        return a.rearrange("p (t c) -> p t c", c=P)

    def bank(a, b):
        return k.ps[a + b % 2]

    with nc.Block() as block:
        @block.sync
        def _(sp):
            def projections(i):
                if not isinstance(i, int):
                    sp.wait_ge(k.wu_done.sem, k.wu_done.at(3 * i))
                for c in range(3):
                    sp.dma_start(pad[:, c, :], k.proj_dram[4 * i + c]).then_inc(k.pad_landed[c].sem, 16)

            load_units(sp, k, first_unit, HB, 4, projections)

        @block.gpsimd
        def _(pool):
            split_units(pool, k, HB, (3, 6, 9, 12))

        def correct(pe, i, r):
            g = r % 3
            pe.wait_ge(k.p1_ready.sem, k.p1_ready.at(LV * i + (r + 1)))
            if r >= 2:
                pe.wait_ge(k.level_done.sem, k.level_done.at(LV * i + (r - 1)))
            if r < LV - 3:
                for t in range(3 * g, 3 * g + 3):
                    pe.matmul(bank(4, r)[:, tile(t % 3)], Y[:, tile(t)], P1[:, tile(t)], start=True, stop=True)
            for t in range(3 * g, 3 * g + 3):
                mm = pe.matmul(bank(6, r)[:, tile(t % 3)], P1[:, tile(t)], Y[:, tile(t)], start=True, stop=True)
            mm.then_inc(k.corrected.sem, 1)

        @block.tensor
        def _(pe):
            with pe.Fori(0, HB) as i:
                filler.products(k, pe, i, 0, xh, xl)
                for r in range(6):
                    filler.products(k, pe, i, 1 + r, xh, xl)
                    pe.wait_ge(k.squared.sem, k.squared.at(9 * i + (r + 1)))
                    if r >= 2:
                        pe.wait_ge(k.lned.sem, k.lned.at(9 * i + (r - 1)))
                    pe.matmul(bank(2, r)[:, 0:THIRD], k.ones[:, :], sq[:, r % 2, :], start=True, stop=True)\
                        .then_inc(k.sq_summed.sem, 1)
                pe.wait_ge(k.per_ready.sem, k.per_ready.at(i + 1))
                pe.wait_ge(k.lned.sem, k.lned.at(9 * i + 6))
                for g in range(3):
                    tiles = range(3 * g, 3 * g + 3)
                    if g >= 1:
                        pe.wait_ge(k.decayed.sem, k.decayed.at(3 * i + g))
                        pe.wait_ge(k.scaled.sem, k.scaled.at(3 * i + g))
                    for t in tiles:
                        o = tile(t % 3)
                        pe.matmul(k.ps[2][:, o], sh[:, 4, t:t + 1].to_broadcast([P, P]), upto if t < 8 else upto16,
                                  start=True, stop=True)
                    for t in tiles:
                        mm = pe.matmul(k.ps[3][:, tile(t % 3)], sh[:, 0, t:t + 1].to_broadcast([P, P]), k.ident[:, :],
                                       start=True, stop=True)
                    mm.then_inc(k.rows_spread.sem, 1)
                    pe.wait_ge(k.l2_done.sem, k.l2_done.at(6 * i + (g + 4)))
                    for t in tiles:
                        pe.matmul(k.ps[4][:, tile(t % 3)], yk[:, tile(t)], yk[:, tile(t)], start=True, stop=True)
                    for t in tiles:
                        mm = pe.matmul(k.ps[5][:, tile(t % 3)], yk[:, tile(t)], yq[:, tile(t)], start=True, stop=True)
                    mm.then_inc(k.grams.sem, 1)
                    for t in tiles:
                        pe.transpose(k.ps[6][:, tile(t % 3)], yk[:, tile(t)], k.ident[:, :])
                    for t in tiles:
                        mm = pe.transpose(k.ps[7][:, tile(t % 3)], yv[:, tile(t)], k.ident[:, :])
                    mm.then_inc(k.kv_turned.sem, 1)
                    filler.products(k, pe, i, 7 + g, xh, xl)
                filler.products(k, pe, i, 10, xh, xl)
                pe.wait_ge(k.decayed.sem, k.decayed.at(3 * i + 3))
                pe.wait_ge(k.scaled.sem, k.scaled.at(3 * i + 3))
                for g in range(3):
                    pe.wait_ge(k.y_started.sem, k.y_started.at(3 * i + (g + 1)))
                    for t in range(3 * g, 3 * g + 3):
                        mm = pe.transpose(k.ps[2 + g][:, tile(t % 3)], Y[:, tile(t)], k.ident[:, :])
                    mm.then_inc(k.y_turned.sem, 1)
                pe.wait_ge(k.x_started.sem, k.x_started.at(3 * i + 3))
                for r in range(LV):
                    g = r % 3
                    pe.wait_ge(k.masked_level.sem, k.masked_level.at(LV * i + (r + 1)))
                    if r >= 2:
                        pe.wait_ge(k.p1_ready.sem, k.p1_ready.at(LV * i + (r - 1)))
                    for t in range(3 * g, 3 * g + 3):
                        mm = pe.matmul(bank(2, r)[:, tile(t % 3)], MT[:, tile(t)], X[:, tile(t)], start=True, stop=True)
                    mm.then_inc(k.p1_done.sem, 1)
                    filler.products(k, pe, i, 11 + r, xh, xl)
                    if r >= 1:
                        correct(pe, i, r - 1)
                correct(pe, i, LV - 1)
                pe.wait_ge(k.level_done.sem, k.level_done.at(LV * i + LV))
                for g in range(3):
                    if g >= 1:
                        pe.wait_ge(k.w_ready.sem, k.w_ready.at(3 * i + g))
                        pe.wait_ge(k.u_ready.sem, k.u_ready.at(3 * i + g))
                    for t in range(3 * g, 3 * g + 3):
                        pe.matmul(k.ps[2][:, tile(t % 3)], kbe[:, tile(t)], Y[:, tile(t)], start=True, stop=True)
                    for t in range(3 * g, 3 * g + 3):
                        mm = pe.matmul(k.ps[3][:, tile(t % 3)], Y[:, tile(t)], vb[:, tile(t)], start=True, stop=True)
                    mm.then_inc(k.wu_done.sem, 1)
                pe.wait_ge(k.w_ready.sem, k.w_ready.at(3 * i + 3))
                pe.wait_ge(k.u_ready.sem, k.u_ready.at(3 * i + 3))
                for t in range(8):
                    s = S[:, t % 2, :]
                    pe.wait_ge(k.s_ready.sem, k.s_ready.at(9 * i + (t + 1)))
                    pe.matmul(bank(2, t)[:, 0:P], wT[:, tile(t)], s, start=True, stop=True).then_inc(k.ws_done.sem, 1)
                    filler.products(k, pe, i, 11 + LV + t, xh, xl)
                    if t >= 2:
                        pe.wait_ge(k.o_copied.sem, k.o_copied.at(9 * i + (t - 1)))
                    pe.wait_ge(k.qg_ready.sem, k.qg_ready.at(3 * i + (t // 3 + 1)))
                    pe.matmul(bank(6, t)[:, 0:P], s, yq[:, tile(t)], start=True, stop=False)
                    pe.wait_ge(k.vw_ready.sem, k.vw_ready.at(9 * i + (t + 1)))
                    pe.matmul(bank(4, t)[:, 0:P], kd[:, tile(t)], vw[:, t % 2, :], start=True, stop=True)\
                        .then_inc(k.kv_done.sem, 1)
                    pe.matmul(bank(6, t)[:, 0:P], vw[:, t % 2, :], intra[:, tile(t)], start=False, stop=True)\
                        .then_inc(k.o_done.sem, 1)
                pe.wait_ge(k.s_loaded.sem, k.s_loaded.at(80 * i + 80))
                pe.wait_ge(k.wz_ready.sem, k.wz_ready.at(i + 1))
                pe.wait_ge(k.s_ready.sem, k.s_ready.at(9 * i + 9))
                for b in range(DB):
                    mm = pe.matmul(k.ps[2][:, 0:P], wz[:, tile(b)], Sb[:, b, :], start=(b == 0), stop=(b == DB - 1))
                mm.then_inc(k.ws_done.sem, 1)
                pe.wait_ge(k.o_copied.sem, k.o_copied.at(9 * i + 7))
                pe.wait_ge(k.vw_ready.sem, k.vw_ready.at(9 * i + 9))
                pe.matmul(k.ps[6][:, 0:P], vw[:, 0, :], intra[:, tile(8)], start=True, stop=False,
                          skip_group_check=True)
                for b in range(DB):
                    c = slice(b * DS, (b + 1) * DS)
                    mm = pe.matmul(k.ps[6][:, c], Sb[:, b, :], yq[:, SEQ + b * DS:SEQ + (b + 1) * DS],
                                   start=False, stop=(b == DB - 1), skip_group_check=True)
                mm.then_inc(k.o_done.sem, 1)
                pe.wait_ge(k.v8_ready.sem, k.v8_ready.at(i + 1))
                for h in range(2):
                    mm = pe.matmul(k.ps[4 + h][:, :], kd[:, tile(8)],
                                   v8[:, 4 * h:4 * h + 4, :].rearrange("p b c -> p (b c)"), start=True, stop=True)
                mm.then_inc(k.kv_done.sem, 1)
                filler.products(k, pe, i, 19 + LV, xh, xl)
                for g in range(3):
                    pe.wait_ge(k.squared.sem, k.squared.at(9 * i + (6 + g + 1)))
                    if g == 2:
                        pe.wait_ge(k.lned.sem, k.lned.at(9 * i + 7))
                    pe.matmul(bank(2, g)[:, 0:THIRD], k.ones[:, :], sq[:, g % 2, :], start=True, stop=True)\
                        .then_inc(k.sq_summed.sem, 1)

        @block.scalar
        def _(act):
            def evacuate(i, place):
                for g in filler.finished(place):
                    act.wait_ge(k.dense_done.sem, k.dense_done.at(12 * i + (g + 1)))
                    b = g % 2
                    act.wait_ge(k.kv_slot[b].sem, k.kv_slot[b].at(96 * i + (16 * (g // 2) + 32)))
                    act.activation(stash[:, b, :], k.ps[g % ND][:, 0:THIRD], ACT.Copy).then_inc(k.evacuated.sem, 1)
                    act.wait_ge(k.evacuated.sem, k.evacuated.at(12 * i + (g + 1 + ND)))
                    act.dma_start(k.gate_dram[4 * i + g // 3][:, third(g % 3)], stash[:, b, :])\
                        .then_inc(k.kv_slot[b].sem, 16)

            with act.Fori(0, HB) as i:
                act.wait_ge(k.kv_done.sem, k.kv_done.at(9 * i + 1))
                act.wait_ge(k.s_out.sem, k.s_out.at(48 * i + 48))
                act.dma_start(cst[:], k.conv_state[i]).then_inc(k.s_loaded.sem, 16)
                act.dma_start(cw[:], k.conv_w[i]).then_inc(k.s_loaded.sem, 16)
                for b in range(3):
                    bb = slice(3 * b, min(DB, 3 * b + 3))
                    act.dma_start(Sb[:, bb, :], k.state_s[i][:, bb, :]).then_inc(k.s_loaded.sem, 16)
                act.dma_start(z[:, :], k.proj_dram[4 * i + 3][:, 0:T]).then_inc(k.z_landed.sem, 16)
                evacuate(i, 0)
                for c in range(3):
                    act.wait_ge(k.convolved.sem, k.convolved.at(3 * i + (c + 1)))
                    act.activation(y[:, c, :], y[:, c, :], ACT.Silu).then_inc(k.silued.sem, 1)
                act.wait_ge(k.z_landed.sem, k.z_landed.at(16 * i + 16))
                act.activation(z[:, :], z[:, :], ACT.Silu).then_inc(k.silued.sem, 1)
                act.wait_ge(k.silued.sem, k.silued.at(4 * i + 4))

                def square(r, src):
                    if r >= 2:
                        act.wait_ge(k.sq_summed.sem, k.sq_summed.at(9 * i + (r - 1)))
                    act.activation(sq[:, r % 2, :], src, ACT.Square).then_inc(k.squared.sem, 1)

                def root(r, scale):
                    act.wait_ge(k.sq_summed.sem, k.sq_summed.at(9 * i + (r + 1)))
                    if 2 <= r < 8:
                        act.wait_ge(k.l2_done.sem, k.l2_done.at(6 * i + min(r - 1, 6)))
                    elif r == 8:
                        act.wait_ge(k.o_normed.sem, k.o_normed.at(3 * i + 1))
                    b = k.ps[2 + r % 2] if r < 6 else k.ps[2 + (r - 6) % 2]
                    act.activation(rr[:, r % 2, :], b[:, 0:THIRD], ACT.Ln, bias=k.eps[:, 0:1], scale=scale)\
                        .then_inc(k.lned.sem, 1)
                    act.wait_ge(k.lned.sem, k.lned.at(9 * i + (r + 1)))
                    act.activation(rr[:, r % 2, :], rr[:, r % 2, :], ACT.Exp, scale=-0.5).then_inc(k.rooted.sem, 1)

                for r in range(7):
                    if r < 6:
                        square(r, y[:, r // 3, third(r % 3)])
                    if r >= 1:
                        root(r - 1, 1.0)
                        evacuate(i, r)
                for g in range(3):
                    act.wait_ge(k.rows_spread.sem, k.rows_spread.at(3 * i + (g + 1)))
                    act.activation(eg[:, third(g)], k.ps[2][:, 0:THIRD], ACT.Exp).then_inc(k.eg_ready.sem, 1)
                    act.wait_ge(k.dt_args.sem, k.dt_args.at(3 * i + (g + 1)))
                    act.activation(DT[:, third(g)], DT[:, third(g)], ACT.Exp).then_inc(k.dt_ready.sem, 1)
                    if g >= 1:
                        evacuate(i, 6 + g)
                evacuate(i, 9)
                evacuate(i, 10)
                for g in range(3):
                    act.wait_ge(k.y_turned.sem, k.y_turned.at(3 * i + (g + 1)))
                    act.activation(X[:, third(g)], k.ps[2 + g][:, 0:THIRD], ACT.Copy).then_inc(k.x_started.sem, 1)
                for r in range(LV):
                    act.wait_ge(k.p1_done.sem, k.p1_done.at(LV * i + (r + 1)))
                    if r >= 3:
                        act.wait_ge(k.corrected.sem, k.corrected.at(LV * i + (r - 2)))
                    act.activation(P1[:, third(r % 3)], bank(2, r)[:, 0:THIRD], ACT.Copy).then_inc(k.p1_ready.sem, 1)
                    if r >= 1:
                        evacuate(i, 10 + r)
                evacuate(i, 10 + LV)
                for g in range(3):
                    act.wait_ge(k.wu_done.sem, k.wu_done.at(3 * i + (g + 1)))
                    act.activation(wT[:, third(g)], k.ps[2][:, 0:THIRD], ACT.Copy).then_inc(k.w_ready.sem, 1)
                for t in range(9):
                    act.wait_ge(k.o_done.sem, k.o_done.at(9 * i + (t + 1)))
                    act.activation(oT[:, tile(t)], (bank(6, t) if t < 8 else k.ps[6])[:, 0:P], ACT.Copy)\
                        .then_inc(k.o_copied.sem, 1)
                    if 1 <= t <= 8:
                        evacuate(i, 10 + LV + t)
                act.wait_ge(k.o_copied.sem, k.o_copied.at(9 * i + 9))
                evacuate(i, 19 + LV)
                for g in range(4):
                    if g < 3:
                        square(6 + g, oT[:, third(g)])
                    if g >= 1:
                        root(6 + g - 1, 1.0 / DHB)
                act.wait_ge(k.s_final.sem, k.s_final.at(i + 1))
                act.dma_start(k.p_s_out[i], S[:, 0, :]).then_inc(k.s_out.sem, 16)
                act.dma_start(k.s_s_out[i], Sb[:]).then_inc(k.s_out.sem, 16)
                act.dma_start(k.conv_out[i], cout[:]).then_inc(k.s_out.sem, 16)
                act.wait_ge(k.o_scaled.sem, k.o_scaled.at(3 * i + 3))
                act.dma_start(k.yb_dram[i], oT[:, :]).then_inc(k.yb_stored.sem, 16)
            act.wait_ge(k.yb_stored.sem, k.yb_stored.at(16 * HB + 16))
            act.wait_ge(k.s_out.sem, k.s_out.at(48 * HB + 48))
            for b in range(2):
                act.wait_ge(k.kv_slot[b].sem, k.kv_slot[b].at(96 * HB + 32))

        @block.vector
        def _(dve):
            with dve.Fori(0, HB) as i:
                dve.tensor_copy(sh[:], per[:, i]).then_inc(k.per_ready.sem, 1)
                dve.wait_ge(k.s_loaded.sem, k.s_loaded.at(80 * i + 80))
                dve.wait_ge(k.yb_stored.sem, k.yb_stored.at(16 * i + 16))
                for c in range(3):
                    dve.wait_ge(k.pad_landed[c].sem, k.pad_landed[c].at(16 * i + 16))
                    dve.memset(pad[:, c, 0:CW - 1], 0.0)
                    m = dve.tensor_copy(pad[:, c, PADP:].rearrange("p (b c) -> p b c", c=PADS)[:, :, 0:CW - 1],
                                        cst[:, c])
                m.then_inc(k.pad_ready.sem, 1)
                dve.wait_ge(k.pad_ready.sem, k.pad_ready.at(i + 1))
                for c in range(3):
                    pp, ss = pad[:, c, 0:PADP], pad[:, c, PADP:].rearrange("p (b c) -> p b c", c=PADS)
                    yp, ys = y[:, c, 0:SEQ], y[:, c, SEQ:T].rearrange("p (b c) -> p b c", c=DS)
                    for j in range(CW):
                        w = cw[:, c, j:j + 1]
                        if j == 0:
                            dve.tensor_scalar(yp, pp[:, 0:SEQ], w, None, ALU.mult)
                            m = dve.tensor_scalar(ys, ss[:, :, 0:DS], w, None, ALU.mult)
                        else:
                            dve.wait_ge(k.tap.sem, k.tap.at(9 * i + (3 * c + j)))
                            dve.scalar_tensor_tensor(out=yp, in0=pp[:, j:j + SEQ], scalar=w, in1=yp,
                                                     op0=ALU.mult, op1=ALU.add)
                            m = dve.scalar_tensor_tensor(out=ys, in0=ss[:, :, j:j + DS], scalar=w, in1=ys,
                                                         op0=ALU.mult, op1=ALU.add)
                        m.then_inc(k.tap.sem if j < CW - 1 else k.convolved.sem, 1)
                    dve.tensor_copy(cout[:, c, 0:CW - 1], pp[:, SEQ:PADP])
                    dve.tensor_copy(cout[:, c, CW - 1:].rearrange("p (b c) -> p b c", c=CW - 1), ss[:, :, DS:PADS])
                for r in range(6):
                    dve.wait_ge(k.rooted.sem, k.rooted.at(9 * i + (r + 1)))
                    a = y[:, r // 3, third(r % 3)]
                    dve.scalar_tensor_tensor(out=a, in0=a, scalar=DHB ** -0.5 if r < 3 else 1.0, in1=rr[:, r % 2, :],
                                             op0=ALU.mult, op1=ALU.mult).then_inc(k.l2_done.sem, 1)
                for g in range(3):
                    dve.wait_ge(k.eg_ready.sem, k.eg_ready.at(3 * i + (g + 1)))
                    for t in range(3 * g, 3 * g + 3):
                        m = dve.scalar_tensor_tensor(out=DT[:, tile(t)], in0=k.ps[2][:, tile(t % 3)],
                                                     scalar=sh[:, 3, t:t + 1], in1=future if t < 8 else future16,
                                                     op0=ALU.add, op1=ALU.add)
                    m.then_inc(k.dt_args.sem, 1)
                    dve.wait_ge(k.grams.sem, k.grams.at(3 * i + (g + 1)))
                    dve.wait_ge(k.dt_ready.sem, k.dt_ready.at(3 * i + (g + 1)))
                    dve.tensor_tensor(intra[:, third(g)], k.ps[5][:, 0:THIRD], DT[:, third(g)], ALU.mult)
                    dve.tensor_tensor(NT[:, third(g)], k.ps[4][:, 0:THIRD], DT[:, third(g)], ALU.mult)\
                        .then_inc(k.nt_made.sem, 1)
                    dve.tensor_tensor(yq[:, third(g)], yq[:, third(g)], eg[:, third(g)], ALU.mult)\
                        .then_inc(k.qg_ready.sem, 1)
                    dve.wait_ge(k.nt_made.sem, k.nt_made.at(3 * i + (g + 1)))
                    dve.tensor_tensor(NT[:, third(g)], k.ps[3][:, 0:THIRD], NT[:, third(g)], ALU.mult)\
                        .then_inc(k.decayed.sem, 1)
                    dve.wait_ge(k.kv_turned.sem, k.kv_turned.at(3 * i + (g + 1)))
                    for dst, src, n in ((kbe, 6, 1), (kd, 6, 2), (vb, 7, 0)):
                        m = dve.tensor_tensor(by_tile(dst[:, third(g)]), by_tile(k.ps[src][:, 0:THIRD]),
                                              sh[:, n, 3 * g:3 * g + 3].unsqueeze(2).to_broadcast([P, 3, P]), ALU.mult)
                    m.then_inc(k.scaled.sem, 1)
                dve.wait_ge(k.decayed.sem, k.decayed.at(3 * i + 3))

                def repeated(a):
                    return a.unsqueeze(1).to_broadcast([P, 3, P])

                for g in range(3):
                    dve.tensor_tensor(by_tile(MT[:, third(g)]), by_tile(NT[:, third(g)]), repeated(level_mask[0]),
                                      ALU.mult).then_inc(k.first_mask.sem, 1)
                    dve.wait_ge(k.first_mask.sem, k.first_mask.at(3 * i + (g + 1)))
                    dve.scalar_tensor_tensor(out=by_tile(Y[:, third(g)]), in0=by_tile(MT[:, third(g)]), scalar=-1.0,
                                             in1=repeated(k.ident[:, :]), op0=ALU.mult, op1=ALU.add)\
                        .then_inc(k.y_started.sem, 1)

                def mask_level(r):
                    if r >= 3:
                        dve.wait_ge(k.p1_done.sem, k.p1_done.at(LV * i + (r - 2)))
                    g = r % 3
                    dve.tensor_tensor(by_tile(MT[:, third(g)]), by_tile(NT[:, third(g)]),
                                      repeated(level_mask[1 + r // 3]), ALU.mult).then_inc(k.masked_level.sem, 1)

                dve.wait_ge(k.y_started.sem, k.y_started.at(3 * i + 3))
                dve.wait_ge(k.x_started.sem, k.x_started.at(3 * i + 3))
                for r in range(3):
                    mask_level(r)
                for r in range(LV):
                    g = r % 3
                    dve.wait_ge(k.corrected.sem, k.corrected.at(LV * i + (r + 1)))
                    if r < LV - 3:
                        dve.tensor_tensor(X[:, third(g)], X[:, third(g)], bank(4, r)[:, 0:THIRD], ALU.subtract)
                    dve.tensor_tensor(Y[:, third(g)], Y[:, third(g)], bank(6, r)[:, 0:THIRD], ALU.subtract)\
                        .then_inc(k.level_done.sem, 1)
                    if r + 3 < LV:
                        mask_level(r + 3)
                for g in range(3):
                    dve.wait_ge(k.wu_done.sem, k.wu_done.at(3 * i + (g + 1)))
                    dve.wait_ge(k.w_ready.sem, k.w_ready.at(3 * i + (g + 1)))
                    dve.tensor_copy(u[:, third(g)], k.ps[3][:, 0:THIRD]).then_inc(k.u_ready.sem, 1)
                dve.tensor_copy(wz.rearrange("p (b m) -> p b m", b=DB)[:, :, 0:DS],
                                wT[:, SEQ:T].rearrange("p (b c) -> p b c", c=DS)).then_inc(k.wz_ready.sem, 1)
                dve.memset(S[:, 0, :], 0.0).then_inc(k.s_ready.sem, 1)
                dve.wait_ge(k.s_ready.sem, k.s_ready.at(9 * i + 1))
                for t in range(8):
                    dve.wait_ge(k.ws_done.sem, k.ws_done.at(9 * i + (t + 1)))
                    if t >= 2:
                        dve.wait_ge(k.o_done.sem, k.o_done.at(9 * i + (t - 1)))
                    dve.tensor_tensor(vw[:, t % 2, :], u[:, tile(t)], bank(2, t)[:, 0:P], ALU.subtract)\
                        .then_inc(k.vw_ready.sem, 1)
                    dve.wait_ge(k.kv_done.sem, k.kv_done.at(9 * i + (t + 1 + 1)))
                    if t >= 1:
                        dve.wait_ge(k.o_done.sem, k.o_done.at(9 * i + t))
                    last = tile(t).stop - 1
                    dve.scalar_tensor_tensor(out=S[:, (t + 1) % 2, :], in0=S[:, t % 2, :], scalar=eg[:, last:last + 1],
                                             in1=bank(4, t)[:, 0:P], op0=ALU.mult, op1=ALU.add)\
                        .then_inc(k.s_ready.sem, 1)
                    dve.wait_ge(k.s_ready.sem, k.s_ready.at(9 * i + (t + 2)))
                dve.wait_ge(k.ws_done.sem, k.ws_done.at(9 * i + 9))
                dve.wait_ge(k.o_done.sem, k.o_done.at(9 * i + 7))
                dve.tensor_tensor(vw[:, 0, :], u[:, tile(8)], k.ps[2][:, 0:P], ALU.subtract).then_inc(k.vw_ready.sem, 1)
                dve.wait_ge(k.vw_ready.sem, k.vw_ready.at(9 * i + 9))
                dve.tensor_tensor(v8[:], vw[:, 0:1, :].to_broadcast([P, DB, P]),
                                  streams.unsqueeze(2).to_broadcast([P, DB, P]), ALU.mult).then_inc(k.v8_ready.sem, 1)
                dve.wait_ge(k.o_done.sem, k.o_done.at(9 * i + 9))
                dve.tensor_tensor(Sb[:], Sb[:], eg[:, SEQ:T].rearrange("p (b c) -> p b c", c=DS)[:, :, DS - 1:DS]
                                  .to_broadcast([P, DB, P]), ALU.mult).then_inc(k.s_decayed.sem, 1)
                dve.wait_ge(k.kv_done.sem, k.kv_done.at(9 * i + 10))
                dve.wait_ge(k.s_decayed.sem, k.s_decayed.at(i + 1))
                dve.tensor_tensor(Sb[:, 0:4, :], Sb[:, 0:4, :], k.ps[4].rearrange("p (b c) -> p b c", c=P), ALU.add)
                dve.tensor_tensor(Sb[:, 4:8, :], Sb[:, 4:8, :], k.ps[5].rearrange("p (b c) -> p b c", c=P), ALU.add)\
                    .then_inc(k.s_final.sem, 1)
                for g in range(3):
                    dve.wait_ge(k.rooted.sem, k.rooted.at(9 * i + (6 + g + 1)))
                    dve.scalar_tensor_tensor(out=oT[:, third(g)], in0=oT[:, third(g)], scalar=gn[:, 0:1],
                                             in1=rr[:, (6 + g) % 2, :], op0=ALU.mult, op1=ALU.mult)\
                        .then_inc(k.o_normed.sem, 1)
                    dve.wait_ge(k.o_normed.sem, k.o_normed.at(3 * i + (g + 1)))
                    dve.tensor_tensor(oT[:, third(g)], oT[:, third(g)], z[:, third(g)], ALU.mult)\
                        .then_inc(k.o_scaled.sem, 1)

    units_done(k, HB, 4)
    for b in range(2):
        k.kv_slot[b].base += 96 * HB
    for c in range(3):
        k.pad_landed[c].base += 16 * HB
    k.z_landed.base += 16 * HB
    for sig, n in ((k.evacuated, 12), (k.dense_done, 12), (k.squared, 9), (k.lned, 9), (k.sq_summed, 9), (k.rooted, 9),
                   (k.per_ready, 1), (k.decayed, 3), (k.scaled, 3), (k.rows_spread, 3), (k.l2_done, 6), (k.grams, 3),
                   (k.kv_turned, 3), (k.y_started, 3), (k.y_turned, 3), (k.x_started, 3), (k.masked_level, LV),
                   (k.p1_ready, LV), (k.p1_done, LV), (k.level_done, LV), (k.corrected, LV), (k.w_ready, 3),
                   (k.u_ready, 3), (k.wu_done, 3), (k.s_ready, 9), (k.ws_done, 9), (k.o_copied, 9), (k.qg_ready, 3),
                   (k.vw_ready, 9), (k.kv_done, 9), (k.o_done, 9), (k.s_loaded, 80), (k.wz_ready, 1), (k.v8_ready, 1),
                   (k.pad_ready, 1), (k.silued, 4), (k.convolved, 3), (k.eg_ready, 3), (k.dt_args, 3), (k.dt_ready, 3),
                   (k.s_final, 1), (k.s_out, 48), (k.o_scaled, 3), (k.o_normed, 3), (k.yb_stored, 16), (k.tap, 9),
                   (k.nt_made, 3), (k.first_mask, 3), (k.s_decayed, 1)):
        sig.base += n * HB


def memory_phase(nc, k, xh, xl, work, first_unit):
    TURNS, TURN = 4, 4
    kv = nc.alloc_sbuf_tensor_at("m_kv", [P, 2, NMEM], F32, offset=work)
    nat = nc.alloc_sbuf_tensor_at("m_nat", [P, 2, NMEM], F32, offset=work + 8 * NMEM)
    with nc.Block() as block:
        @block.sync
        def _(sp):
            load_units(sp, k, first_unit, TURNS, TURN)

        @block.gpsimd
        def _(pool):
            split_units(pool, k, TURNS, (1, 2, 3, 4))

        @block.tensor
        def _(pe):
            with pe.Fori(0, TURNS) as i:
                for j in range(TURN):
                    s = j % RING
                    pe.wait_ge(k.unit_split.sem, k.unit_split.at(TURN * i + (j + 1)))
                    pe.wait_ge(k.evacuated.sem, k.evacuated.at(TURN * i + (j + 1)))
                    tiles = [(k.w_hi[s][:, c * P:(c + 1) * P], k.w_lo[s][:, c * P:(c + 1) * P], xh[:, c, :], xl[:, c, :])
                             for c in range(KD)]
                    product(pe, k.ps[j % 2][:, 0:NMEM], tiles, 0, NMEM).then_inc(k.dense_done.sem, 1)
                    pe.wait_ge(k.evacuated.sem, k.evacuated.at(TURN * i + (j + 1 + 2)))
                    for h in range(2):
                        mm = pe.transpose(k.ps[2 + j % 2][:, h * P:(h + 1) * P], kv[:, j % 2, h * P:(h + 1) * P],
                                          k.ident[:, :])
                    mm.then_inc(k.turned.sem, 1)

        @block.scalar
        def _(act):
            with act.Fori(0, TURNS) as i:
                for j in range(TURN):
                    act.wait_ge(k.dense_done.sem, k.dense_done.at(TURN * i + (j + 1)))
                    act.wait_ge(k.kv_slot[j % 2].sem, k.kv_slot[j % 2].at(32 * (TURN // 2) * i + (32 * (j // 2) + 32)))
                    act.activation(kv[:, j % 2, :], k.ps[j % 2][:, 0:NMEM], ACT.Copy).then_inc(k.evacuated.sem, 1)
                    act.wait_ge(k.evacuated.sem, k.evacuated.at(TURN * i + (j + 1 + 2)))
                    act.dma_start(k.mem_out[TURN * i + j], kv[:, j % 2, :]).then_inc(k.kv_slot[j % 2].sem, 16)
                    act.wait_ge(k.turned.sem, k.turned.at(TURN * i + (j + 1)))
                    act.activation(nat[:, j % 2, :], k.ps[2 + j % 2][:, 0:NMEM], ACT.Copy).then_inc(k.pt_ready.sem, 1)
                    act.wait_ge(k.pt_ready.sem, k.pt_ready.at(TURN * i + (j + 1)))
                    act.dma_start(k.mem_turned[TURN * i + j], nat[:, j % 2, :]).then_inc(k.kv_slot[j % 2].sem, 16)
            for b in range(2):
                act.wait_ge(k.kv_slot[b].sem, k.kv_slot[b].at(32 * (TURNS * TURN // 2) + 32))

    units_done(k, TURNS, TURN)
    n = TURNS * TURN
    for sig in (k.dense_done, k.evacuated, k.turned, k.pt_ready):
        sig.base += n
    for b in range(2):
        k.kv_slot[b].base += 16 * n


def gather_phase(nc, k, name, chunks, hi, lo, work):
    st = nc.alloc_sbuf_tensor_at(name + "_st", [P, 2, T], F32, offset=work)
    with nc.Block() as block:
        @block.sync
        def _(sp):
            for c in range(KD):
                if c >= 2:
                    sp.wait_ge(k.nsplit.sem, k.nsplit.at(c - 1))
                sp.dma_start(st[:, c % 2, :], chunks[c]).then_inc(k.nout[c % 2].sem, 16)

        @block.scalar
        def _(act):
            for c in range(KD):
                act.wait_ge(k.nout[c % 2].sem, k.nout[c % 2].at(16 * (c // 2 + 1)))
                act.activation(hi[:, c, :], st[:, c % 2, :], ACT.Copy).then_inc(k.nhi.sem, 1)

        @block.vector
        def _(dve):
            for c in range(KD):
                dve.wait_ge(k.nhi.sem, k.nhi.at(c + 1))
                dve.wait_ge(k.nout[c % 2].sem, k.nout[c % 2].at(16 * (c // 2 + 1)))
                dve.tensor_tensor(lo[:, c, :], st[:, c % 2, :], hi[:, c, :].bitcast(F32), ALU.subtract)\
                    .then_inc(k.nsplit.sem, 1)

    k.nhi.base += KD
    k.nsplit.base += KD
    for b in range(2):
        k.nout[b].base += 16 * KD // 2


def merge_phase(nc, k, yh, yl, hi, lo, work, first_unit):
    TURNS = 2
    gt = nc.alloc_sbuf_tensor_at("e_gate", [P, 2, 2, THIRD], F32, offset=work)
    a1 = nc.alloc_sbuf_tensor_at("e_a", [P, 2, THIRD], F32, offset=work + 16 * THIRD)
    b1 = nc.alloc_sbuf_tensor_at("e_b", [P, 2, THIRD], F32, offset=work + 24 * THIRD)
    m1 = nc.alloc_sbuf_tensor_at("e_m", [P, 2, THIRD], F32, offset=work + 32 * THIRD)
    JOBS = 12

    def chunk(a, i, j):
        return a[:, 4 * i + j // 3, j % 3 * THIRD:(j % 3 + 1) * THIRD]

    with nc.Block() as block:
        @block.sync
        def _(sp):
            load_units(sp, k, first_unit, TURNS, 4)

        @block.gpsimd
        def _(pool):
            split_units(pool, k, TURNS, (12, 12, 24, 24))

        @block.tensor
        def _(pe):
            with pe.Fori(0, TURNS) as i:
                for j in range(JOBS):
                    m, n = j // 3, j % 3
                    if j % 6 == 0:
                        pe.wait_ge(k.unit_split.sem, k.unit_split.at(4 * i + (2 * (j // 6) + 2)))
                    pe.wait_ge(k.merged.sem, k.merged.at(JOBS * i + (j + 1)))
                    for ab in range(2):
                        s = (2 * (m // 2) + ab) % RING
                        tiles = [(k.w_hi[s][:, c * P:(c + 1) * P], k.w_lo[s][:, c * P:(c + 1) * P],
                                  yh[:, 4 * ab + c % 4, :], yl[:, 4 * ab + c % 4, :])
                                 for c in range(4 * (m % 2), 4 * (m % 2) + 4)]
                        product(pe, k.ps[2 * (j % 2) + ab][:, 0:THIRD], tiles, n * THIRD, (n + 1) * THIRD)\
                            .then_inc(k.dense_done.sem, 1)

        @block.scalar
        def _(act):
            def load(i, j):
                for ab in range(2):
                    act.dma_start(gt[:, j % 2, ab, :],
                                  k.gate_dram[4 * i + (8 * ab + j // 3)][:, j % 3 * THIRD:(j % 3 + 1) * THIRD])\
                        .then_inc(k.kv_slot[j % 2].sem, 16)

            def gates(i, j):
                act.wait_ge(k.kv_slot[j % 2].sem, k.kv_slot[j % 2].at(16 * JOBS * i + (32 * (j // 2) + 32 + 32)))
                act.activation(gt[:, j % 2], gt[:, j % 2], ACT.Sigmoid).then_inc(k.gate_sigmoid.sem, 1)

            for i in range(TURNS):
                for j in range(JOBS):
                    if j == 0:
                        load(i, 0)
                        load(i, 1)
                        gates(i, 0)
                    if j + 1 < JOBS:
                        gates(i, j + 1)
                    act.wait_ge(k.merged.sem, k.merged.at(JOBS * i + (j + 1 + 2)))
                    act.activation(chunk(hi, i, j), m1[:, j % 2, :], ACT.Copy).then_inc(k.nhi.sem, 1)
                    if j + 2 < JOBS:
                        load(i, j + 2)

        @block.vector
        def _(dve):
            for i in range(TURNS):
                for j in range(JOBS):
                    dve.wait_ge(k.dense_done.sem, k.dense_done.at(2 * JOBS * i + (2 * j + 2)))
                    dve.wait_ge(k.gate_sigmoid.sem, k.gate_sigmoid.at(JOBS * i + (j + 1)))
                    dve.tensor_tensor(a1[:, j % 2, :], k.ps[2 * (j % 2)][:, 0:THIRD], gt[:, j % 2, 0, :], ALU.mult)
                    dve.tensor_tensor(b1[:, j % 2, :], k.ps[2 * (j % 2) + 1][:, 0:THIRD], gt[:, j % 2, 1, :], ALU.mult)\
                        .then_inc(k.gated.sem, 1)
                    dve.wait_ge(k.gated.sem, k.gated.at(JOBS * i + (j + 1)))
                    dve.tensor_tensor(m1[:, j % 2, :], a1[:, j % 2, :], b1[:, j % 2, :], ALU.add)\
                        .then_inc(k.merged.sem, 1)
                    dve.wait_ge(k.nhi.sem, k.nhi.at(JOBS * i + (j + 1)))
                    dve.tensor_tensor(chunk(lo, i, j), m1[:, j % 2, :], chunk(hi, i, j).bitcast(F32),
                                      ALU.subtract).then_inc(k.nsplit.sem, 1)

    units_done(k, TURNS, 4)
    k.dense_done.base += 2 * JOBS * TURNS
    for sig in (k.merged, k.gated, k.gate_sigmoid, k.nhi, k.nsplit):
        sig.base += JOBS * TURNS
    for b in range(2):
        k.kv_slot[b].base += 16 * JOBS * TURNS


def residual_phase(nc, k, x, xh, xl, first_unit):
    TURNS, TURN = 2, 4
    with nc.Block() as block:
        @block.sync
        def _(sp):
            load_units(sp, k, first_unit, TURNS, TURN)

        @block.gpsimd
        def _(pool):
            split_units(pool, k, TURNS, (3, 6, 9, 12))

        @block.tensor
        def _(pe):
            for i in range(TURNS):
                for j in range(3 * TURN):
                    s = j // 3 % RING
                    if j % 3 == 0:
                        pe.wait_ge(k.unit_split.sem, k.unit_split.at(TURN * i + (j // 3 + 1)))
                    pe.wait_ge(k.x_added.sem, k.x_added.at(12 * i + (j + 1)))
                    tiles = [(k.w_hi[s][:, c * P:(c + 1) * P], k.w_lo[s][:, c * P:(c + 1) * P], xh[:, c, :], xl[:, c, :])
                             for c in range(KD)]
                    product(pe, k.ps[j % NPS][:, 0:THIRD], tiles, j % 3 * THIRD, (j % 3 + 1) * THIRD)\
                        .then_inc(k.dense_done.sem, 1)

        @block.vector
        def _(dve):
            for i in range(TURNS):
                for j in range(3 * TURN):
                    dve.wait_ge(k.dense_done.sem, k.dense_done.at(12 * i + (j + 1)))
                    xs = x[:, TURN * i + j // 3, j % 3 * THIRD:(j % 3 + 1) * THIRD]
                    dve.tensor_tensor(xs, xs, k.ps[j % NPS][:, 0:THIRD], ALU.add).then_inc(k.x_added.sem, 1)

    units_done(k, TURNS, TURN)
    for sig in (k.dense_done, k.x_added):
        sig.base += 12 * TURNS


def cross_phase(nc, k, xh, xl, room1, room2, first_unit):
    at = {1: room1, 2: room2}

    def sb(name, room, shape):
        t = nc.alloc_sbuf_tensor_at(name, shape, F32, offset=at[room])
        at[room] += (4 * int(np.prod(shape[1:])) + 31) // 32 * 32
        return t

    q, oc = sb("x_q", 1, [P, 2, T]), sb("x_o", 1, [P, 2, T])
    mk, mv = sb("x_mk", 1, [P, 2, NMEM]), sb("x_mv", 1, [P, 2, 2, P])
    qz = sb("x_qz", 1, [P, 2, DB, 32])
    sk = sb("x_sk", 2, [P, 2, DB, NMEM])
    sv = [sb("x_sv0", 1, [P, 4, 2, DHX]), sb("x_sv1", 2, [P, 4, 2, DHX])]
    sc, pt = sb("x_sc", 1, [P, 2, NMEM]), sb("x_pt", 1, [P, 2, 2, P])
    nmax, rsum, rinv = (sb(n, 2, [P, 2]) for n in ("x_nmax", "x_rsum", "x_rinv"))
    STEPS, LOADS = 9, 7

    def bank(a, b):
        return k.ps[a + b % 2]

    with nc.Block() as block:
        @block.sync
        def _(sp):
            load_units(sp, k, first_unit, HX, 2)

        @block.gpsimd
        def _(pool):
            split_units(pool, k, HX, (3, 6))

        @block.tensor
        def _(pe):
            def scores(i, s):
                pe.wait_ge(k.score_read.sem, k.score_read.at(STEPS * i + (s + 1)))
                o = bank(2, s)
                if s < 8:
                    for c in range(2):
                        mm = pe.matmul(o[:, 0:NMEM], q[:, c, s * P:(s + 1) * P], mk[:, c, :], start=(c == 0),
                                       stop=(c == 1))
                else:
                    for b in range(DB):
                        r = 32 * (b // 2)
                        for c in range(2):
                            mm = pe.matmul(o[r:r + 32, 0:NMEM], qz[:, c, b, :], sk[:, c, b, :],
                                           start=(b % 2 == 0 and c == 0), stop=(b % 2 == 1 and c == 1),
                                           tile_position=(0, r))
                mm.then_inc(k.scored.sem, 1)

            def turn_probs(i, s):
                pe.wait_ge(k.normed.sem, k.normed.at(STEPS * i + (s + 1)))
                if s >= 2:
                    pe.wait_ge(k.pt_ready.sem, k.pt_ready.at(STEPS * i + (s - 1)))
                for j in range(2):
                    mm = pe.transpose(bank(4, s)[:, j * P:(j + 1) * P], sc[:, s % 2, j * P:(j + 1) * P], k.ident[:, :])
                mm.then_inc(k.turned.sem, 1)

            def values(i, s):
                pe.wait_ge(k.pt_ready.sem, k.pt_ready.at(STEPS * i + (s + 1)))
                if s >= 2:
                    pe.wait_ge(k.o_read.sem, k.o_read.at(STEPS * i + (s - 1)))
                o = bank(6, s)
                for c in range(2):
                    if s < 8:
                        for j in range(2):
                            mm = pe.matmul(o[:, c * P:(c + 1) * P], mv[:, c, j, :], pt[:, s % 2, j, :],
                                           start=(j == 0), stop=(j == 1))
                        continue
                    for b in range(DB):
                        for j in range(2):
                            mm = pe.matmul(o[:, c * P + DS * b:c * P + DS * (b + 1)],
                                           sv[b // 4][:, b % 4, j, c * P:(c + 1) * P], pt[:, s % 2, j, DS * b:DS * (b + 1)],
                                           start=(j == 0), stop=(j == 1))
                mm.then_inc(k.valued.sem, 1)

            with pe.Fori(0, HX) as i:
                for g in range(6):
                    if g % 3 == 0:
                        pe.wait_ge(k.unit_split.sem, k.unit_split.at(2 * i + (g // 3 + 1)))
                    pe.wait_ge(k.evacuated.sem, k.evacuated.at(6 * i + (g + 1)))
                    s = g // 3
                    tiles = [(k.w_hi[s][:, c * P:(c + 1) * P], k.w_lo[s][:, c * P:(c + 1) * P], xh[:, c, :], xl[:, c, :])
                             for c in range(KD)]
                    product(pe, k.ps[g % 2][:, 0:THIRD], tiles, g % 3 * THIRD, (g % 3 + 1) * THIRD)\
                        .then_inc(k.dense_done.sem, 1)
                pe.wait_ge(k.evacuated.sem, k.evacuated.at(6 * i + 8))
                pe.wait_ge(k.a_loaded.sem, k.a_loaded.at(16 * LOADS * i + 16 * LOADS))
                pe.wait_ge(k.qbd_ready.sem, k.qbd_ready.at(i + 1))
                for s in range(STEPS + 2):
                    if s < STEPS:
                        scores(i, s)
                    if s >= 2:
                        values(i, s - 2)
                    if 1 <= s <= STEPS:
                        turn_probs(i, s - 1)

        @block.scalar
        def _(act):
            with act.Fori(0, HX) as i:
                act.wait_ge(k.valued.sem, k.valued.at(STEPS * i + 1))
                for dst, src in ((mk[:], k.mem_out[bass.ds(2 * i, 2)].rearrange("c p m -> p c m")),
                                 (mv[:].rearrange("p c j d -> p c (j d)"),
                                  k.mem_turned[bass.ds(2 * i + 8, 2)].rearrange("c p m -> p c m")),
                                 (sk[:, 0], k.mem_k[i][:, 0]), (sk[:, 1], k.mem_k[i][:, 1]),
                                 (sv[0][:, 0:4], k.mem_v[i][:, 0:4]), (sv[1][:, 0:2], k.mem_v[i][:, 4:6]),
                                 (sv[1][:, 2:4], k.mem_v[i][:, 6:8])):
                    act.dma_start(dst, src).then_inc(k.a_loaded.sem, 16)
                for g in range(6):
                    act.wait_ge(k.dense_done.sem, k.dense_done.at(6 * i + (g + 1)))
                    act.activation(q[:, g // 3, g % 3 * THIRD:(g % 3 + 1) * THIRD], k.ps[g % 2][:, 0:THIRD], ACT.Copy,
                                   scale=DHX ** -0.5).then_inc(k.evacuated.sem, 1)

                def exps(s):
                    act.wait_ge(k.maxed.sem, k.maxed.at(STEPS * i + (s + 1)))
                    if s >= 2:
                        act.wait_ge(k.turned.sem, k.turned.at(STEPS * i + (s - 1)))
                    b = s % 2
                    act.activation(sc[:, b, :], bank(2, s)[:, 0:NMEM], ACT.Exp, bias=nmax[:, b:b + 1],
                                   accum_out=rsum[:, b:b + 1]).then_inc(k.score_read.sem, 1)

                def copy_turned(s):
                    act.wait_ge(k.turned.sem, k.turned.at(STEPS * i + (s + 1)))
                    if s >= 2:
                        act.wait_ge(k.valued.sem, k.valued.at(STEPS * i + (s - 1 + 1)))
                    act.activation(pt[:, s % 2].rearrange("p j c -> p (j c)"), bank(4, s)[:, 0:NMEM], ACT.Copy)\
                        .then_inc(k.pt_ready.sem, 1)

                def copy_o(s):
                    act.wait_ge(k.valued.sem, k.valued.at(STEPS * i + (s + 1 + 1)))
                    if s == 0:
                        act.wait_ge(k.ya_stored.sem, k.ya_stored.at(16 * i + 16))
                    act.activation(oc[:, :, s * P:(s + 1) * P], bank(6, s)[:, 0:2 * P].rearrange("p (c t) -> p c t", c=2),
                                   ACT.Copy).then_inc(k.o_read.sem, 1)

                for s in range(STEPS + 3):
                    if s < STEPS:
                        exps(s)
                    if 1 <= s <= STEPS:
                        copy_turned(s - 1)
                    if s >= 3:
                        copy_o(s - 3)
                act.wait_ge(k.o_read.sem, k.o_read.at(STEPS * i + STEPS))
                act.dma_start(k.o_dram[bass.ds(2 * i, 2)].rearrange("c p t -> p c t"), oc[:]).then_inc(k.ya_stored.sem, 16)
            act.wait_ge(k.ya_stored.sem, k.ya_stored.at(16 * HX + 16))

        @block.vector
        def _(dve):
            dve.memset(qz[:], 0.0).then_inc(k.qbd_zero.sem, 1)
            dve.wait_ge(k.qbd_zero.sem, k.qbd_zero.at(1))
            with dve.Fori(0, HX) as i:
                dve.wait_ge(k.evacuated.sem, k.evacuated.at(6 * i + 8))
                for c in range(2):
                    qs = q[:, c, SEQ:T].rearrange("p (b w c) -> p w b c", w=2, c=DS)
                    for odd in range(2):
                        m = dve.tensor_copy(qz[:, c].rearrange("p (b w) c -> p w b c", w=2)[:, odd, :,
                                                                                              DS * odd:DS * (odd + 1)],
                                            qs[:, odd])
                m.then_inc(k.qbd_ready.sem, 1)

                def logits(s):
                    dve.wait_ge(k.scored.sem, k.scored.at(STEPS * i + (s + 1)))
                    if s >= 2:
                        dve.wait_ge(k.score_read.sem, k.score_read.at(STEPS * i + (s - 1 + 2)))
                    dve.tensor_reduce(nmax[:, s % 2:s % 2 + 1], bank(2, s)[:, 0:NMEM], AX_X, ALU.max, negate=True)\
                        .then_inc(k.maxed.sem, 1)

                def normalise(s):
                    b = s % 2
                    dve.wait_ge(k.score_read.sem, k.score_read.at(STEPS * i + (s + 1 + 2)))
                    dve.reciprocal(rinv[:, b:b + 1], rsum[:, b:b + 1]).then_inc(k.inverted.sem, 1)
                    dve.wait_ge(k.inverted.sem, k.inverted.at(STEPS * i + (s + 1)))
                    dve.tensor_scalar(sc[:, b, :], sc[:, b, :], rinv[:, b:b + 1], None, ALU.mult)\
                        .then_inc(k.normed.sem, 1)

                for s in range(STEPS + 1):
                    if s < STEPS:
                        logits(s)
                    if s >= 1:
                        normalise(s - 1)

    units_done(k, HX, 2)
    k.qbd_zero.base += 1
    for sig, n in ((k.dense_done, 6), (k.evacuated, 6), (k.scored, STEPS), (k.maxed, STEPS), (k.score_read, STEPS),
                   (k.inverted, STEPS), (k.normed, STEPS), (k.turned, STEPS), (k.pt_ready, STEPS), (k.valued, STEPS),
                   (k.o_read, STEPS), (k.a_loaded, 16 * LOADS), (k.ya_stored, 16), (k.qbd_ready, 1)):
        sig.base += n * HX




OUTPUTS = {"y_out": (KD, P, T), "a_k_out": (4, P, T), "a_v_out": (4, P, T), "conv_out": (HB, P, 3, (DB + 1) * (CW - 1)),
           "p_s_out": (HB, P, P), "s_s_out": (HB, P, DB, P), "mem_out": (2 * KD, P, NMEM)}
SCRATCH = {"bias_dram": (P, HA * NBIAS + 256), "ya_dram": (4, P, T), "yb_dram": (4, P, T), "x_dram": (KD, P, T),
           "proj_dram": (4 * HB, P, PADDED), "gate_dram": (2 * KD, P, T), "mem_turned": (2 * KD, P, NMEM), "o_dram": (KD, P, T)}


def copy_x(nc, k, dst, src):
    with nc.Block() as block:
        @block.sync
        def _(sp):
            sp.dma_start(dst, src).then_inc(k.loaded.sem, 16)
            sp.wait_ge(k.loaded.sem, k.loaded.at(16))

    k.loaded.base += 16


def hybrid_layer(nc, io):
    with ExitStack() as ctx:
        k = Core(nc, ctx)
        k.units, k.xt, k.memt, k.gains_dram, k.ident_dram = (io[n] for n in ("units", "xt", "memt", "gains_dram",
                                                                             "ident_dram"))
        k.table, k.k_cache, k.v_cache = io["table"], io["k_cache"], io["v_cache"]
        k.b_consts, k.w_beta_decay, k.a_log, k.dt_bias = (io[n] for n in ("b_consts", "w_beta_decay", "a_log", "dt_bias"))
        k.b_gain, k.conv_state, k.conv_w, k.state_s = io["b_gain"], io["conv_state"], io["conv_w"], io["state_s"]
        k.mem_k, k.mem_v = io["mem_k"], io["mem_v"]
        k.y_out, k.a_k_out, k.a_v_out, k.conv_out = io["y_out"], io["a_k_out"], io["a_v_out"], io["conv_out"]
        k.p_s_out, k.s_s_out, k.mem_out = io["p_s_out"], io["s_s_out"], io["mem_out"]
        k.bias_dram, k.ya_dram, k.yb_dram, k.x_dram = io["bias_dram"], io["ya_dram"], io["yb_dram"], io["x_dram"]
        k.proj_dram = io["proj_dram"]
        k.gate_dram, k.mem_turned, k.o_dram = io["gate_dram"], io["mem_turned"], io["o_dram"]
        k.bias_pitch = HA * NBIAS + 256
        k.bias_dram_flat = k.bias_dram.rearrange("p m -> (p m)")
        big = KD * T * 4
        r1 = k.arena
        r2 = r1 + 2 * big

        def split_pair(name, at):
            return (nc.alloc_sbuf_tensor_at(name + "_hi", [P, KD, T], F32R, offset=at),
                    nc.alloc_sbuf_tensor_at(name + "_lo", [P, KD, T], F32R, offset=at + big))

        xh1, xl1 = split_pair("x1", r1)
        xh2, xl2 = split_pair("x2", r2)
        x_early = nc.alloc_sbuf_tensor_at("x_early", [P, KD, T], F32, offset=r2)
        x_late = nc.alloc_sbuf_tensor_at("x_late", [P, KD, T], F32, offset=r1)
        mem = nc.alloc_sbuf_tensor_at("mem", [P, KD, NMEM], F32, offset=r2 + big)
        mh = nc.alloc_sbuf_tensor_at("mem_hi", [P, KD, NMEM], F32R, offset=r1)
        ml = nc.alloc_sbuf_tensor_at("mem_lo", [P, KD, NMEM], F32R, offset=r1 + KD * NMEM * 4)

        def gain(n):
            return k.gains[:, n * KD:(n + 1) * KD]

        with nc.Block() as block:
            @block.sync
            def _(sp):
                for dst, src in ((x_early[:], k.xt.rearrange("c p t -> p c t")), (mem[:], k.memt.rearrange("c p t -> p c t")),
                                 (k.gains[:], k.gains_dram), (k.ident[:], k.ident_dram)):
                    sp.dma_start(dst, src).then_inc(k.loaded.sem, 16)
                sp.wait_ge(k.loaded.sem, k.loaded.at(64))
                for s, n in k.tokens:
                    sp.sem_inc(s.sem, n)

            @block.vector
            def _(dve):
                dve.memset(k.ones[:, :], 1.0)
                dve.memset(k.eps[:, :], EPS)
                dve.memset(k.zero[:, :], 0.0)

        k.loaded.base += 64
        make_bias_rows(nc, k, r1)
        work = r2 + big + 4 * KD * NMEM
        unit = 0
        norm_phase(nc, k, "nm", mem, gain(4), mh, ml, work, NMEM, NMEM)
        memory_phase(nc, k, mh, ml, work, unit)
        unit += 2 * KD
        work = r2 + big
        norm_phase(nc, k, "n1", x_early, gain(0), xh1, xl1, work, T, THIRD)
        ffn_phase(nc, k, "f1", x_early, xh1, xl1, work, unit)
        unit += 3 * NFF
        norm_phase(nc, k, "n2", x_early, gain(1), xh1, xl1, work, T, THIRD)
        copy_x(nc, k, k.x_dram.rearrange("c p t -> p c t"), x_early[:])
        attention_phase(nc, k, xh1, xl1, r2, unit)
        unit += 28
        delta_phase(nc, k, xh1, xl1, r2, unit)
        unit += 16
        gather_phase(nc, k, "gy", [k.ya_dram[c] for c in range(4)] + [k.yb_dram[c] for c in range(4)], xh1, xl1, r2)
        merge_phase(nc, k, xh1, xl1, xh2, xl2, r2 + 2 * big, unit)
        unit += 8
        copy_x(nc, k, x_late[:], k.x_dram.rearrange("c p t -> p c t"))
        residual_phase(nc, k, x_late, xh2, xl2, unit)
        unit += 8
        work = r1 + big
        norm_phase(nc, k, "n3", x_late, gain(2), xh2, xl2, work, T, THIRD)
        cross_phase(nc, k, xh2, xl2, work, r2 + 2 * big, unit)
        unit += 8
        gather_phase(nc, k, "go", [k.o_dram[c] for c in range(KD)], xh2, xl2, work)
        residual_phase(nc, k, x_late, xh2, xl2, unit)
        unit += 8
        norm_phase(nc, k, "n4", x_late, gain(3), xh2, xl2, work, T, THIRD)
        ffn_phase(nc, k, "f2", x_late, xh2, xl2, work, unit)
        norm_phase(nc, k, "n5", x_late, gain(5), None, None, work, T, THIRD, out=k.y_out.rearrange("c p t -> p c t"))



def stationary(w):
    kk, m = w.shape
    return w.reshape(kk // P, P, m // P, P).transpose(2, 1, 0, 3).reshape(m // P, P, kk)


def weight_units(a):
    units = list(stationary(a["xattn_wk"])) + list(stationary(a["xattn_wv"]))

    def ffn(n):
        g, u, d = stationary(a[n + "_w_gate"]), stationary(a[n + "_w_up"]), a[n + "_w_down"].reshape(NFF, P, D)
        for i in range(0, NFF, 2):
            units.extend([g[i], u[i], g[i + 1], u[i + 1], d[i], d[i + 1]])

    ffn("ffn1")
    w_in = a["w_in"]
    wa, wb = 3 * HA * DHA, 4 * HB * DHB
    mixer_a = stationary(w_in[:, 0:wa])
    mixer_b = stationary(w_in[:, wa:wa + wb])
    for p in range(4):
        units.extend([mixer_a[4 * j + p] for j in range(3)] + [mixer_b[4 * j + p] for j in range(4)])
    units.extend(stationary(w_in[:, wa + wb + 2 * HB:]))
    ba, bb = (stationary(a[n]).reshape(4, 2, P, 512).transpose(0, 2, 1, 3).reshape(4, P, D)
              for n in ("w_branch_a", "w_branch_b"))
    for j in range(4):
        units.extend([ba[j], bb[j]])
    for n in ("w_mix_out", "xattn_wq", "xattn_wo"):
        units.extend(stationary(a[n]))
    ffn("ffn2")
    return np.stack(units)


def kernel(**inputs):
    import concourse.bacc as bacc
    from concourse.bass_utils import run_bass_kernel_spmd as run

    def features(x):
        return x.reshape(-1, D).T.reshape(KD, P, -1)

    a = {n: np.asarray(v) for n, v in inputs.items()}
    for n in a:
        if n not in ("x_prompt", "x_sample", "mem_prompt", "final_norm"):
            a[n] = a[n][0]
    wa, wb = 3 * HA * DHA, 4 * HB * DHB
    arrays = {
        "units": weight_units(a),
        "xt": np.concatenate([features(a["x_prompt"]), features(a["x_sample"])], axis=2),
        "memt": features(a["mem_prompt"]),
        "gains_dram": np.concatenate([a[n].reshape(KD, P).T for n in ("ffn1_norm", "mix_norm", "xattn_norm",
                                                                      "ffn2_norm", "mem_norm", "final_norm")], axis=1),
        "ident_dram": np.eye(P, dtype=np.float32),
        "table": a["a_rel_bias"][:, ::-1],
        "k_cache": a["cache_a_k"].reshape(DB, REACH, 4, P).transpose(2, 3, 0, 1),
        "v_cache": a["cache_a_v"].reshape(DB, 4, P, 4, P).transpose(3, 2, 0, 1, 4),
        "b_consts": delta_constants(),
        "w_beta_decay": a["w_in"][:, wa + wb:wa + wb + 2 * HB].reshape(KD, P, 2 * HB).transpose(1, 0, 2),
        "a_log": a["b_a_log"].reshape(HB), "dt_bias": a["b_dt_bias"].reshape(HB),
        "b_gain": a["b_out_norm"].reshape(P, 1),
        "conv_state": a["state_b_conv"].reshape(DB, CW - 1, 3, HB, P).transpose(3, 4, 2, 0, 1),
        "conv_w": a["b_conv_w"].reshape(CW, 3, HB, P).transpose(2, 3, 1, 0),
        "state_s": a["state_b_s"].transpose(1, 2, 0, 3),
        "mem_k": a["cache_mem_k"].reshape(DB, NMEM, HX, 2, P).transpose(2, 4, 3, 0, 1),
        "mem_v": a["cache_mem_v"].reshape(DB, 2, P, HX, DHX).transpose(3, 2, 0, 1, 4),
    }
    arrays = {n: np.ascontiguousarray(v) for n, v in arrays.items()}
    nc = bacc.Bacc("TRN2", target_bir_lowering=False, num_devices=1)
    io = {n: nc.dram_tensor(n, v.shape, F32, kind="ExternalInput").ap() for n, v in arrays.items()}
    for n, shape in OUTPUTS.items():
        io[n] = nc.dram_tensor(n, shape, F32, kind="ExternalOutput").ap()
    for n, shape in SCRATCH.items():
        io[n] = nc.dram_tensor(n, shape, F32, kind="Internal").ap()
    hybrid_layer(nc, io)
    r = run(nc, [arrays], core_ids=[0]).results[0]

    def frames(o):
        o = o.reshape(-1, T).T
        return o[:SEQ], o[SEQ:]

    yp, ys = frames(r["y_out"])
    kp, ks = frames(r["a_k_out"])
    vp, vs = frames(r["a_v_out"])
    conv = r["conv_out"].reshape(HB, P, 3, DB + 1, CW - 1).transpose(3, 4, 2, 0, 1).reshape(DB + 1, CW - 1, -1)
    mk, mv = (r["mem_out"][n * KD:(n + 1) * KD].reshape(D, NMEM).T.reshape(1, 1, NMEM, HX, DHX) for n in range(2))
    keep = min(REACH, SEQ)
    return (yp.reshape(1, SEQ, D), ys.reshape(DB, DS, D),
            kp[SEQ - keep:].reshape(1, 1, keep, HA, DHA), vp[SEQ - keep:].reshape(1, 1, keep, HA, DHA),
            conv[None, 0:1], r["p_s_out"][None, None], mk, mv,
            ks.reshape(1, DB, DS, HA, DHA), vs.reshape(1, DB, DS, HA, DHA),
            conv[None, 1:], r["s_s_out"].transpose(2, 0, 1, 3)[None])
```

```python
from contextlib import ExitStack

import numpy as np

import concourse.bass as bass
from concourse import mybir

F32 = mybir.dt.float32
F32R = mybir.dt.float32r
ALU = mybir.AluOpType
ACT = mybir.ActivationFunctionType
AX_X = mybir.AxisListType.X

P = 128
D = 1024
KD = D // P
SEQ = 1024
DB, DS = 8, 16
T = SEQ + DB * DS
NT_TILES = T // P
THIRD = T // 3
FF = 2816
NFF = FF // P
HA, DHA, REACH, REL = 8, 64, 512, 128
HB, DHB, CW = 4, 128, 4
HX, DHX, NMEM = 4, 256, 256
WIN = REACH + P
NBIAS = WIN + P
PADP, PADS = SEQ + CW - 1, DS + CW - 1
PADDED = PADP + DB * PADS
NEG = -1e30
EPS = 1e-6
RING = 3
NPS = 4


class Counter:

    def __init__(self, nc, ctx, name):
        self.sem = ctx.enter_context(nc.semaphore(name))
        self.base = 0

    def at(self, k):
        return self.base + k



def slot(j, turn):
    return 1 if turn % RING == 1 and j == turn - 1 else j % RING


def sharing(j, turn):
    return [u for u in range(turn) if slot(u, turn) == slot(j, turn)]


def last_use(j, turn):
    same = sharing(j, turn)
    at = same.index(j)
    return (0, same[at - 1]) if at else (1, same[-1])


def load_units(sp, k, first, turns, turn, at_turn=None):
    def one(i, j):
        back, last = last_use(j, turn)
        if not (isinstance(i, int) and i < back):
            sp.wait_ge(k.unit_split.sem, k.unit_split.at(turn * i + (last + 1 - turn * back)))
        sp.dma_start(k.w_raw[slot(j, turn)][:, :], k.units[turn * i + (first + j)])\
            .then_inc(k.raw_landed[slot(j, turn)].sem, 16)
    if at_turn:
        at_turn(0)
    for j in range(turn):
        one(0, j)
    if turns > 1:
        with sp.Fori(1, turns) as i:
            if at_turn:
                at_turn(i)
            for j in range(turn):
                one(i, j)


def split_units(pool, k, turns, jobs, norm=None):
    turn = len(jobs)

    def one(i, j):
        s, same = slot(j, turn), sharing(j, turn)
        back, last = last_use(j, turn)
        if not (isinstance(i, int) and i < back):
            pool.wait_ge(k.dense_done.sem, k.dense_done.at(jobs[-1] * i + (jobs[last] - jobs[-1] * back)))
        pool.wait_ge(k.raw_landed[s].sem, k.raw_landed[s].at(16 * len(same) * i + 16 * (same.index(j) + 1)))
        pool.tensor_tensor(k.w_hi[s][:, :], k.w_raw[s][:, :], k.zero[:, 0:1].to_broadcast([P, D]), ALU.add)\
            .then_inc(k.unit_hi.sem, 1)
        pool.wait_ge(k.unit_hi.sem, k.unit_hi.at(turn * i + (j + 1)))
        pool.tensor_tensor(k.w_lo[s][:, :], k.w_raw[s][:, :], k.w_hi[s][:, :].bitcast(F32),
                           ALU.subtract).then_inc(k.unit_split.sem, 1)

    for j in range(turn):
        one(0, j)
        if norm and j == min(turn, RING) - 1:
            norm.gpsimd(pool)
    if turns > 1:
        with pool.Fori(1, turns) as i:
            for j in range(turn):
                one(i, j)


def product(pe, out, tiles, n0, n1):
    last = len(tiles) - 1
    for part in range(3):
        for i, (wh, wl, xh, xl) in enumerate(tiles):
            mm = pe.matmul(out, wl if part == 2 else wh, (xl if part == 1 else xh)[:, n0:n1],
                           start=(part == 0 and i == 0), stop=(part == 2 and i == last))
    return mm


def units_done(k, turns, turn):
    for u in range(turn):
        k.raw_landed[slot(u, turn)].base += 16 * turns
    for sig in (k.unit_hi, k.unit_split):
        sig.base += turns * turn
    k.next_unit += turns * turn


class Filler:
    UNITS, PRODUCTS, PIECES = 4, 12, 24

    def __init__(self, main, plan):
        self.main, self.plan = main, plan
        assert sum(plan) == self.PRODUCTS * self.PIECES, sum(plan)

    def jobs(self):
        return tuple(3 * (u + 1) for u in range(self.main + self.UNITS))

    def products(self, k, pe, i, place, xh, xl):
        turn, per_turn = self.main + self.UNITS, 3 * (self.main + self.UNITS)
        first = sum(self.plan[:place])
        for m in range(first, first + self.plan[place]):
            g, r = 3 * self.main + m // self.PIECES, m % self.PIECES
            u, n, part, c = g // 3, g % 3, r // KD, r % KD
            if r == 0:
                if n == 0:
                    pe.wait_ge(k.unit_split.sem, k.unit_split.at(turn * i + (u + 1)))
                pe.wait_ge(k.evacuated.sem, k.evacuated.at(per_turn * i + (g + 1)))
            w = (k.w_lo if part == 2 else k.w_hi)[slot(u, turn)]
            mm = pe.matmul(k.ps[g % 2][:, 0:THIRD], w[:, c * P:(c + 1) * P],
                           (xl if part == 1 else xh)[:, c, n * THIRD:(n + 1) * THIRD], start=(r == 0),
                           stop=(r == self.PIECES - 1))
            if r == self.PIECES - 1:
                mm.then_inc(k.dense_done.sem, 1)

    def finished(self, place):
        a = sum(self.plan[:place])
        b = a + self.plan[place]
        return [3 * self.main + g for g in range(self.PRODUCTS) if a < (g + 1) * self.PIECES <= b]


def ffn_phase(nc, k, name, norm, x, xh, xl, work, bias_rows=None):
    turns = NFF // 2
    h_hi = nc.alloc_sbuf_tensor_at(name + "_h_hi", [P, 2, T], F32R, offset=work)
    h_lo = nc.alloc_sbuf_tensor_at(name + "_h_lo", [P, 2, T], F32R, offset=work + 8 * T)
    gate = nc.alloc_sbuf_tensor_at(name + "_gate", [P, 3, THIRD], F32, offset=work + 16 * T)
    hid = nc.alloc_sbuf_tensor_at(name + "_hid", [P, 2, THIRD], F32, offset=work + 20 * T)
    JOBS = 36

    with nc.Block() as block:
        @block.sync
        def _(sp):
            load_units(sp, k, k.next_unit, turns, 6)

        @block.gpsimd
        def _(pool):
            split_units(pool, k, turns, (3, 6, 9, 12, 36, 36), norm)

        @block.tensor
        def _(pe):
            if norm:
                norm.tensor(pe)
            with pe.Fori(0, turns) as i:
                g = 0
                for u in range(4):
                    pe.wait_ge(k.unit_split.sem, k.unit_split.at(6 * i + (u + 1)))
                    for n in range(3):
                        if norm and u == 0:
                            pe.wait_ge(norm.s.nsplit[0].sem, norm.s.nsplit[0].at(n + 1))
                            pe.wait_ge(norm.s.nsplit[1].sem, norm.s.nsplit[1].at(n + 1))
                        if g < NPS:
                            pe.wait_ge(k.x_added.sem, k.x_added.at(24 * i + (g + 1)))
                        elif (g - NPS) % 6 < 3:
                            pe.wait_ge(k.gate_ready.sem, k.gate_ready.at(6 * i + ((g - NPS) // 6 * 3 + (g - NPS) % 6 + 1)))
                        else:
                            pe.wait_ge(k.gate_used.sem, k.gate_used.at(6 * i + ((g - NPS) // 6 * 3 + (g - NPS) % 6 - 3 + 1 + 3)))
                        tiles = [(k.w_hi[u % RING][:, c * P:(c + 1) * P], k.w_lo[u % RING][:, c * P:(c + 1) * P],
                                  xh[:, c, :], xl[:, c, :]) for c in range(KD)]
                        mm = product(pe, k.ps[g % NPS][:, 0:THIRD], tiles, n * THIRD, (n + 1) * THIRD)
                        mm.then_inc(k.dense_done.sem, 1)
                        g += 1
                pe.wait_ge(k.unit_split.sem, k.unit_split.at(6 * i + 6))
                for n in range(3):
                    pe.wait_ge(k.h_ready.sem, k.h_ready.at(6 * i + (3 + n + 1)))
                    for d in range(KD):
                        if g >= 12 + NPS:
                            pe.wait_ge(k.x_added.sem, k.x_added.at(24 * i + (g - 12 + 1)))
                        elif g == 12:
                            pe.wait_ge(k.gate_ready.sem, k.gate_ready.at(6 * i + 6))
                        else:
                            pe.wait_ge(k.gate_used.sem, k.gate_used.at(6 * i + (g - 13 + 4 + 3)))
                        tiles = [(k.w_hi[1 + c][:, d * P:(d + 1) * P], k.w_lo[1 + c][:, d * P:(d + 1) * P],
                                  h_hi[:, c, :], h_lo[:, c, :]) for c in range(2)]
                        mm = product(pe, k.ps[g % NPS][:, 0:THIRD], tiles, n * THIRD, (n + 1) * THIRD)
                        mm.then_inc(k.dense_done.sem, 1)
                        g += 1

        @block.scalar
        def _(act):
            if bias_rows:
                bias_rows.load(act)
            if norm:
                norm.scalar(act)
            if bias_rows:
                bias_rows.store(act)
            with act.Fori(0, turns) as i:
                for c in range(2):
                    for n in range(3):
                        g = 6 * c + n
                        act.wait_ge(k.dense_done.sem, k.dense_done.at(JOBS * i + (g + 1)))
                        act.wait_ge(k.gate_used.sem, k.gate_used.at(6 * i + (3 * c + n + 1)))
                        act.activation(gate[:, n, :], k.ps[g % NPS][:, 0:THIRD], ACT.Silu)\
                            .then_inc(k.gate_ready.sem, 1)
            if bias_rows:
                bias_rows.stored(act)

        @block.vector
        def _(dve):
            if norm:
                norm.vector(dve)
            if bias_rows:
                bias_rows.spread(dve)
            with dve.Fori(0, turns) as i:
                for c in range(2):
                    for n in range(3):
                        g = 6 * c + 3 + n
                        j = 3 * c + n
                        cols = slice(n * THIRD, (n + 1) * THIRD)
                        dve.wait_ge(k.dense_done.sem, k.dense_done.at(JOBS * i + (g + 1)))
                        dve.wait_ge(k.gate_ready.sem, k.gate_ready.at(6 * i + (j + 1)))
                        up = k.ps[g % NPS][:, 0:THIRD]
                        dve.tensor_tensor(hid[:, j % 2, :], up, gate[:, n, :], ALU.mult).then_inc(k.hid_made.sem, 1)
                        dve.tensor_tensor(h_hi[:, c, cols], up, gate[:, n, :], ALU.mult)\
                            .then_inc(k.gate_used.sem, 1)
                        dve.wait_ge(k.hid_made.sem, k.hid_made.at(6 * i + (j + 1)))
                        dve.wait_ge(k.gate_used.sem, k.gate_used.at(6 * i + (j + 1 + 3)))
                        dve.tensor_tensor(h_lo[:, c, cols], hid[:, j % 2, :], h_hi[:, c, cols].bitcast(F32),
                                          ALU.subtract).then_inc(k.h_ready.sem, 1)
                g = 12
                for n in range(3):
                    for d in range(KD):
                        dve.wait_ge(k.dense_done.sem, k.dense_done.at(JOBS * i + (g + 1)))
                        xs = x[:, d, n * THIRD:(n + 1) * THIRD]
                        dve.scalar_tensor_tensor(out=xs, in0=k.ps[g % NPS][:, 0:THIRD], scalar=0.5, in1=xs,
                                                 op0=ALU.mult, op1=ALU.add).then_inc(k.x_added.sem, 1)
                        g += 1

    units_done(k, turns, 6)
    if norm:
        norm.done()
    k.dense_done.base += JOBS * turns
    k.x_added.base += 24 * turns
    for sig in (k.gate_used, k.gate_ready, k.hid_made, k.h_ready):
        sig.base += 6 * turns


class NormSignals:

    def __init__(self, k, name):
        self.nsq, self.ntotal = k.counter(name + "_squared"), k.counter(name + "_total")
        self.nln, self.nrinv = k.counter(name + "_ln"), k.counter(name + "_rinv")
        self.nscaled, self.nhi = k.counter(name + "_scaled"), k.counter(name + "_upper")
        self.nsplit = [k.counter(f"{name}_lower{h}") for h in range(2)]
        self.nout = [k.counter(f"{name}_stored{b}") for b in range(2)]


class Norm:

    def __init__(self, nc, k, signals, name, x, gains, hi, lo, work, width, cols, squares_at,
                 rinv_at=None, out=None):
        self.k, self.s, self.x, self.gains, self.hi, self.lo, self.out = k, signals, x, gains, hi, lo, out
        self.nb, self.width = width // cols, cols
        self.tmp = nc.alloc_sbuf_tensor_at(name + "_tmp", [P, 2, KD, cols], F32, offset=work)
        self.rinv = nc.alloc_sbuf_tensor_at(name + "_rinv", [P, 2, cols], F32,
                                            offset=work + 8 * KD * cols if rinv_at is None else rinv_at)
        self.squares = nc.alloc_sbuf_tensor_at(name + "_squares", [P, KD, width], F32, offset=squares_at)

    def cols(self, n):
        return slice(n * self.width, (n + 1) * self.width)

    def square(self, act, n):
        s = self.s
        for h in range(2):
            c = slice(4 * h, 4 * h + 4)
            act.activation(self.squares[:, c, self.cols(n)], self.x[:, c, self.cols(n)], ACT.Square)\
                .then_inc(s.nsq.sem, 1)

    def sums(self, pe, n):
        k, s = self.k, self.s
        for c in range(KD):
            if c % 4 == 0:
                pe.wait_ge(s.nsq.sem, s.nsq.at(2 * n + c // 4 + 1))
            mm = pe.matmul(k.ps[4 + n][:, 0:self.width], k.ones[:, :], self.squares[:, c, self.cols(n)],
                           start=(c == 0), stop=(c == KD - 1))
        mm.then_inc(s.ntotal.sem, 1)

    def root(self, act, n):
        k, s = self.k, self.s
        act.wait_ge(s.ntotal.sem, s.ntotal.at(n + 1))
        if n >= 2:
            act.wait_ge(s.nscaled.sem, s.nscaled.at(2 * (n - 1)))
        r = self.rinv[:, n % 2, :]
        act.activation(r, k.ps[4 + n][:, 0:self.width], ACT.Ln, bias=k.eps[:, 0:1], scale=1.0 / D)\
            .then_inc(s.nln.sem, 1)
        act.wait_ge(s.nln.sem, s.nln.at(n + 1))
        act.activation(r, r, ACT.Exp, scale=-0.5).then_inc(s.nrinv.sem, 1)

    def scale(self, dve, n):
        s, b = self.s, n % 2
        dve.wait_ge(s.nrinv.sem, s.nrinv.at(n + 1))
        if n >= 2 and self.out is None:
            dve.wait_ge(s.nsplit[0].sem, s.nsplit[0].at(n - 1))
            dve.wait_ge(s.nsplit[1].sem, s.nsplit[1].at(n - 1))
        elif n >= 2:
            dve.wait_ge(s.nout[b].sem, s.nout[b].at(16 * (n // 2)))
        for c in range(KD):
            mm = dve.scalar_tensor_tensor(out=self.tmp[:, b, c, :], in0=self.x[:, c, self.cols(n)],
                                          scalar=self.gains[:, c:c + 1], in1=self.rinv[:, b, :], op0=ALU.mult, op1=ALU.mult)
            if c % 4 == 3:
                mm.then_inc(s.nscaled.sem, 1)

    def upper(self, act, n):
        s = self.s
        for h in range(2):
            c = slice(4 * h, 4 * h + 4)
            act.wait_ge(s.nscaled.sem, s.nscaled.at(2 * n + h + 1))
            act.activation(self.hi[:, c, self.cols(n)], self.tmp[:, n % 2, c, :], ACT.Copy).then_inc(s.nhi.sem, 1)

    def lower(self, eng, n, h):
        s = self.s
        c = slice(4 * h, 4 * h + 4)
        eng.wait_ge(s.nhi.sem, s.nhi.at(2 * n + h + 1))
        eng.wait_ge(s.nscaled.sem, s.nscaled.at(2 * n + h + 1))
        eng.tensor_tensor(self.lo[:, c, self.cols(n)], self.tmp[:, n % 2, c, :], self.hi[:, c, self.cols(n)].bitcast(F32),
                          ALU.subtract).then_inc(s.nsplit[h].sem, 1)


    def tensor(self, pe):
        for n in range(self.nb):
            self.sums(pe, n)

    def scalar(self, act):
        act.preload_act_table_set("natural_log_exp_and_others")
        for n in range(self.nb):
            self.square(act, n)
        for n in range(self.nb):
            self.root(act, n)
            if self.out is None:
                self.upper(act, n)

    def vector(self, dve, both=False):
        for n in range(self.nb):
            self.scale(dve, n)
            if self.out is None:
                self.lower(dve, n, 0)
                if both:
                    self.lower(dve, n, 1)

    def gpsimd(self, pool):
        for n in range(self.nb):
            self.lower(pool, n, 1)

    def done(self):
        s, nb = self.s, self.nb
        for sig, n in ((s.nsq, 2), (s.ntotal, 1), (s.nln, 1), (s.nrinv, 1), (s.nscaled, 2)):
            sig.base += n * nb
        if self.out is None:
            for sig, n in ((s.nhi, 2), (s.nsplit[0], 1), (s.nsplit[1], 1)):
                sig.base += n * nb
        else:
            for b in range(2):
                s.nout[b].base += 16 * len(range(b, nb, 2))


def last_norm_phase(nc, k, norm):
    with nc.Block() as block:
        @block.tensor
        def _(pe):
            norm.tensor(pe)

        @block.scalar
        def _(act):
            norm.scalar(act)

        @block.vector
        def _(dve):
            norm.vector(dve)

        @block.sync
        def _(sp):
            for n in range(norm.nb):
                sp.wait_ge(norm.s.nscaled.sem, norm.s.nscaled.at(2 * n + 2))
                sp.dma_start(norm.out[:, :, norm.cols(n)], norm.tmp[:, n % 2]).then_inc(norm.s.nout[n % 2].sem, 16)
            for b in range(2):
                sp.wait_ge(norm.s.nout[b].sem, norm.s.nout[b].at(16 * len(range(b, norm.nb, 2))))

    norm.done()


class Core:

    def __init__(self, nc, ctx):
        self.nc, self.ctx, self.tokens, self.next_unit = nc, ctx, [], 0
        at = (nc.sbuf_base + 63) // 64 * 64
        self.ones = nc.alloc_sbuf_tensor_at("ones", [P, P], F32, offset=at)
        self.ident = nc.alloc_sbuf_tensor_at("ident", [P, P], F32, offset=at + 512)
        self.eps = nc.alloc_sbuf_tensor_at("eps", [P, 1], F32, offset=at + 1024)
        self.zero = nc.alloc_sbuf_tensor_at("zero", [P, 1], F32, offset=at + 1056)
        self.gains = nc.alloc_sbuf_tensor_at("gains", [P, 6 * KD], F32, offset=at + 1088)
        at += 1088 + 6 * KD * 4
        self.w_raw = [nc.alloc_sbuf_tensor_at(f"w_raw{s}", [P, D], F32, offset=at + 4096 * s) for s in range(RING)]
        self.w_hi = [nc.alloc_sbuf_tensor_at(f"w_hi{s}", [P, D], F32R, offset=at + 4096 * (RING + s))
                     for s in range(RING)]
        self.w_lo = [nc.alloc_sbuf_tensor_at(f"w_lo{s}", [P, D], F32R, offset=at + 4096 * (2 * RING + s))
                     for s in range(RING)]
        self.arena = at + 4096 * 3 * RING
        self.psum = ctx.enter_context(nc.psum_tensor("psum", [P, 8, 512], F32))
        self.ps = [self.psum[:, b, :] for b in range(8)]
        self.raw_landed = [self.counter(f"raw_landed{s}") for s in range(RING)]
        self.unit_hi, self.unit_split = self.counter("unit_hi"), self.counter("unit_split")
        self.dense_done, self.evacuated = self.counter("dense_done"), self.counter("evacuated", 2)
        self.gate_ready, self.gate_used = self.counter("gate_ready"), self.counter("gate_used", 3)
        self.hid_made, self.h_ready = self.counter("hid_made"), self.counter("h_ready")
        self.x_added = self.counter("x_added", NPS)
        self.norm, self.memory_norm = NormSignals(self, "norm"), NormSignals(self, "memory_norm")
        self.merged_hi, self.merged_split = self.counter("merged_hi"), self.counter("merged_split")
        self.x_loaded = self.counter("x_loaded")
        self.loaded = self.counter("loaded")
        self.table_loaded, self.rows_made = self.counter("table_loaded"), self.counter("rows_made")
        self.rows_stored = self.counter("rows_stored")
        self.v_turned, self.vn_ready = self.counter("v_turned"), self.counter("vn_ready")
        self.qbd_zero, self.qbd_ready, self.masked = self.counter("qbd_zero"), self.counter("qbd_ready"), self.counter("masked")
        self.scored, self.biased, self.maxed = self.counter("scored"), self.counter("biased"), self.counter("maxed")
        self.exped, self.inverted, self.normed = self.counter("exped"), self.counter("inverted"), self.counter("normed")
        self.turned, self.pt_ready = self.counter("turned"), self.counter("pt_ready")
        self.valued, self.o_read = self.counter("valued", 1), self.counter("o_read")
        self.a_loaded, self.kv_stored = self.counter("a_loaded"), self.counter("kv_stored", 32)
        self.ya_stored = self.counter("ya_stored", 16)

        self.kv_slot = [self.counter(f"slot_stored{b}", 32) for b in range(2)]
        self.score_read = self.counter("score_read", 2)
        self.merged, self.gated = self.counter("merged", 2), self.counter("gated")
        self.squared = self.counter("squared")
        self.lned = self.counter("lned")
        self.sq_summed = self.counter("sq_summed")
        self.rooted = self.counter("rooted")
        self.per_ready = self.counter("per_ready")
        self.decayed = self.counter("decayed")
        self.scaled = self.counter("scaled")
        self.rows_spread = self.counter("rows_spread")
        self.l2_done = self.counter("l2_done")
        self.grams = self.counter("grams")
        self.kv_turned = self.counter("kv_turned")
        self.y_started = self.counter("y_started")
        self.y_turned = self.counter("y_turned")
        self.x_started = self.counter("x_started")
        self.masked_level = self.counter("masked_level")
        self.p1_ready = self.counter("p1_ready")
        self.p1_done = self.counter("p1_done")
        self.level_done = self.counter("level_done")
        self.corrected = self.counter("corrected")
        self.w_ready = self.counter("w_ready")
        self.u_ready = self.counter("u_ready")
        self.wu_done = self.counter("wu_done")
        self.s_ready = self.counter("s_ready")
        self.ws_done = self.counter("ws_done")
        self.o_copied = self.counter("o_copied")
        self.qg_ready = self.counter("qg_ready")
        self.vw_ready = self.counter("vw_ready")
        self.o_done = self.counter("o_done")
        self.s_loaded = self.counter("s_loaded")
        self.wz_ready = self.counter("wz_ready")
        self.v8_ready = self.counter("v8_ready")
        self.pad_ready = self.counter("pad_ready")
        self.silued = self.counter("silued")
        self.convolved = self.counter("convolved")
        self.eg_ready = self.counter("eg_ready")
        self.dt_args = self.counter("dt_args")
        self.dt_ready = self.counter("dt_ready")
        self.s_final = self.counter("s_final")
        self.o_scaled = self.counter("o_scaled")
        self.o_normed = self.counter("o_normed")
        self.pad_landed = [self.counter(f"pad_landed{c}") for c in range(3)]
        self.z_landed, self.stash_clear = self.counter("z_landed"), self.counter("stash_clear")
        self.gate_sigmoid = self.counter("gate_sigmoid")
        self.third_landed = [self.counter(f"third_landed{b}") for b in range(2)]
        self.third_hi, self.third_split = self.counter("third_hi"), self.counter("third_split")
        self.x_landed = [self.counter(f"x_landed{c}") for c in range(KD)]
        self.tap = self.counter("tap")
        self.nt_made = self.counter("nt_made")
        self.first_mask = self.counter("first_mask")
        self.s_decayed = self.counter("s_decayed")
        self.pre = self.counter("pre")
        self.pre_pe = self.counter("pre_pe")
        self.pre_act = self.counter("pre_act")
        self.b_loaded = self.counter("b_loaded")
        self.kv_done, self.s_out, self.yb_stored = (self.counter("kv_done", 1), self.counter("s_out", 48),
                                                    self.counter("yb_stored", 16))

    def counter(self, name, tokens=0):
        s = Counter(self.nc, self.ctx, name)
        if tokens:
            self.tokens.append((s, tokens))
        return s



class BiasRows:

    def __init__(self, nc, k, work):
        self.k, self.far = k, NBIAS - (2 * REL + 1)
        self.rows = nc.alloc_sbuf_tensor_at("bias_rows", [P, HA, NBIAS], F32, offset=work)

    def load(self, act):
        act.dma_start(self.rows[:, :, self.far:], self.k.table.partition_broadcast(P))\
            .then_inc(self.k.table_loaded.sem, 16)

    def spread(self, dve):
        dve.wait_ge(self.k.table_loaded.sem, self.k.table_loaded.at(16))
        dve.tensor_copy(self.rows[:, :, 0:self.far], self.rows[:, :, self.far:self.far + 1]
                        .to_broadcast([P, HA, self.far])).then_inc(self.k.rows_made.sem, 1)

    def store(self, act):
        act.wait_ge(self.k.rows_made.sem, self.k.rows_made.at(1))
        act.dma_start(self.k.bias_dram[:, 0:HA * NBIAS], self.rows[:].rearrange("p h m -> p (h m)"))\
            .then_inc(self.k.rows_stored.sem, 16)

    def stored(self, act):
        act.wait_ge(self.k.rows_stored.sem, self.k.rows_stored.at(16))


def attention_phase(nc, k, make_norm, xh, xl, x, x_to, work):
    at = [work]

    def sb(name, shape):
        t = nc.alloc_sbuf_tensor_at(name, shape, F32, offset=at[0])
        at[0] += (4 * int(np.prod(shape[1:])) + 31) // 32 * 32
        return t

    kc, vc = sb("a_kc", [P, DB, REACH]), sb("a_vc", [P, DB, 4, P])
    vns = sb("a_vns", [DS, DB, P])
    at[0] = work + 4 * KD * T
    q, kt, vt = sb("a_q", [P, T]), sb("a_k", [P, T]), sb("a_v", [P, T])
    qbd = sb("a_qbd", [P, DB, 32])
    bias, bias_s = sb("a_bias", [P, 2, WIN]), sb("a_bias_s", [P, REACH + DS])
    nmax, rsum, rinv = sb("a_nmax", [P, 2]), sb("a_rsum", [P, 2]), sb("a_rinv", [P, 2])
    norm = make_norm(at[0])
    vn = sb("a_vn", [P, 8, P])
    sc, pt = sb("a_sc", [P, 2, WIN]), sb("a_pt", [P, 2, 5, P])
    ya = sb("a_y", [P, T])
    PAIRS, STEPS, ND = HA // 2, 18, 2
    stash = sb("a_stash", [P, 2, PADDED])
    filler = Filler(3, [15] * 8 + [14] * 12)
    DONE = 9 + filler.PRODUCTS
    psS, psT = k.psum[:, 3:5, :].rearrange("p b c -> p (b c)"), k.psum[:, 5:7, :].rearrange("p b c -> p (b c)")
    obank = (7, 2)
    shifted = k.bias_dram_flat[P - 1:P - 1 + P * (k.bias_pitch - 1)].rearrange("(q m) -> q m", q=P)[:, 0:HA * NBIAS]\
        .rearrange("q (h m) -> h q m", h=HA)

    def window(t):
        n = min(5, t + 1)
        return t + 1 - n, n

    with nc.Block() as block:
        @block.sync
        def _(sp):
            def store_x(i):
                if isinstance(i, int):
                    for c in range(KD):
                        sp.dma_start(x_to[c], x[:, c, :]).then_inc(k.loaded.sem, 16)

            load_units(sp, k, k.next_unit, PAIRS, 7, store_x)

        @block.gpsimd
        def _(pool):
            split_units(pool, k, PAIRS, filler.jobs(), norm)

        @block.tensor
        def _(pe):
            def scores(i, s):
                if s >= 1:
                    pe.wait_ge(k.biased.sem, k.biased.at(STEPS * i + s))
                if s < 16:
                    t, h = s // 2, s % 2
                    k0, n = window(t)
                    hp = slice(64 * h, 64 * h + 64)
                    for a, b in ((0, min(4, n)), (4, n)):
                        if b > a:
                            mm = pe.matmul(psS[:, a * P:b * P], q[hp, t * P:(t + 1) * P],
                                           kt[hp, (k0 + a) * P:(k0 + b) * P], start=True, stop=True)
                    mm.then_inc(k.scored.sem, 1)
                    return
                for b in range(4):
                    st = 4 * (s - 16) + b
                    pe.matmul(psS[32 * b:32 * b + 32, 0:REACH], qbd[:, st, :], kc[:, st, :], start=True, stop=True,
                              tile_position=(0, 32 * b))
                    mm = pe.matmul(psS[32 * b:32 * b + 32, REACH:REACH + DS], qbd[:, st, :],
                                   kt[:, SEQ + DS * st:SEQ + DS * (st + 1)], start=True, stop=True,
                                   tile_position=(0, 32 * b))
                mm.then_inc(k.scored.sem, 1)

            def turn_probs(i, s):
                pe.wait_ge(k.normed.sem, k.normed.at(STEPS * i + (s + 1)))
                if s >= 1:
                    pe.wait_ge(k.pt_ready.sem, k.pt_ready.at(STEPS * i + s))
                b = s % 2
                n = window(s // 2)[1] if s < 16 else 4
                for j in range(n):
                    mm = pe.transpose(psT[:, j * P:(j + 1) * P], sc[:, b, j * P:(j + 1) * P], k.ident[:, :])
                if s >= 16:
                    mm = pe.transpose(psT[0:DS, 4 * P:5 * P], sc[:, b, REACH:REACH + DS], k.ident[:, :])
                mm.then_inc(k.turned.sem, 1)

            def values(i, s):
                pe.wait_ge(k.pt_ready.sem, k.pt_ready.at(STEPS * i + (s + 1)))
                o = k.ps[obank[(s // 2) % 2 if s < 16 else s % 2]]
                b = s % 2
                if s < 16:
                    t, h = s // 2, s % 2
                    k0, n = window(t)
                    if h == 0 and t >= 2:
                        pe.wait_ge(k.o_read.sem, k.o_read.at(10 * i + (t - 1)))
                    for j in range(n):
                        mm = pe.matmul(o[64 * h:64 * h + 64, 0:P], vn[:, k0 + j, 64 * h:64 * h + 64], pt[:, b, j, :],
                                       start=(j == 0), stop=(j == n - 1), tile_position=(0, 64 * h))
                    mm.then_inc(k.valued.sem, 1)
                    return
                pe.wait_ge(k.o_read.sem, k.o_read.at(10 * i + (8 + (s - 16) - 1)))
                for c in range(4):
                    st = 4 * (s - 16) + c
                    out = o[:, 32 * c:32 * c + 32]
                    for j in range(4):
                        pe.matmul(out, vc[:, st, j, :], pt[:, b, j, 32 * c:32 * c + 32], start=(j == 0), stop=False)
                    mm = pe.matmul(out, vns[0:DS, st, :], pt[0:DS, b, 4, 32 * c:32 * c + 32], start=False, stop=True)
                mm.then_inc(k.valued.sem, 1)

            norm.tensor(pe)
            with pe.Fori(0, PAIRS) as i:
                for u in range(3):
                    pe.wait_ge(k.unit_split.sem, k.unit_split.at(7 * i + (u + 1)))
                    for n in range(3):
                        g = 3 * u + n
                        if u == 0:
                            pe.wait_ge(norm.s.nsplit[0].sem, norm.s.nsplit[0].at(n + 1))
                            pe.wait_ge(norm.s.nsplit[1].sem, norm.s.nsplit[1].at(n + 1))
                        pe.wait_ge(k.evacuated.sem, k.evacuated.at(DONE * i + max(g + 1, 2)))
                        tiles = [(k.w_hi[u][:, c * P:(c + 1) * P], k.w_lo[u][:, c * P:(c + 1) * P],
                                  xh[:, c, :], xl[:, c, :]) for c in range(KD)]
                        product(pe, k.ps[g % ND][:, 0:THIRD], tiles, n * THIRD, (n + 1) * THIRD)\
                            .then_inc(k.dense_done.sem, 1)
                pe.wait_ge(k.evacuated.sem, k.evacuated.at(DONE * i + (9 + ND)))
                for t in range(8):
                    mm = pe.transpose(psT[:, t * P:(t + 1) * P], vt[:, t * P:(t + 1) * P], k.ident[:, :])
                mm.then_inc(k.v_turned.sem, 1)
                for b in range(DB):
                    mm = pe.transpose(psS[0:DS, b * P:(b + 1) * P], vt[:, SEQ + DS * b:SEQ + DS * (b + 1)], k.ident[:, :])
                mm.then_inc(k.v_turned.sem, 1)
                pe.wait_ge(k.vn_ready.sem, k.vn_ready.at(2 * i + 2))
                for s in range(STEPS + 2):
                    if s == 16:
                        pe.wait_ge(k.a_loaded.sem, k.a_loaded.at(192 * i + 192))
                        pe.wait_ge(k.qbd_ready.sem, k.qbd_ready.at(2 * i + 2))
                    if s < STEPS:
                        scores(i, s)
                    if s >= 2:
                        values(i, s - 2)
                    filler.products(k, pe, i, s, xh, xl)
                    if 1 <= s <= STEPS:
                        turn_probs(i, s - 1)

        @block.scalar
        def _(act):
            def evacuate(i, g):
                act.wait_ge(k.dense_done.sem, k.dense_done.at(DONE * i + (g + 1)))
                u, n = g // 3 - 3, g % 3
                row, src = stash[:, u % 2, :], k.ps[g % ND]
                if n == 0:
                    act.wait_ge(k.kv_slot[u % 2].sem, k.kv_slot[u % 2].at(32 * i + (16 * (u // 2) + 32)))
                if u == 3:
                    act.activation(row[:, n * THIRD:(n + 1) * THIRD], src[:, 0:THIRD], ACT.Copy)\
                        .then_inc(k.evacuated.sem, 1)
                elif n < 2:
                    act.activation(row[:, CW - 1 + n * THIRD:CW - 1 + (n + 1) * THIRD], src[:, 0:THIRD], ACT.Copy)\
                        .then_inc(k.evacuated.sem, 1)
                else:
                    act.activation(row[:, CW - 1 + 2 * THIRD:PADP], src[:, 0:THIRD - P], ACT.Copy)
                    act.activation(row[:, PADP:].rearrange("p (b c) -> p b c", c=PADS)[:, :, CW - 1:],
                                   src[:, THIRD - P:THIRD].rearrange("p (b c) -> p b c", c=DS), ACT.Copy)\
                        .then_inc(k.evacuated.sem, 1)
                if n == 2:
                    act.wait_ge(k.evacuated.sem, k.evacuated.at(DONE * i + (g + 1 + ND)))
                    act.dma_start(k.proj_dram[4 * i + u], row).then_inc(k.kv_slot[u % 2].sem, 16)

            norm.scalar(act)
            act.wait_ge(k.stash_clear.sem, k.stash_clear.at(1))
            with act.Fori(0, PAIRS) as i:
                act.wait_ge(k.valued.sem, k.valued.at(STEPS * i + 1))
                loads = []
                for h in range(2):
                    loads.append((bias[:, h, :], shifted[2 * i + h][:, 0:WIN]))
                    for b in range(4):
                        r = 32 * b + 16 * h
                        loads.append((bias_s[r:r + 16, :], shifted[2 * i + h][0:16, 0:REACH + DS]))
                for dst, src in loads:
                    act.dma_start(dst, src).then_inc(k.a_loaded.sem, 16)
                for g in range(9):
                    if g == 3:
                        act.wait_ge(k.kv_stored.sem, k.kv_stored.at(32 * i + 32))
                    act.wait_ge(k.dense_done.sem, k.dense_done.at(DONE * i + (g + 1)))
                    dst = (q, kt, vt)[g // 3][:, (g % 3) * THIRD:(g % 3 + 1) * THIRD]
                    act.activation(dst, k.ps[g % ND][:, 0:THIRD], ACT.Copy,
                                   scale=DHA ** -0.5 if g < 3 else 1.0).then_inc(k.evacuated.sem, 1)
                    if g == 5:
                        act.wait_ge(norm.s.nscaled.sem, norm.s.nscaled.at(2 * norm.nb))
                        act.wait_ge(k.loaded.sem, k.loaded.at(16 * KD))
                        for dst, src in ((kc[:], k.k_cache[i]), (vc[:], k.v_cache[i])):
                            act.dma_start(dst, src).then_inc(k.a_loaded.sem, 16)
                act.wait_ge(k.evacuated.sem, k.evacuated.at(DONE * i + (9 + ND)))
                act.dma_start(k.a_k_out[i], kt[:, :]).then_inc(k.kv_stored.sem, 16)
                act.dma_start(k.a_v_out[i], vt[:, :]).then_inc(k.kv_stored.sem, 16)
                act.wait_ge(k.v_turned.sem, k.v_turned.at(2 * i + 1))
                act.activation(vn[:].rearrange("p t c -> p (t c)"), psT[:, :], ACT.Copy).then_inc(k.vn_ready.sem, 1)
                act.wait_ge(k.v_turned.sem, k.v_turned.at(2 * i + 2))
                act.activation(vns[:].rearrange("p t c -> p (t c)"), psS[0:DS, :], ACT.Copy).then_inc(k.vn_ready.sem, 1)

                def exps(s):
                    act.wait_ge(k.maxed.sem, k.maxed.at(STEPS * i + (s + 1)))
                    n = window(s // 2)[1] * P if s < 16 else REACH + DS
                    b = s % 2
                    act.activation(sc[:, b, 0:n], sc[:, b, 0:n], ACT.Exp, bias=nmax[:, b:b + 1],
                                   accum_out=rsum[:, b:b + 1]).then_inc(k.exped.sem, 1)

                def copy_turned(s):
                    act.wait_ge(k.turned.sem, k.turned.at(STEPS * i + (s + 1)))
                    if s >= 2:
                        act.wait_ge(k.valued.sem, k.valued.at(STEPS * i + (s - 1 + 1)))
                    n = window(s // 2)[1] if s < 16 else 4
                    b = s % 2
                    if s >= 16:
                        act.activation(pt[0:DS, b, 4, :], psT[0:DS, 4 * P:5 * P], ACT.Copy)
                    act.activation(pt[:, b, 0:n, :].rearrange("p t c -> p (t c)"), psT[:, 0:n * P], ACT.Copy)\
                        .then_inc(k.pt_ready.sem, 1)

                def copy_o(s):
                    act.wait_ge(k.valued.sem, k.valued.at(STEPS * i + (s + 1 + 1)))
                    if s == 1:
                        act.wait_ge(k.ya_stored.sem, k.ya_stored.at(16 * i + 16))
                    if s < 16:
                        t = s // 2
                        act.activation(ya[:, t * P:(t + 1) * P], k.ps[obank[t % 2]][:, 0:P], ACT.Copy)\
                            .then_inc(k.o_read.sem, 1)
                        return
                    o = k.ps[obank[s % 2]]
                    for h in range(2):
                        hp = slice(64 * h, 64 * h + 64)
                        c0 = SEQ + 64 * (s - 16)
                        a = act.activation(ya[hp, c0:c0 + 64].rearrange("p (b c) -> p b c", c=16),
                                           o[hp, 0:P].rearrange("p (b c) -> p b c", c=32)[:, :, 16 * h:16 * h + 16],
                                           ACT.Copy)
                    a.then_inc(k.o_read.sem, 1)

                for s in range(STEPS + 3):
                    if s >= 1:
                        for g in filler.finished(s - 1):
                            evacuate(i, g)
                    if s < STEPS:
                        exps(s)
                    if 1 <= s <= STEPS:
                        copy_turned(s - 1)
                    if s >= 3 and ((s - 3) % 2 == 1 or s - 3 >= 16):
                        copy_o(s - 3)
                act.wait_ge(k.o_read.sem, k.o_read.at(10 * i + 10))
                act.dma_start(k.ya_dram[i], ya[:, :]).then_inc(k.ya_stored.sem, 16)
            act.wait_ge(k.ya_stored.sem, k.ya_stored.at(16 * PAIRS + 16))
            act.wait_ge(k.kv_stored.sem, k.kv_stored.at(32 * PAIRS + 32))
            for b in range(2):
                act.wait_ge(k.kv_slot[b].sem, k.kv_slot[b].at(32 * PAIRS + 32))

        @block.vector
        def _(dve):
            norm.vector(dve)
            dve.wait_ge(norm.s.nsplit[1].sem, norm.s.nsplit[1].at(norm.nb))
            dve.memset(stash[:], 0.0).then_inc(k.stash_clear.sem, 1)
            dve.memset(qbd[:], 0.0).then_inc(k.qbd_zero.sem, 1)
            dve.wait_ge(k.qbd_zero.sem, k.qbd_zero.at(1))
            with dve.Fori(0, PAIRS) as i:
                dve.wait_ge(k.evacuated.sem, k.evacuated.at(DONE * i + (3 + ND)))
                for h in range(2):
                    hp = slice(64 * h, 64 * h + 64)
                    dve.tensor_copy(qbd[hp, :, 16 * h:16 * h + 16], q[hp, SEQ:T].rearrange("p (b c) -> p b c", c=DS))\
                        .then_inc(k.qbd_ready.sem, 1)
                dve.wait_ge(k.a_loaded.sem, k.a_loaded.at(192 * i + 192))
                for h in range(2):
                    dve.memset(bias[0:64, h, WIN - 64:WIN], NEG)
                    m = dve.memset(bias[64:P, h, 0:64], NEG)
                m.then_inc(k.masked.sem, 1)
                dve.wait_ge(k.masked.sem, k.masked.at(i + 1))

                def logits(s):
                    dve.wait_ge(k.scored.sem, k.scored.at(STEPS * i + (s + 1)))
                    if s >= 2:
                        dve.wait_ge(k.turned.sem, k.turned.at(STEPS * i + (s - 1)))
                    b = s % 2
                    if s < 16:
                        n = window(s // 2)[1] * P
                        add = bias[:, s % 2, WIN - n:WIN]
                    else:
                        n, add = REACH + DS, bias_s[:, :]
                    dve.tensor_tensor(sc[:, b, 0:n], psS[:, 0:n], add, ALU.add).then_inc(k.biased.sem, 1)
                    dve.wait_ge(k.biased.sem, k.biased.at(STEPS * i + (s + 1)))
                    dve.tensor_reduce(nmax[:, b:b + 1], sc[:, b, 0:n], AX_X, ALU.max, negate=True)\
                        .then_inc(k.maxed.sem, 1)

                def normalise(s):
                    b = s % 2
                    n = window(s // 2)[1] * P if s < 16 else REACH + DS
                    dve.wait_ge(k.exped.sem, k.exped.at(STEPS * i + (s + 1)))
                    dve.reciprocal(rinv[:, b:b + 1], rsum[:, b:b + 1]).then_inc(k.inverted.sem, 1)
                    dve.wait_ge(k.inverted.sem, k.inverted.at(STEPS * i + (s + 1)))
                    dve.tensor_scalar(sc[:, b, 0:n], sc[:, b, 0:n], rinv[:, b:b + 1], None, ALU.mult)\
                        .then_inc(k.normed.sem, 1)

                for s in range(STEPS + 1):
                    if s < STEPS:
                        logits(s)
                    if s >= 1:
                        normalise(s - 1)

    units_done(k, PAIRS, 7)
    k.qbd_zero.base += 1
    k.stash_clear.base += 1
    k.loaded.base += 16 * KD
    norm.done()
    for b in range(2):
        k.kv_slot[b].base += 32 * PAIRS
    for s_, n in ((k.dense_done, DONE), (k.evacuated, DONE), (k.v_turned, 2), (k.vn_ready, 2), (k.scored, STEPS),
                  (k.biased, STEPS), (k.maxed, STEPS), (k.exped, STEPS), (k.inverted, STEPS), (k.normed, STEPS),
                  (k.turned, STEPS), (k.pt_ready, STEPS), (k.valued, STEPS), (k.o_read, 10), (k.a_loaded, 192),
                  (k.kv_stored, 32), (k.ya_stored, 16), (k.masked, 1), (k.qbd_ready, 2)):
        s_.base += n * PAIRS



MASKS = ("upto", "upto16", "future", "future16", "same16")


def delta_constants():
    j, i = np.arange(P)[:, None], np.arange(P)[None, :]
    same = j // DS == i // DS
    out = [j <= i, (j <= i) & same, np.where(j <= i, 0, NEG), np.where((j <= i) & same, 0, NEG), same]
    for level in range(7):
        half = 1 << level
        out.append((i // (2 * half) == j // (2 * half)) & (i % (2 * half) >= half) & (j % (2 * half) < half))
    streams = (j // DS) == np.arange(DB)[None, :]
    return np.concatenate([np.asarray(m, np.float32) for m in out + [streams]], axis=1)


PLAN_START, PLAN_NORM, PLAN_GROUP, PLAN_BEFORE, PLAN_LEVEL, PLAN_STEP = 96, 6, 8, 8, 4, 6


def delta_phase(nc, k, xh, xl, work):
    at = [work]

    def sb(name, shape, dt=F32):
        t = nc.alloc_sbuf_tensor_at(name, shape, dt, offset=at[0])
        at[0] += (4 * int(np.prod(shape[1:])) + 31) // 32 * 32
        return t

    def alias(name, shape, offset):
        return nc.alloc_sbuf_tensor_at(name, shape, F32, offset=offset)

    NM = 12
    consts = sb("b_consts", [P, NM * P + DB])

    def const(n):
        return consts[:, n * P:(n + 1) * P]

    upto, upto16, future, future16, same16 = (const(n) for n in range(5))
    level_mask = [const(5 + n) for n in range(7)]
    streams = consts[:, NM * P:NM * P + DB]
    pad_at = at[0]
    pad = sb("b_pad", [P, 3, PADDED])
    X, Y, P1 = (alias(n, [P, T], pad_at + 4 * T * m) for m, n in enumerate(("b_X", "b_Y", "b_P1")))
    yq_at = at[0]
    y = sb("b_y", [P, 3, T])
    yq, yk, yv = y[:, 0, :], y[:, 1, :], y[:, 2, :]
    oT, MT = alias("b_oT", [P, T], yq_at + 4 * T), alias("b_MT", [P, T], yq_at + 8 * T)
    z = sb("b_z", [P, T])
    kbe, kd, vb = sb("b_kbe", [P, T]), sb("b_kd", [P, T]), sb("b_vb", [P, T])
    eg = sb("b_eg", [P, T])
    DT = sb("b_DT", [P, T])
    wT = alias("b_wT", [P, T], at[0] - 4 * T)
    NT = sb("b_NT", [P, T])
    u = alias("b_u", [P, T], at[0] - 4 * T)
    intra = sb("b_intra", [P, T])
    S = sb("b_S", [P, 2, P])
    Sb, v8 = sb("b_Sb", [P, DB, P]), sb("b_v8", [P, DB, P])
    wz = sb("b_wz", [P, DB * (P + DS)])[:]
    vw = sb("b_vw", [P, 2, P])
    sq = sb("b_sq", [P, 2, THIRD])
    rr = sb("b_rr", [P, 2, THIRD])
    cst, cout = sb("b_cst", [P, 3, DB, CW - 1]), sb("b_cout", [P, 3, (DB + 1) * (CW - 1)])
    cw = sb("b_cw", [P, 3, CW])
    gn = sb("b_gn", [P, 1])
    w8, w8h, w8l = sb("b_w8", [P, KD, 8]), sb("b_w8h", [P, KD, 8], F32R), sb("b_w8l", [P, KD, 8], F32R)
    rate, dtb = sb("b_rate", [P, HB]), sb("b_dtb", [P, HB])
    stash = sb("b_stash", [P, 2, THIRD])
    per = sb("b_per", [P, HB, 5, NT_TILES])
    sh = sb("b_sh", [P, 5, NT_TILES])
    t1, t2, t3 = sb("b_t1", [P, HB, NT_TILES]), sb("b_t2", [P, HB, NT_TILES]), sb("b_t3", [P, HB, NT_TILES])
    ND = 2
    LV = 18
    PLAN = [PLAN_START] + [PLAN_NORM] * 6 + [PLAN_GROUP] * 3 + [PLAN_BEFORE] + [PLAN_LEVEL] * LV + [PLAN_STEP] * 8
    filler = Filler(0, PLAN + [12 * 24 - sum(PLAN)])

    with nc.Block() as block:
        @block.sync
        def _(sp):
            for dst, src in ((consts[:], k.b_consts), (w8[:], k.w_beta_decay), (rate[:], k.a_log.partition_broadcast(P)),
                             (dtb[:], k.dt_bias.partition_broadcast(P)), (gn[:], k.b_gain)):
                sp.dma_start(dst, src).then_inc(k.b_loaded.sem, 16)
            sp.wait_ge(k.b_loaded.sem, k.b_loaded.at(80))

        @block.tensor
        def _(pe):
            pe.wait_ge(k.pre.sem, k.pre.at(2))
            for t in range(NT_TILES):
                for part in range(3):
                    for c in range(KD):
                        mm = pe.matmul(k.ps[0][:, 8 * t:8 * t + 8], (xl if part == 1 else xh)[:, c, t * P:(t + 1) * P],
                                       (w8l if part == 2 else w8h)[:, c, :], start=(part == 0 and c == 0),
                                       stop=(part == 2 and c == KD - 1))
            mm.then_inc(k.pre_pe.sem, 1)
            pe.wait_ge(k.pre.sem, k.pre.at(10))
            for dst, m16, m in ((0, upto16, upto), (64, same16, k.ones[:, :])):
                pe.matmul(k.ps[1][:, dst:dst + 32], m, t1[:, :, 0:8], start=True, stop=True)
                mm = pe.matmul(k.ps[1][:, dst + 32:dst + 36], m16, t1[:, :, 8:9], start=True, stop=True)
            mm.then_inc(k.pre_pe.sem, 1)

        @block.scalar
        def _(act):
            act.wait_ge(k.b_loaded.sem, k.b_loaded.at(80))
            act.activation(rate[:, :], rate[:, :], ACT.Exp).then_inc(k.pre_act.sem, 1)
            act.wait_ge(k.pre.sem, k.pre.at(3))
            act.activation(t2[:], t2[:], ACT.Exp).then_inc(k.pre_act.sem, 1)
            act.wait_ge(k.pre.sem, k.pre.at(6))
            act.activation(t3[:], t3[:], ACT.Exp).then_inc(k.pre_act.sem, 1)
            act.wait_ge(k.pre_act.sem, k.pre_act.at(3))
            act.activation(t3[:], t3[:], ACT.Ln, bias=1.0).then_inc(k.pre_act.sem, 1)
            act.wait_ge(k.pre.sem, k.pre.at(12))
            act.activation(t2[:], t2[:], ACT.Exp).then_inc(k.pre_act.sem, 1)
            act.wait_ge(k.pre_act.sem, k.pre_act.at(5))
            act.wait_ge(k.pre.sem, k.pre.at(14))
            act.activation(per[:, :, 2, :], t3[:], ACT.Exp).then_inc(k.pre_act.sem, 1)

        @block.vector
        def _(dve):
            n = [0]

            def then(ins):
                ins.then_inc(k.pre.sem, 1)
                n[0] += 1
                dve.wait_ge(k.pre.sem, k.pre.at(n[0]))

            def both(off):
                return k.ps[0][:, 0:8 * NT_TILES].rearrange("p (t c) -> p c t", c=8)[:, off:off + HB, :]

            dve.memset(wz, 0.0)
            dve.wait_ge(k.b_loaded.sem, k.b_loaded.at(80))
            then(dve.tensor_copy(w8h[:], w8[:]))
            then(dve.tensor_tensor(w8l[:], w8[:], w8h[:].bitcast(F32), ALU.subtract))
            dve.wait_ge(k.pre_pe.sem, k.pre_pe.at(1))
            then(dve.tensor_scalar(t2[:], both(0), -1.0, None, ALU.mult))
            then(dve.tensor_tensor(t1[:], both(HB), dtb[:, :].unsqueeze(2).to_broadcast([P, HB, NT_TILES]), ALU.add))
            then(dve.tensor_scalar(t3[:], t1[:], -1.0, None, ALU.mult))
            then(dve.tensor_tensor(t3[:], t1[:], t3[:], ALU.min))
            dve.wait_ge(k.pre_act.sem, k.pre_act.at(2))
            then(dve.tensor_scalar(t2[:], t2[:], 1.0, None, ALU.add))
            then(dve.reciprocal(per[:, :, 0, :], t2[:]))
            dve.wait_ge(k.pre_act.sem, k.pre_act.at(4))
            then(dve.scalar_tensor_tensor(out=t1[:], in0=t1[:], scalar=0.0, in1=t3[:], op0=ALU.max, op1=ALU.add))
            then(dve.scalar_tensor_tensor(out=t1[:], in0=t1[:], scalar=-1.0,
                                          in1=rate[:, :].unsqueeze(2).to_broadcast([P, HB, NT_TILES]),
                                          op0=ALU.mult, op1=ALU.mult))
            dve.wait_ge(k.pre_pe.sem, k.pre_pe.at(2))
            gc8, gc1 = k.ps[1][:, 0:32].rearrange("p (h t) -> p h t", h=HB), k.ps[1][:, 32:36].unsqueeze(2)
            gl8, gl1 = k.ps[1][:, 64:96].rearrange("p (h t) -> p h t", h=HB), k.ps[1][:, 96:100].unsqueeze(2)
            then(dve.tensor_copy(t2[:, :, 0:8], gc8))
            then(dve.tensor_copy(t2[:, :, 8:9], gc1))
            dve.tensor_scalar(per[:, :, 3, 0:8], gc8, -1.0, None, ALU.mult)
            then(dve.tensor_scalar(per[:, :, 3, 8:9], gc1, -1.0, None, ALU.mult))
            dve.tensor_tensor(t3[:, :, 0:8], gl8, per[:, :, 3, 0:8], ALU.add)
            then(dve.tensor_tensor(t3[:, :, 8:9], gl1, per[:, :, 3, 8:9], ALU.add))
            dve.wait_ge(k.pre_act.sem, k.pre_act.at(6))
            dve.tensor_tensor(per[:, :, 1, :], per[:, :, 0, :], t2[:], ALU.mult)
            then(dve.tensor_copy(per[:, :, 4, :], t1[:]))

    k.pre.base += 15
    k.pre_pe.base += 2
    k.pre_act.base += 6
    k.b_loaded.base += 80

    def third(g):
        return slice(g * THIRD, (g + 1) * THIRD)

    def tile(t):
        return slice(t * P, (t + 1) * P)

    def by_tile(a):
        return a.rearrange("p (t c) -> p t c", c=P)

    def bank(a, b):
        return k.ps[a + b % 2]

    with nc.Block() as block:
        @block.sync
        def _(sp):
            def projections(i):
                if not isinstance(i, int):
                    sp.wait_ge(k.wu_done.sem, k.wu_done.at(3 * i))
                for c in range(3):
                    sp.dma_start(pad[:, c, :], k.proj_dram[4 * i + c]).then_inc(k.pad_landed[c].sem, 16)

            load_units(sp, k, k.next_unit, HB, 4, projections)

        @block.gpsimd
        def _(pool):
            split_units(pool, k, HB, (3, 6, 9, 12))

        def correct(pe, i, r):
            g = r % 3
            pe.wait_ge(k.p1_ready.sem, k.p1_ready.at(LV * i + (r + 1)))
            if r >= 2:
                pe.wait_ge(k.level_done.sem, k.level_done.at(LV * i + (r - 1)))
            if r < LV - 3:
                for t in range(3 * g, 3 * g + 3):
                    pe.matmul(bank(4, r)[:, tile(t % 3)], Y[:, tile(t)], P1[:, tile(t)], start=True, stop=True)
            for t in range(3 * g, 3 * g + 3):
                mm = pe.matmul(bank(6, r)[:, tile(t % 3)], P1[:, tile(t)], Y[:, tile(t)], start=True, stop=True)
            mm.then_inc(k.corrected.sem, 1)

        @block.tensor
        def _(pe):
            with pe.Fori(0, HB) as i:
                filler.products(k, pe, i, 0, xh, xl)
                for r in range(6):
                    filler.products(k, pe, i, 1 + r, xh, xl)
                    pe.wait_ge(k.squared.sem, k.squared.at(9 * i + (r + 1)))
                    if r >= 2:
                        pe.wait_ge(k.lned.sem, k.lned.at(9 * i + (r - 1)))
                    pe.matmul(bank(2, r)[:, 0:THIRD], k.ones[:, :], sq[:, r % 2, :], start=True, stop=True)\
                        .then_inc(k.sq_summed.sem, 1)
                pe.wait_ge(k.per_ready.sem, k.per_ready.at(i + 1))
                pe.wait_ge(k.lned.sem, k.lned.at(9 * i + 6))
                for g in range(3):
                    tiles = range(3 * g, 3 * g + 3)
                    if g >= 1:
                        pe.wait_ge(k.decayed.sem, k.decayed.at(3 * i + g))
                        pe.wait_ge(k.scaled.sem, k.scaled.at(3 * i + g))
                    for t in tiles:
                        o = tile(t % 3)
                        pe.matmul(k.ps[2][:, o], sh[:, 4, t:t + 1].to_broadcast([P, P]), upto if t < 8 else upto16,
                                  start=True, stop=True)
                    for t in tiles:
                        mm = pe.matmul(k.ps[3][:, tile(t % 3)], sh[:, 0, t:t + 1].to_broadcast([P, P]), k.ident[:, :],
                                       start=True, stop=True)
                    mm.then_inc(k.rows_spread.sem, 1)
                    pe.wait_ge(k.l2_done.sem, k.l2_done.at(6 * i + (g + 4)))
                    for t in tiles:
                        pe.matmul(k.ps[4][:, tile(t % 3)], yk[:, tile(t)], yk[:, tile(t)], start=True, stop=True)
                    for t in tiles:
                        mm = pe.matmul(k.ps[5][:, tile(t % 3)], yk[:, tile(t)], yq[:, tile(t)], start=True, stop=True)
                    mm.then_inc(k.grams.sem, 1)
                    for t in tiles:
                        pe.transpose(k.ps[6][:, tile(t % 3)], yk[:, tile(t)], k.ident[:, :])
                    for t in tiles:
                        mm = pe.transpose(k.ps[7][:, tile(t % 3)], yv[:, tile(t)], k.ident[:, :])
                    mm.then_inc(k.kv_turned.sem, 1)
                    filler.products(k, pe, i, 7 + g, xh, xl)
                filler.products(k, pe, i, 10, xh, xl)
                pe.wait_ge(k.decayed.sem, k.decayed.at(3 * i + 3))
                pe.wait_ge(k.scaled.sem, k.scaled.at(3 * i + 3))
                for g in range(3):
                    pe.wait_ge(k.y_started.sem, k.y_started.at(3 * i + (g + 1)))
                    for t in range(3 * g, 3 * g + 3):
                        mm = pe.transpose(k.ps[2 + g][:, tile(t % 3)], Y[:, tile(t)], k.ident[:, :])
                    mm.then_inc(k.y_turned.sem, 1)
                pe.wait_ge(k.x_started.sem, k.x_started.at(3 * i + 3))
                for r in range(LV):
                    g = r % 3
                    pe.wait_ge(k.masked_level.sem, k.masked_level.at(LV * i + (r + 1)))
                    if r >= 2:
                        pe.wait_ge(k.p1_ready.sem, k.p1_ready.at(LV * i + (r - 1)))
                    for t in range(3 * g, 3 * g + 3):
                        mm = pe.matmul(bank(2, r)[:, tile(t % 3)], MT[:, tile(t)], X[:, tile(t)], start=True, stop=True)
                    mm.then_inc(k.p1_done.sem, 1)
                    filler.products(k, pe, i, 11 + r, xh, xl)
                    if r >= 1:
                        correct(pe, i, r - 1)
                correct(pe, i, LV - 1)
                pe.wait_ge(k.level_done.sem, k.level_done.at(LV * i + LV))
                for g in range(3):
                    if g >= 1:
                        pe.wait_ge(k.w_ready.sem, k.w_ready.at(3 * i + g))
                        pe.wait_ge(k.u_ready.sem, k.u_ready.at(3 * i + g))
                    for t in range(3 * g, 3 * g + 3):
                        pe.matmul(k.ps[2][:, tile(t % 3)], kbe[:, tile(t)], Y[:, tile(t)], start=True, stop=True)
                    for t in range(3 * g, 3 * g + 3):
                        mm = pe.matmul(k.ps[3][:, tile(t % 3)], Y[:, tile(t)], vb[:, tile(t)], start=True, stop=True)
                    mm.then_inc(k.wu_done.sem, 1)
                pe.wait_ge(k.w_ready.sem, k.w_ready.at(3 * i + 3))
                pe.wait_ge(k.u_ready.sem, k.u_ready.at(3 * i + 3))
                for t in range(8):
                    s = S[:, t % 2, :]
                    pe.wait_ge(k.s_ready.sem, k.s_ready.at(9 * i + (t + 1)))
                    pe.matmul(bank(2, t)[:, 0:P], wT[:, tile(t)], s, start=True, stop=True).then_inc(k.ws_done.sem, 1)
                    filler.products(k, pe, i, 11 + LV + t, xh, xl)
                    if t >= 2:
                        pe.wait_ge(k.o_copied.sem, k.o_copied.at(9 * i + (t - 1)))
                    pe.wait_ge(k.qg_ready.sem, k.qg_ready.at(3 * i + (t // 3 + 1)))
                    pe.matmul(bank(6, t)[:, 0:P], s, yq[:, tile(t)], start=True, stop=False)
                    pe.wait_ge(k.vw_ready.sem, k.vw_ready.at(9 * i + (t + 1)))
                    pe.matmul(bank(4, t)[:, 0:P], kd[:, tile(t)], vw[:, t % 2, :], start=True, stop=True)\
                        .then_inc(k.kv_done.sem, 1)
                    pe.matmul(bank(6, t)[:, 0:P], vw[:, t % 2, :], intra[:, tile(t)], start=False, stop=True)\
                        .then_inc(k.o_done.sem, 1)
                pe.wait_ge(k.s_loaded.sem, k.s_loaded.at(80 * i + 80))
                pe.wait_ge(k.wz_ready.sem, k.wz_ready.at(i + 1))
                pe.wait_ge(k.s_ready.sem, k.s_ready.at(9 * i + 9))
                for b in range(DB):
                    mm = pe.matmul(k.ps[2][:, 0:P], wz[:, tile(b)], Sb[:, b, :], start=(b == 0), stop=(b == DB - 1))
                mm.then_inc(k.ws_done.sem, 1)
                pe.wait_ge(k.o_copied.sem, k.o_copied.at(9 * i + 7))
                pe.wait_ge(k.vw_ready.sem, k.vw_ready.at(9 * i + 9))
                pe.matmul(k.ps[6][:, 0:P], vw[:, 0, :], intra[:, tile(8)], start=True, stop=False,
                          skip_group_check=True)
                for b in range(DB):
                    c = slice(b * DS, (b + 1) * DS)
                    mm = pe.matmul(k.ps[6][:, c], Sb[:, b, :], yq[:, SEQ + b * DS:SEQ + (b + 1) * DS],
                                   start=False, stop=(b == DB - 1), skip_group_check=True)
                mm.then_inc(k.o_done.sem, 1)
                pe.wait_ge(k.v8_ready.sem, k.v8_ready.at(i + 1))
                for h in range(2):
                    mm = pe.matmul(k.ps[4 + h][:, :], kd[:, tile(8)],
                                   v8[:, 4 * h:4 * h + 4, :].rearrange("p b c -> p (b c)"), start=True, stop=True)
                mm.then_inc(k.kv_done.sem, 1)
                filler.products(k, pe, i, 19 + LV, xh, xl)
                for g in range(3):
                    pe.wait_ge(k.squared.sem, k.squared.at(9 * i + (6 + g + 1)))
                    if g == 2:
                        pe.wait_ge(k.lned.sem, k.lned.at(9 * i + 7))
                    pe.matmul(bank(2, g)[:, 0:THIRD], k.ones[:, :], sq[:, g % 2, :], start=True, stop=True)\
                        .then_inc(k.sq_summed.sem, 1)

        @block.scalar
        def _(act):
            def evacuate(i, place):
                for g in filler.finished(place):
                    act.wait_ge(k.dense_done.sem, k.dense_done.at(12 * i + (g + 1)))
                    b = g % 2
                    act.wait_ge(k.kv_slot[b].sem, k.kv_slot[b].at(96 * i + (16 * (g // 2) + 32)))
                    act.activation(stash[:, b, :], k.ps[g % ND][:, 0:THIRD], ACT.Copy).then_inc(k.evacuated.sem, 1)
                    act.wait_ge(k.evacuated.sem, k.evacuated.at(12 * i + (g + 1 + ND)))
                    act.dma_start(k.gate_dram[4 * i + g // 3][:, third(g % 3)], stash[:, b, :])\
                        .then_inc(k.kv_slot[b].sem, 16)

            with act.Fori(0, HB) as i:
                act.wait_ge(k.kv_done.sem, k.kv_done.at(9 * i + 1))
                act.wait_ge(k.s_out.sem, k.s_out.at(48 * i + 48))
                act.dma_start(cst[:], k.conv_state[i]).then_inc(k.s_loaded.sem, 16)
                act.dma_start(cw[:], k.conv_w[i]).then_inc(k.s_loaded.sem, 16)
                for b in range(3):
                    bb = slice(3 * b, min(DB, 3 * b + 3))
                    act.dma_start(Sb[:, bb, :], k.state_s[i][:, bb, :]).then_inc(k.s_loaded.sem, 16)
                act.dma_start(z[:, :], k.proj_dram[4 * i + 3][:, 0:T]).then_inc(k.z_landed.sem, 16)
                evacuate(i, 0)
                for c in range(3):
                    act.wait_ge(k.convolved.sem, k.convolved.at(3 * i + (c + 1)))
                    act.activation(y[:, c, :], y[:, c, :], ACT.Silu).then_inc(k.silued.sem, 1)
                act.wait_ge(k.z_landed.sem, k.z_landed.at(16 * i + 16))
                act.activation(z[:, :], z[:, :], ACT.Silu).then_inc(k.silued.sem, 1)
                act.preload_act_table_set("natural_log_exp_and_others")
                act.wait_ge(k.silued.sem, k.silued.at(4 * i + 4))

                def square(r, src):
                    if r >= 2:
                        act.wait_ge(k.sq_summed.sem, k.sq_summed.at(9 * i + (r - 1)))
                    act.activation(sq[:, r % 2, :], src, ACT.Square).then_inc(k.squared.sem, 1)

                def root(r, scale):
                    act.wait_ge(k.sq_summed.sem, k.sq_summed.at(9 * i + (r + 1)))
                    if 2 <= r < 8:
                        act.wait_ge(k.l2_done.sem, k.l2_done.at(6 * i + min(r - 1, 6)))
                    elif r == 8:
                        act.wait_ge(k.o_normed.sem, k.o_normed.at(3 * i + 1))
                    b = k.ps[2 + r % 2] if r < 6 else k.ps[2 + (r - 6) % 2]
                    act.activation(rr[:, r % 2, :], b[:, 0:THIRD], ACT.Ln, bias=k.eps[:, 0:1], scale=scale)\
                        .then_inc(k.lned.sem, 1)
                    act.wait_ge(k.lned.sem, k.lned.at(9 * i + (r + 1)))
                    act.activation(rr[:, r % 2, :], rr[:, r % 2, :], ACT.Exp, scale=-0.5).then_inc(k.rooted.sem, 1)

                for r in range(7):
                    if r < 6:
                        square(r, y[:, r // 3, third(r % 3)])
                    if r >= 1:
                        root(r - 1, 1.0)
                        evacuate(i, r)
                for g in range(3):
                    act.wait_ge(k.rows_spread.sem, k.rows_spread.at(3 * i + (g + 1)))
                    act.activation(eg[:, third(g)], k.ps[2][:, 0:THIRD], ACT.Exp).then_inc(k.eg_ready.sem, 1)
                    act.wait_ge(k.dt_args.sem, k.dt_args.at(3 * i + (g + 1)))
                    act.activation(DT[:, third(g)], DT[:, third(g)], ACT.Exp).then_inc(k.dt_ready.sem, 1)
                    if g >= 1:
                        evacuate(i, 6 + g)
                evacuate(i, 9)
                evacuate(i, 10)
                for g in range(3):
                    act.wait_ge(k.y_turned.sem, k.y_turned.at(3 * i + (g + 1)))
                    act.activation(X[:, third(g)], k.ps[2 + g][:, 0:THIRD], ACT.Copy).then_inc(k.x_started.sem, 1)
                for r in range(LV):
                    act.wait_ge(k.p1_done.sem, k.p1_done.at(LV * i + (r + 1)))
                    if r >= 3:
                        act.wait_ge(k.corrected.sem, k.corrected.at(LV * i + (r - 2)))
                    act.activation(P1[:, third(r % 3)], bank(2, r)[:, 0:THIRD], ACT.Copy).then_inc(k.p1_ready.sem, 1)
                    if r >= 1:
                        evacuate(i, 10 + r)
                evacuate(i, 10 + LV)
                for g in range(3):
                    act.wait_ge(k.wu_done.sem, k.wu_done.at(3 * i + (g + 1)))
                    act.activation(wT[:, third(g)], k.ps[2][:, 0:THIRD], ACT.Copy).then_inc(k.w_ready.sem, 1)
                for t in range(9):
                    act.wait_ge(k.o_done.sem, k.o_done.at(9 * i + (t + 1)))
                    act.activation(oT[:, tile(t)], (bank(6, t) if t < 8 else k.ps[6])[:, 0:P], ACT.Copy)\
                        .then_inc(k.o_copied.sem, 1)
                    if 1 <= t <= 8:
                        evacuate(i, 10 + LV + t)
                act.wait_ge(k.o_copied.sem, k.o_copied.at(9 * i + 9))
                evacuate(i, 19 + LV)
                for g in range(4):
                    if g < 3:
                        square(6 + g, oT[:, third(g)])
                    if g >= 1:
                        root(6 + g - 1, 1.0 / DHB)
                act.wait_ge(k.s_final.sem, k.s_final.at(i + 1))
                act.dma_start(k.p_s_out[i], S[:, 0, :]).then_inc(k.s_out.sem, 16)
                act.dma_start(k.s_s_out[i], Sb[:]).then_inc(k.s_out.sem, 16)
                act.dma_start(k.conv_out[i], cout[:]).then_inc(k.s_out.sem, 16)
                act.wait_ge(k.o_scaled.sem, k.o_scaled.at(3 * i + 3))
                act.dma_start(k.yb_dram[i], oT[:, :]).then_inc(k.yb_stored.sem, 16)
            act.wait_ge(k.yb_stored.sem, k.yb_stored.at(16 * HB + 16))
            act.wait_ge(k.s_out.sem, k.s_out.at(48 * HB + 48))
            for b in range(2):
                act.wait_ge(k.kv_slot[b].sem, k.kv_slot[b].at(96 * HB + 32))

        @block.vector
        def _(dve):
            with dve.Fori(0, HB) as i:
                dve.tensor_copy(sh[:], per[:, i]).then_inc(k.per_ready.sem, 1)
                dve.wait_ge(k.s_loaded.sem, k.s_loaded.at(80 * i + 80))
                dve.wait_ge(k.yb_stored.sem, k.yb_stored.at(16 * i + 16))
                for c in range(3):
                    dve.wait_ge(k.pad_landed[c].sem, k.pad_landed[c].at(16 * i + 16))
                    dve.memset(pad[:, c, 0:CW - 1], 0.0)
                    m = dve.tensor_copy(pad[:, c, PADP:].rearrange("p (b c) -> p b c", c=PADS)[:, :, 0:CW - 1],
                                        cst[:, c])
                m.then_inc(k.pad_ready.sem, 1)
                dve.wait_ge(k.pad_ready.sem, k.pad_ready.at(i + 1))
                for c in range(3):
                    pp, ss = pad[:, c, 0:PADP], pad[:, c, PADP:].rearrange("p (b c) -> p b c", c=PADS)
                    yp, ys = y[:, c, 0:SEQ], y[:, c, SEQ:T].rearrange("p (b c) -> p b c", c=DS)
                    for j in range(CW):
                        w = cw[:, c, j:j + 1]
                        if j == 0:
                            dve.tensor_scalar(yp, pp[:, 0:SEQ], w, None, ALU.mult)
                            m = dve.tensor_scalar(ys, ss[:, :, 0:DS], w, None, ALU.mult)
                        else:
                            dve.wait_ge(k.tap.sem, k.tap.at(9 * i + (3 * c + j)))
                            dve.scalar_tensor_tensor(out=yp, in0=pp[:, j:j + SEQ], scalar=w, in1=yp,
                                                     op0=ALU.mult, op1=ALU.add)
                            m = dve.scalar_tensor_tensor(out=ys, in0=ss[:, :, j:j + DS], scalar=w, in1=ys,
                                                         op0=ALU.mult, op1=ALU.add)
                        m.then_inc(k.tap.sem if j < CW - 1 else k.convolved.sem, 1)
                    dve.tensor_copy(cout[:, c, 0:CW - 1], pp[:, SEQ:PADP])
                    dve.tensor_copy(cout[:, c, CW - 1:].rearrange("p (b c) -> p b c", c=CW - 1), ss[:, :, DS:PADS])
                for r in range(6):
                    dve.wait_ge(k.rooted.sem, k.rooted.at(9 * i + (r + 1)))
                    a = y[:, r // 3, third(r % 3)]
                    dve.scalar_tensor_tensor(out=a, in0=a, scalar=DHB ** -0.5 if r < 3 else 1.0, in1=rr[:, r % 2, :],
                                             op0=ALU.mult, op1=ALU.mult).then_inc(k.l2_done.sem, 1)
                for g in range(3):
                    dve.wait_ge(k.eg_ready.sem, k.eg_ready.at(3 * i + (g + 1)))
                    for t in range(3 * g, 3 * g + 3):
                        m = dve.scalar_tensor_tensor(out=DT[:, tile(t)], in0=k.ps[2][:, tile(t % 3)],
                                                     scalar=sh[:, 3, t:t + 1], in1=future if t < 8 else future16,
                                                     op0=ALU.add, op1=ALU.add)
                    m.then_inc(k.dt_args.sem, 1)
                    dve.wait_ge(k.grams.sem, k.grams.at(3 * i + (g + 1)))
                    dve.wait_ge(k.dt_ready.sem, k.dt_ready.at(3 * i + (g + 1)))
                    dve.tensor_tensor(intra[:, third(g)], k.ps[5][:, 0:THIRD], DT[:, third(g)], ALU.mult)
                    dve.tensor_tensor(NT[:, third(g)], k.ps[4][:, 0:THIRD], DT[:, third(g)], ALU.mult)\
                        .then_inc(k.nt_made.sem, 1)
                    dve.tensor_tensor(yq[:, third(g)], yq[:, third(g)], eg[:, third(g)], ALU.mult)\
                        .then_inc(k.qg_ready.sem, 1)
                    dve.wait_ge(k.nt_made.sem, k.nt_made.at(3 * i + (g + 1)))
                    dve.tensor_tensor(NT[:, third(g)], k.ps[3][:, 0:THIRD], NT[:, third(g)], ALU.mult)\
                        .then_inc(k.decayed.sem, 1)
                    dve.wait_ge(k.kv_turned.sem, k.kv_turned.at(3 * i + (g + 1)))
                    for dst, src, n in ((kbe, 6, 1), (kd, 6, 2), (vb, 7, 0)):
                        m = dve.tensor_tensor(by_tile(dst[:, third(g)]), by_tile(k.ps[src][:, 0:THIRD]),
                                              sh[:, n, 3 * g:3 * g + 3].unsqueeze(2).to_broadcast([P, 3, P]), ALU.mult)
                    m.then_inc(k.scaled.sem, 1)
                dve.wait_ge(k.decayed.sem, k.decayed.at(3 * i + 3))

                def repeated(a):
                    return a.unsqueeze(1).to_broadcast([P, 3, P])

                for g in range(3):
                    dve.tensor_tensor(by_tile(MT[:, third(g)]), by_tile(NT[:, third(g)]), repeated(level_mask[0]),
                                      ALU.mult).then_inc(k.first_mask.sem, 1)
                    dve.wait_ge(k.first_mask.sem, k.first_mask.at(3 * i + (g + 1)))
                    dve.scalar_tensor_tensor(out=by_tile(Y[:, third(g)]), in0=by_tile(MT[:, third(g)]), scalar=-1.0,
                                             in1=repeated(k.ident[:, :]), op0=ALU.mult, op1=ALU.add)\
                        .then_inc(k.y_started.sem, 1)

                def mask_level(r):
                    if r >= 3:
                        dve.wait_ge(k.p1_done.sem, k.p1_done.at(LV * i + (r - 2)))
                    g = r % 3
                    dve.tensor_tensor(by_tile(MT[:, third(g)]), by_tile(NT[:, third(g)]),
                                      repeated(level_mask[1 + r // 3]), ALU.mult).then_inc(k.masked_level.sem, 1)

                dve.wait_ge(k.y_started.sem, k.y_started.at(3 * i + 3))
                dve.wait_ge(k.x_started.sem, k.x_started.at(3 * i + 3))
                for r in range(3):
                    mask_level(r)
                for r in range(LV):
                    g = r % 3
                    dve.wait_ge(k.corrected.sem, k.corrected.at(LV * i + (r + 1)))
                    if r < LV - 3:
                        dve.tensor_tensor(X[:, third(g)], X[:, third(g)], bank(4, r)[:, 0:THIRD], ALU.subtract)
                    dve.tensor_tensor(Y[:, third(g)], Y[:, third(g)], bank(6, r)[:, 0:THIRD], ALU.subtract)\
                        .then_inc(k.level_done.sem, 1)
                    if r + 3 < LV:
                        mask_level(r + 3)
                for g in range(3):
                    dve.wait_ge(k.wu_done.sem, k.wu_done.at(3 * i + (g + 1)))
                    dve.wait_ge(k.w_ready.sem, k.w_ready.at(3 * i + (g + 1)))
                    dve.tensor_copy(u[:, third(g)], k.ps[3][:, 0:THIRD]).then_inc(k.u_ready.sem, 1)
                dve.tensor_copy(wz.rearrange("p (b m) -> p b m", b=DB)[:, :, 0:DS],
                                wT[:, SEQ:T].rearrange("p (b c) -> p b c", c=DS)).then_inc(k.wz_ready.sem, 1)
                dve.memset(S[:, 0, :], 0.0).then_inc(k.s_ready.sem, 1)
                dve.wait_ge(k.s_ready.sem, k.s_ready.at(9 * i + 1))
                for t in range(8):
                    dve.wait_ge(k.ws_done.sem, k.ws_done.at(9 * i + (t + 1)))
                    if t >= 2:
                        dve.wait_ge(k.o_done.sem, k.o_done.at(9 * i + (t - 1)))
                    dve.tensor_tensor(vw[:, t % 2, :], u[:, tile(t)], bank(2, t)[:, 0:P], ALU.subtract)\
                        .then_inc(k.vw_ready.sem, 1)
                    dve.wait_ge(k.kv_done.sem, k.kv_done.at(9 * i + (t + 1 + 1)))
                    if t >= 1:
                        dve.wait_ge(k.o_done.sem, k.o_done.at(9 * i + t))
                    last = tile(t).stop - 1
                    dve.scalar_tensor_tensor(out=S[:, (t + 1) % 2, :], in0=S[:, t % 2, :], scalar=eg[:, last:last + 1],
                                             in1=bank(4, t)[:, 0:P], op0=ALU.mult, op1=ALU.add)\
                        .then_inc(k.s_ready.sem, 1)
                    dve.wait_ge(k.s_ready.sem, k.s_ready.at(9 * i + (t + 2)))
                dve.wait_ge(k.ws_done.sem, k.ws_done.at(9 * i + 9))
                dve.wait_ge(k.o_done.sem, k.o_done.at(9 * i + 7))
                dve.tensor_tensor(vw[:, 0, :], u[:, tile(8)], k.ps[2][:, 0:P], ALU.subtract).then_inc(k.vw_ready.sem, 1)
                dve.wait_ge(k.vw_ready.sem, k.vw_ready.at(9 * i + 9))
                dve.tensor_tensor(v8[:], vw[:, 0:1, :].to_broadcast([P, DB, P]),
                                  streams.unsqueeze(2).to_broadcast([P, DB, P]), ALU.mult).then_inc(k.v8_ready.sem, 1)
                dve.wait_ge(k.o_done.sem, k.o_done.at(9 * i + 9))
                dve.tensor_tensor(Sb[:], Sb[:], eg[:, SEQ:T].rearrange("p (b c) -> p b c", c=DS)[:, :, DS - 1:DS]
                                  .to_broadcast([P, DB, P]), ALU.mult).then_inc(k.s_decayed.sem, 1)
                dve.wait_ge(k.kv_done.sem, k.kv_done.at(9 * i + 10))
                dve.wait_ge(k.s_decayed.sem, k.s_decayed.at(i + 1))
                dve.tensor_tensor(Sb[:, 0:4, :], Sb[:, 0:4, :], k.ps[4].rearrange("p (b c) -> p b c", c=P), ALU.add)
                dve.tensor_tensor(Sb[:, 4:8, :], Sb[:, 4:8, :], k.ps[5].rearrange("p (b c) -> p b c", c=P), ALU.add)\
                    .then_inc(k.s_final.sem, 1)
                for g in range(3):
                    dve.wait_ge(k.rooted.sem, k.rooted.at(9 * i + (6 + g + 1)))
                    dve.scalar_tensor_tensor(out=oT[:, third(g)], in0=oT[:, third(g)], scalar=gn[:, 0:1],
                                             in1=rr[:, (6 + g) % 2, :], op0=ALU.mult, op1=ALU.mult)\
                        .then_inc(k.o_normed.sem, 1)
                    dve.wait_ge(k.o_normed.sem, k.o_normed.at(3 * i + (g + 1)))
                    dve.tensor_tensor(oT[:, third(g)], oT[:, third(g)], z[:, third(g)], ALU.mult)\
                        .then_inc(k.o_scaled.sem, 1)

    units_done(k, HB, 4)
    for b in range(2):
        k.kv_slot[b].base += 96 * HB
    for c in range(3):
        k.pad_landed[c].base += 16 * HB
    k.z_landed.base += 16 * HB
    for sig, n in ((k.evacuated, 12), (k.dense_done, 12), (k.squared, 9), (k.lned, 9), (k.sq_summed, 9), (k.rooted, 9),
                   (k.per_ready, 1), (k.decayed, 3), (k.scaled, 3), (k.rows_spread, 3), (k.l2_done, 6), (k.grams, 3),
                   (k.kv_turned, 3), (k.y_started, 3), (k.y_turned, 3), (k.x_started, 3), (k.masked_level, LV),
                   (k.p1_ready, LV), (k.p1_done, LV), (k.level_done, LV), (k.corrected, LV), (k.w_ready, 3),
                   (k.u_ready, 3), (k.wu_done, 3), (k.s_ready, 9), (k.ws_done, 9), (k.o_copied, 9), (k.qg_ready, 3),
                   (k.vw_ready, 9), (k.kv_done, 9), (k.o_done, 9), (k.s_loaded, 80), (k.wz_ready, 1), (k.v8_ready, 1),
                   (k.pad_ready, 1), (k.silued, 4), (k.convolved, 3), (k.eg_ready, 3), (k.dt_args, 3), (k.dt_ready, 3),
                   (k.s_final, 1), (k.s_out, 48), (k.o_scaled, 3), (k.o_normed, 3), (k.yb_stored, 16), (k.tap, 9),
                   (k.nt_made, 3), (k.first_mask, 3), (k.s_decayed, 1)):
        sig.base += n * HB


def memory_phase(nc, k, own_norm, norm, xh, xl, work):
    kv = nc.alloc_sbuf_tensor_at("m_kv", [P, 2, NMEM], F32, offset=work)
    nat = nc.alloc_sbuf_tensor_at("m_nat", [P, 2, NMEM], F32, offset=work + 8 * NMEM)
    pe_norm = {3: [lambda pe: norm.sums(pe, 0)], 5: [lambda pe: norm.sums(pe, 1)], 7: [lambda pe: norm.sums(pe, 2)]}
    act_norm = {0: [lambda act: norm.square(act, 0)], 1: [lambda act: norm.square(act, 1)],
                2: [lambda act: norm.square(act, 2)], 4: [lambda act: norm.root(act, 0), lambda act: norm.upper(act, 0)],
                6: [lambda act: norm.root(act, 1), lambda act: norm.upper(act, 1)],
                8: [lambda act: norm.root(act, 2), lambda act: norm.upper(act, 2)]}
    UNITS = 2 * KD
    with nc.Block() as block:
        @block.sync
        def _(sp):
            load_units(sp, k, k.next_unit, 1, UNITS)

        @block.gpsimd
        def _(pool):
            for j in range(UNITS):
                s = slot(j, UNITS)
                pool.wait_ge(k.unit_hi.sem, k.unit_hi.at(j + 1))
                if j >= RING:
                    pool.wait_ge(k.dense_done.sem, k.dense_done.at(last_use(j, UNITS)[1] + 1))
                pool.tensor_tensor(k.w_lo[s][:, :], k.w_raw[s][:, :], k.w_hi[s][:, :].bitcast(F32), ALU.subtract)\
                    .then_inc(k.unit_split.sem, 1)

        @block.tensor
        def _(pe):
            own_norm.tensor(pe)
            for h in range(2):
                pe.wait_ge(own_norm.s.nsplit[h].sem, own_norm.s.nsplit[h].at(1))

            def turn(j):
                pe.wait_ge(k.evacuated.sem, k.evacuated.at(j + 1 + 2))
                for h in range(2):
                    mm = pe.transpose(k.ps[2 + j % 2][:, h * P:(h + 1) * P], kv[:, j % 2, h * P:(h + 1) * P],
                                      k.ident[:, :])
                mm.then_inc(k.turned.sem, 1)

            for j in range(UNITS):
                s = slot(j, UNITS)
                pe.wait_ge(k.unit_split.sem, k.unit_split.at(j + 1))
                pe.wait_ge(k.evacuated.sem, k.evacuated.at(j + 1))
                tiles = [(k.w_hi[s][:, c * P:(c + 1) * P], k.w_lo[s][:, c * P:(c + 1) * P], xh[:, c, :], xl[:, c, :])
                         for c in range(KD)]
                product(pe, k.ps[j % 2][:, 0:NMEM], tiles, 0, NMEM).then_inc(k.dense_done.sem, 1)
                if j >= 1:
                    turn(j - 1)
                for step in pe_norm.get(j, []):
                    step(pe)
            turn(UNITS - 1)

        @block.scalar
        def _(act):
            def unit_upper(j):
                s = slot(j, UNITS)
                act.wait_ge(k.raw_landed[s].sem, k.raw_landed[s].at(16 * (sharing(j, UNITS).index(j) + 1)))
                if j >= RING:
                    act.wait_ge(k.dense_done.sem, k.dense_done.at(last_use(j, UNITS)[1] + 1))
                act.activation(k.w_hi[s][:, :], k.w_raw[s][:, :], ACT.Copy).then_inc(k.unit_hi.sem, 1)

            own_norm.scalar(act)
            act.wait_ge(k.x_loaded.sem, k.x_loaded.at(16))
            for j in range(2):
                unit_upper(j)
            for j in range(UNITS + 1):
                if j + 2 < UNITS:
                    unit_upper(j + 2)
                if j < UNITS:
                    act.wait_ge(k.dense_done.sem, k.dense_done.at(j + 1))
                    act.wait_ge(k.kv_slot[j % 2].sem, k.kv_slot[j % 2].at(32 * (j // 2) + 32))
                    act.activation(kv[:, j % 2, :], k.ps[j % 2][:, 0:NMEM], ACT.Copy).then_inc(k.evacuated.sem, 1)
                    act.wait_ge(k.evacuated.sem, k.evacuated.at(j + 1 + 2))
                    act.dma_start(k.mem_out[j], kv[:, j % 2, :]).then_inc(k.kv_slot[j % 2].sem, 16)
                if j >= 1:
                    act.wait_ge(k.turned.sem, k.turned.at(j))
                    act.activation(nat[:, (j - 1) % 2, :], k.ps[2 + (j - 1) % 2][:, 0:NMEM], ACT.Copy)\
                        .then_inc(k.pt_ready.sem, 1)
                    act.wait_ge(k.pt_ready.sem, k.pt_ready.at(j))
                    act.dma_start(k.mem_turned[j - 1], nat[:, (j - 1) % 2, :]).then_inc(k.kv_slot[(j - 1) % 2].sem, 16)
                for step in act_norm.get(j, []):
                    step(act)
            for b in range(2):
                act.wait_ge(k.kv_slot[b].sem, k.kv_slot[b].at(32 * (UNITS // 2) + 32))

        @block.vector
        def _(dve):
            own_norm.vector(dve, both=True)
            dve.wait_ge(k.x_loaded.sem, k.x_loaded.at(16))
            norm.vector(dve, both=True)

    own_norm.done()
    norm.done()
    units_done(k, 1, UNITS)
    k.x_loaded.base += 16
    n = UNITS
    for sig in (k.dense_done, k.evacuated, k.turned, k.pt_ready):
        sig.base += n
    for b in range(2):
        k.kv_slot[b].base += 16 * n


def job_order(units):
    return [(u, n) for n in range(3) for u in range(RING)] + [(u, n) for u in range(RING, units) for n in range(3)]


def used_after(order, per_job):
    return tuple(per_job * (1 + max(j for j, (u, _) in enumerate(order) if u == m)) for m in range(KD))


def load_third(eng, k, st, sources, n):
    if n >= 2:
        eng.wait_ge(k.third_split.sem, k.third_split.at(n - 1))
    for c, src in sources:
        eng.dma_start(st[n % 2][:, c:c + 4, :], src[:, :, n * THIRD:(n + 1) * THIRD])\
            .then_inc(k.third_landed[n % 2].sem, 16)


def third_upper(act, k, st, hi, n):
    act.wait_ge(k.third_landed[n % 2].sem, k.third_landed[n % 2].at(32 * (n // 2 + 1)))
    act.activation(hi[:, :, n * THIRD:(n + 1) * THIRD], st[n % 2][:], ACT.Copy).then_inc(k.third_hi.sem, 1)


def third_lower(dve, k, st, hi, lo, n):
    dve.wait_ge(k.third_hi.sem, k.third_hi.at(n + 1))
    dve.tensor_tensor(lo[:, :, n * THIRD:(n + 1) * THIRD], st[n % 2][:], hi[:, :, n * THIRD:(n + 1) * THIRD].bitcast(F32),
                      ALU.subtract).then_inc(k.third_split.sem, 1)


def thirds_done(k):
    k.third_hi.base += 3
    k.third_split.base += 3
    for b in range(2):
        k.third_landed[b].base += 32 * (2 - b)


def merge_phase(nc, k, sources, yh, yl, hi, lo, work, stage):
    gt = nc.alloc_sbuf_tensor_at("e_gate", [P, 2, 2, THIRD], F32, offset=work)
    a1 = nc.alloc_sbuf_tensor_at("e_a", [P, 2, THIRD], F32, offset=work + 16 * THIRD)
    b1 = nc.alloc_sbuf_tensor_at("e_b", [P, 2, THIRD], F32, offset=work + 24 * THIRD)
    m1 = nc.alloc_sbuf_tensor_at("e_m", [P, 2, THIRD], F32, offset=work + 32 * THIRD)
    st = [nc.alloc_sbuf_tensor_at(f"e_st{b}", [P, KD, THIRD], F32, offset=at + RING * 4 * T) for b, at in enumerate(stage)]
    order = job_order(KD)
    JOBS = len(order)

    def chunk(a, j):
        m, n = order[j]
        return a[:, m, n * THIRD:(n + 1) * THIRD]

    with nc.Block() as block:
        @block.sync
        def _(sp):
            for n in range(2):
                load_third(sp, k, st, sources, n)
            load_units(sp, k, k.next_unit, 1, KD)

        @block.gpsimd
        def _(pool):
            split_units(pool, k, 1, used_after(order, 2))

        @block.tensor
        def _(pe):
            for j, (m, n) in enumerate(order):
                if n == 0:
                    pe.wait_ge(k.unit_split.sem, k.unit_split.at(m + 1))
                if m < RING:
                    pe.wait_ge(k.third_split.sem, k.third_split.at(n + 1))
                pe.wait_ge(k.merged.sem, k.merged.at(j + 1))
                s = m % RING
                for ab in range(2):
                    tiles = [(k.w_hi[s][:, c * P:(c + 1) * P], k.w_lo[s][:, c * P:(c + 1) * P], yh[:, c, :], yl[:, c, :])
                             for c in range(4 * ab, 4 * ab + 4)]
                    product(pe, k.ps[2 * (j % 2) + ab][:, 0:THIRD], tiles, n * THIRD, (n + 1) * THIRD)\
                        .then_inc(k.dense_done.sem, 1)

        @block.scalar
        def _(act):
            def load(j):
                m, n = order[j]
                for ab in range(2):
                    act.dma_start(gt[:, j % 2, ab, :], k.gate_dram[8 * ab + m][:, n * THIRD:(n + 1) * THIRD])\
                        .then_inc(k.kv_slot[j % 2].sem, 16)

            def gates(j):
                act.wait_ge(k.kv_slot[j % 2].sem, k.kv_slot[j % 2].at(32 * (j // 2) + 32 + 32))
                act.activation(gt[:, j % 2], gt[:, j % 2], ACT.Sigmoid).then_inc(k.gate_sigmoid.sem, 1)

            load(0)
            load(1)
            third_upper(act, k, st, yh, 0)
            gates(0)
            load_third(act, k, st, sources, 2)
            third_upper(act, k, st, yh, 1)
            for j in range(JOBS):
                if j == RING:
                    third_upper(act, k, st, yh, 2)
                if j + 1 < JOBS:
                    gates(j + 1)
                act.wait_ge(k.merged.sem, k.merged.at(j + 1 + 2))
                act.activation(chunk(hi, j), m1[:, j % 2, :], ACT.Copy).then_inc(k.merged_hi.sem, 1)
                if j + 2 < JOBS:
                    load(j + 2)

        @block.vector
        def _(dve):
            third_lower(dve, k, st, yh, yl, 0)
            third_lower(dve, k, st, yh, yl, 1)
            for j in range(JOBS):
                if j == RING:
                    third_lower(dve, k, st, yh, yl, 2)
                dve.wait_ge(k.dense_done.sem, k.dense_done.at(2 * j + 2))
                dve.wait_ge(k.gate_sigmoid.sem, k.gate_sigmoid.at(j + 1))
                dve.tensor_tensor(a1[:, j % 2, :], k.ps[2 * (j % 2)][:, 0:THIRD], gt[:, j % 2, 0, :], ALU.mult)
                dve.tensor_tensor(b1[:, j % 2, :], k.ps[2 * (j % 2) + 1][:, 0:THIRD], gt[:, j % 2, 1, :], ALU.mult)\
                    .then_inc(k.gated.sem, 1)
                dve.wait_ge(k.gated.sem, k.gated.at(j + 1))
                if j >= 2:
                    dve.wait_ge(k.merged_hi.sem, k.merged_hi.at(j - 1))
                dve.tensor_tensor(m1[:, j % 2, :], a1[:, j % 2, :], b1[:, j % 2, :], ALU.add).then_inc(k.merged.sem, 1)
                dve.wait_ge(k.merged_hi.sem, k.merged_hi.at(j + 1))
                dve.tensor_tensor(chunk(lo, j), m1[:, j % 2, :], chunk(hi, j).bitcast(F32), ALU.subtract)\
                    .then_inc(k.merged_split.sem, 1)

    units_done(k, 1, KD)
    thirds_done(k)
    k.dense_done.base += 2 * JOBS
    for sig in (k.merged, k.gated, k.gate_sigmoid, k.merged_hi, k.merged_split):
        sig.base += JOBS
    for b in range(2):
        k.kv_slot[b].base += 16 * JOBS


def residual_phase(nc, k, x, xh, xl, sources=None, work=None, x_from=None):
    order = job_order(KD)
    if sources:
        st = [nc.alloc_sbuf_tensor_at(f"r_st{b}", [P, KD, THIRD], F32, offset=work + 4 * KD * THIRD * b) for b in range(2)]

    with nc.Block() as block:
        @block.sync
        def _(sp):
            if sources:
                for n in range(2):
                    load_third(sp, k, st, sources, n)
            load_units(sp, k, k.next_unit, 1, KD)

        @block.gpsimd
        def _(pool):
            split_units(pool, k, 1, used_after(order, 1))

        @block.tensor
        def _(pe):
            for j, (m, n) in enumerate(order):
                if n == 0:
                    pe.wait_ge(k.unit_split.sem, k.unit_split.at(m + 1))
                if sources and m < RING:
                    pe.wait_ge(k.third_split.sem, k.third_split.at(n + 1))
                pe.wait_ge(k.x_added.sem, k.x_added.at(j + 1))
                s = m % RING
                tiles = [(k.w_hi[s][:, c * P:(c + 1) * P], k.w_lo[s][:, c * P:(c + 1) * P], xh[:, c, :], xl[:, c, :])
                         for c in range(KD)]
                product(pe, k.ps[j % NPS][:, 0:THIRD], tiles, n * THIRD, (n + 1) * THIRD).then_inc(k.dense_done.sem, 1)

        @block.scalar
        def _(act):
            if x_from is not None:
                for c in range(KD):
                    act.dma_start(x[:, c, :], x_from[c]).then_inc(k.x_landed[c].sem, 16)
            if sources:
                third_upper(act, k, st, xh, 0)
                load_third(act, k, st, sources, 2)
                third_upper(act, k, st, xh, 1)
                third_upper(act, k, st, xh, 2)

        @block.vector
        def _(dve):
            if sources:
                third_lower(dve, k, st, xh, xl, 0)
                third_lower(dve, k, st, xh, xl, 1)
            for j, (m, n) in enumerate(order):
                if sources and j == RING:
                    third_lower(dve, k, st, xh, xl, 2)
                dve.wait_ge(k.dense_done.sem, k.dense_done.at(j + 1))
                if x_from is not None and n == 0:
                    dve.wait_ge(k.x_landed[m].sem, k.x_landed[m].at(16))
                xs = x[:, m, n * THIRD:(n + 1) * THIRD]
                dve.tensor_tensor(xs, xs, k.ps[j % NPS][:, 0:THIRD], ALU.add).then_inc(k.x_added.sem, 1)

    units_done(k, 1, KD)
    if sources:
        thirds_done(k)
    if x_from is not None:
        for c in range(KD):
            k.x_landed[c].base += 16
    for sig in (k.dense_done, k.x_added):
        sig.base += len(order)


def cross_phase(nc, k, make_norm, xh, xl, room1, room2):
    at = {1: room1, 2: room2}

    def sb(name, room, shape):
        t = nc.alloc_sbuf_tensor_at(name, shape, F32, offset=at[room])
        at[room] += (4 * int(np.prod(shape[1:])) + 31) // 32 * 32
        return t

    q, oc = sb("x_q", 1, [P, 2, T]), sb("x_o", 1, [P, 2, T])
    mk, mv = sb("x_mk", 1, [P, 2, NMEM]), sb("x_mv", 1, [P, 2, 2, P])
    qz = sb("x_qz", 1, [P, 2, DB, 32])
    sk = sb("x_sk", 2, [P, 2, DB, NMEM])
    sv = [sb("x_sv0", 1, [P, 4, 2, DHX]), sb("x_sv1", 2, [P, 4, 2, DHX])]
    sc, pt = sb("x_sc", 1, [P, 2, NMEM]), sb("x_pt", 1, [P, 2, 2, P])
    nmax, rsum, rinv = (sb(n, 2, [P, 2]) for n in ("x_nmax", "x_rsum", "x_rinv"))
    STEPS, LOADS = 9, 7
    norm = make_norm(room2, room1 + 8 * T)

    def bank(a, b):
        return k.ps[a + b % 2]

    with nc.Block() as block:
        @block.sync
        def _(sp):
            load_units(sp, k, k.next_unit, HX, 2)

        @block.gpsimd
        def _(pool):
            split_units(pool, k, HX, (3, 6), norm)

        @block.tensor
        def _(pe):
            def scores(i, s):
                pe.wait_ge(k.score_read.sem, k.score_read.at(STEPS * i + (s + 1)))
                o = bank(2, s)
                if s < 8:
                    for c in range(2):
                        mm = pe.matmul(o[:, 0:NMEM], q[:, c, s * P:(s + 1) * P], mk[:, c, :], start=(c == 0),
                                       stop=(c == 1))
                else:
                    for b in range(DB):
                        r = 32 * (b // 2)
                        for c in range(2):
                            mm = pe.matmul(o[r:r + 32, 0:NMEM], qz[:, c, b, :], sk[:, c, b, :],
                                           start=(b % 2 == 0 and c == 0), stop=(b % 2 == 1 and c == 1),
                                           tile_position=(0, r))
                mm.then_inc(k.scored.sem, 1)

            def turn_probs(i, s):
                pe.wait_ge(k.normed.sem, k.normed.at(STEPS * i + (s + 1)))
                if s >= 2:
                    pe.wait_ge(k.pt_ready.sem, k.pt_ready.at(STEPS * i + (s - 1)))
                for j in range(2):
                    mm = pe.transpose(bank(4, s)[:, j * P:(j + 1) * P], sc[:, s % 2, j * P:(j + 1) * P], k.ident[:, :])
                mm.then_inc(k.turned.sem, 1)

            def values(i, s):
                pe.wait_ge(k.pt_ready.sem, k.pt_ready.at(STEPS * i + (s + 1)))
                if s >= 2:
                    pe.wait_ge(k.o_read.sem, k.o_read.at(STEPS * i + (s - 1)))
                o = bank(6, s)
                for c in range(2):
                    if s < 8:
                        for j in range(2):
                            mm = pe.matmul(o[:, c * P:(c + 1) * P], mv[:, c, j, :], pt[:, s % 2, j, :],
                                           start=(j == 0), stop=(j == 1))
                        continue
                    for b in range(DB):
                        for j in range(2):
                            mm = pe.matmul(o[:, c * P + DS * b:c * P + DS * (b + 1)],
                                           sv[b // 4][:, b % 4, j, c * P:(c + 1) * P], pt[:, s % 2, j, DS * b:DS * (b + 1)],
                                           start=(j == 0), stop=(j == 1))
                mm.then_inc(k.valued.sem, 1)

            norm.tensor(pe)
            with pe.Fori(0, HX) as i:
                for g in range(6):
                    if g < 3:
                        pe.wait_ge(norm.s.nsplit[0].sem, norm.s.nsplit[0].at(g + 1))
                        pe.wait_ge(norm.s.nsplit[1].sem, norm.s.nsplit[1].at(g + 1))
                    if g % 3 == 0:
                        pe.wait_ge(k.unit_split.sem, k.unit_split.at(2 * i + (g // 3 + 1)))
                    pe.wait_ge(k.evacuated.sem, k.evacuated.at(6 * i + (g + 1)))
                    s = g // 3
                    tiles = [(k.w_hi[s][:, c * P:(c + 1) * P], k.w_lo[s][:, c * P:(c + 1) * P], xh[:, c, :], xl[:, c, :])
                             for c in range(KD)]
                    product(pe, k.ps[g % 2][:, 0:THIRD], tiles, g % 3 * THIRD, (g % 3 + 1) * THIRD)\
                        .then_inc(k.dense_done.sem, 1)
                pe.wait_ge(k.evacuated.sem, k.evacuated.at(6 * i + 8))
                pe.wait_ge(k.a_loaded.sem, k.a_loaded.at(16 * LOADS * i + 16 * LOADS))
                pe.wait_ge(k.qbd_ready.sem, k.qbd_ready.at(i + 1))
                for s in range(STEPS + 2):
                    if s < STEPS:
                        scores(i, s)
                    if s >= 2:
                        values(i, s - 2)
                    if 1 <= s <= STEPS:
                        turn_probs(i, s - 1)

        @block.scalar
        def _(act):
            norm.scalar(act)
            with act.Fori(0, HX) as i:
                act.wait_ge(k.valued.sem, k.valued.at(STEPS * i + 1))
                for dst, src in ((mk[:], k.mem_out[bass.ds(2 * i, 2)].rearrange("c p m -> p c m")),
                                 (mv[:].rearrange("p c j d -> p c (j d)"),
                                  k.mem_turned[bass.ds(2 * i + 8, 2)].rearrange("c p m -> p c m")),
                                 (sv[0][:, 0:4], k.mem_v[i][:, 0:4])):
                    act.dma_start(dst, src).then_inc(k.a_loaded.sem, 16)
                for g in range(6):
                    act.wait_ge(k.dense_done.sem, k.dense_done.at(6 * i + (g + 1)))
                    act.activation(q[:, g // 3, g % 3 * THIRD:(g % 3 + 1) * THIRD], k.ps[g % 2][:, 0:THIRD], ACT.Copy,
                                   scale=DHX ** -0.5).then_inc(k.evacuated.sem, 1)
                    if g == 3:
                        for dst, src in ((sk[:, 0], k.mem_k[i][:, 0]), (sk[:, 1], k.mem_k[i][:, 1]),
                                         (sv[1][:, 0:2], k.mem_v[i][:, 4:6]), (sv[1][:, 2:4], k.mem_v[i][:, 6:8])):
                            act.dma_start(dst, src).then_inc(k.a_loaded.sem, 16)

                def exps(s):
                    act.wait_ge(k.maxed.sem, k.maxed.at(STEPS * i + (s + 1)))
                    if s >= 2:
                        act.wait_ge(k.turned.sem, k.turned.at(STEPS * i + (s - 1)))
                    b = s % 2
                    act.activation(sc[:, b, :], bank(2, s)[:, 0:NMEM], ACT.Exp, bias=nmax[:, b:b + 1],
                                   accum_out=rsum[:, b:b + 1]).then_inc(k.score_read.sem, 1)

                def copy_turned(s):
                    act.wait_ge(k.turned.sem, k.turned.at(STEPS * i + (s + 1)))
                    if s >= 2:
                        act.wait_ge(k.valued.sem, k.valued.at(STEPS * i + (s - 1 + 1)))
                    act.activation(pt[:, s % 2].rearrange("p j c -> p (j c)"), bank(4, s)[:, 0:NMEM], ACT.Copy)\
                        .then_inc(k.pt_ready.sem, 1)

                def copy_o(s):
                    act.wait_ge(k.valued.sem, k.valued.at(STEPS * i + (s + 1 + 1)))
                    if s == 0:
                        act.wait_ge(k.ya_stored.sem, k.ya_stored.at(16 * i + 16))
                    act.activation(oc[:, :, s * P:(s + 1) * P], bank(6, s)[:, 0:2 * P].rearrange("p (c t) -> p c t", c=2),
                                   ACT.Copy).then_inc(k.o_read.sem, 1)

                for s in range(STEPS + 3):
                    if s < STEPS:
                        exps(s)
                    if 1 <= s <= STEPS:
                        copy_turned(s - 1)
                    if s >= 3:
                        copy_o(s - 3)
                act.wait_ge(k.o_read.sem, k.o_read.at(STEPS * i + STEPS))
                act.dma_start(k.o_dram[bass.ds(2 * i, 2)].rearrange("c p t -> p c t"), oc[:]).then_inc(k.ya_stored.sem, 16)
            act.wait_ge(k.ya_stored.sem, k.ya_stored.at(16 * HX + 16))

        @block.vector
        def _(dve):
            norm.vector(dve)
            dve.memset(qz[:], 0.0).then_inc(k.qbd_zero.sem, 1)
            dve.wait_ge(k.qbd_zero.sem, k.qbd_zero.at(1))
            with dve.Fori(0, HX) as i:
                dve.wait_ge(k.evacuated.sem, k.evacuated.at(6 * i + 8))
                for c in range(2):
                    qs = q[:, c, SEQ:T].rearrange("p (b w c) -> p w b c", w=2, c=DS)
                    for odd in range(2):
                        m = dve.tensor_copy(qz[:, c].rearrange("p (b w) c -> p w b c", w=2)[:, odd, :,
                                                                                              DS * odd:DS * (odd + 1)],
                                            qs[:, odd])
                m.then_inc(k.qbd_ready.sem, 1)

                def logits(s):
                    dve.wait_ge(k.scored.sem, k.scored.at(STEPS * i + (s + 1)))
                    if s >= 2:
                        dve.wait_ge(k.score_read.sem, k.score_read.at(STEPS * i + (s - 1 + 2)))
                    dve.tensor_reduce(nmax[:, s % 2:s % 2 + 1], bank(2, s)[:, 0:NMEM], AX_X, ALU.max, negate=True)\
                        .then_inc(k.maxed.sem, 1)

                def normalise(s):
                    b = s % 2
                    dve.wait_ge(k.score_read.sem, k.score_read.at(STEPS * i + (s + 1 + 2)))
                    dve.reciprocal(rinv[:, b:b + 1], rsum[:, b:b + 1]).then_inc(k.inverted.sem, 1)
                    dve.wait_ge(k.inverted.sem, k.inverted.at(STEPS * i + (s + 1)))
                    dve.tensor_scalar(sc[:, b, :], sc[:, b, :], rinv[:, b:b + 1], None, ALU.mult)\
                        .then_inc(k.normed.sem, 1)

                for s in range(STEPS + 1):
                    if s < STEPS:
                        logits(s)
                    if s >= 1:
                        normalise(s - 1)

    units_done(k, HX, 2)
    norm.done()
    k.qbd_zero.base += 1
    for sig, n in ((k.dense_done, 6), (k.evacuated, 6), (k.scored, STEPS), (k.maxed, STEPS), (k.score_read, STEPS),
                   (k.inverted, STEPS), (k.normed, STEPS), (k.turned, STEPS), (k.pt_ready, STEPS), (k.valued, STEPS),
                   (k.o_read, STEPS), (k.a_loaded, 16 * LOADS), (k.ya_stored, 16), (k.qbd_ready, 1)):
        sig.base += n * HX




OUTPUTS = {"y_out": (KD, P, T), "a_k_out": (4, P, T), "a_v_out": (4, P, T), "conv_out": (HB, P, 3, (DB + 1) * (CW - 1)),
           "p_s_out": (HB, P, P), "s_s_out": (HB, P, DB, P), "mem_out": (2 * KD, P, NMEM)}
SCRATCH = {"bias_dram": (P, HA * NBIAS + 256), "ya_dram": (4, P, T), "yb_dram": (4, P, T), "x_dram": (KD, P, T),
           "proj_dram": (4 * HB, P, PADDED), "gate_dram": (2 * KD, P, T), "mem_turned": (2 * KD, P, NMEM), "o_dram": (KD, P, T)}


def by_frame(a):
    return a.rearrange("c p t -> p c t")


def hybrid_layer(nc, io):
    with ExitStack() as ctx:
        k = Core(nc, ctx)
        k.units, k.xt, k.memt, k.gains_dram, k.ident_dram = (io[n] for n in ("units", "xt", "memt", "gains_dram",
                                                                             "ident_dram"))
        k.table, k.k_cache, k.v_cache = io["table"], io["k_cache"], io["v_cache"]
        k.b_consts, k.w_beta_decay, k.a_log, k.dt_bias = (io[n] for n in ("b_consts", "w_beta_decay", "a_log", "dt_bias"))
        k.b_gain, k.conv_state, k.conv_w, k.state_s = io["b_gain"], io["conv_state"], io["conv_w"], io["state_s"]
        k.mem_k, k.mem_v = io["mem_k"], io["mem_v"]
        k.y_out, k.a_k_out, k.a_v_out, k.conv_out = io["y_out"], io["a_k_out"], io["a_v_out"], io["conv_out"]
        k.p_s_out, k.s_s_out, k.mem_out = io["p_s_out"], io["s_s_out"], io["mem_out"]
        k.bias_dram, k.ya_dram, k.yb_dram, k.x_dram = io["bias_dram"], io["ya_dram"], io["yb_dram"], io["x_dram"]
        k.proj_dram = io["proj_dram"]
        k.gate_dram, k.mem_turned, k.o_dram = io["gate_dram"], io["mem_turned"], io["o_dram"]
        k.bias_pitch = HA * NBIAS + 256
        k.bias_dram_flat = k.bias_dram.rearrange("p m -> (p m)")
        big = KD * T * 4
        r1 = k.arena
        r2 = r1 + 2 * big

        def split_pair(name, at):
            return (nc.alloc_sbuf_tensor_at(name + "_hi", [P, KD, T], F32R, offset=at),
                    nc.alloc_sbuf_tensor_at(name + "_lo", [P, KD, T], F32R, offset=at + big))

        xh1, xl1 = split_pair("x1", r1)
        xh2, xl2 = split_pair("x2", r2)
        x_early = nc.alloc_sbuf_tensor_at("x_early", [P, KD, T], F32, offset=r2)
        x_late = nc.alloc_sbuf_tensor_at("x_late", [P, KD, T], F32, offset=r1)
        mem = nc.alloc_sbuf_tensor_at("mem", [P, KD, NMEM], F32, offset=r2 + big)
        mh, ml = (nc.alloc_sbuf_tensor_at(n, [P, KD, NMEM], F32R, offset=r2 + big + 4 * KD * NMEM * (1 + j))
                  for j, n in enumerate(("mem_hi", "mem_lo")))

        def gain(n):
            return k.gains[:, n * KD:(n + 1) * KD]

        with nc.Block() as block:
            @block.sync
            def _(sp):
                for dst, src in ((mem[:], by_frame(k.memt)), (k.gains[:], k.gains_dram), (k.ident[:], k.ident_dram)):
                    sp.dma_start(dst, src).then_inc(k.loaded.sem, 16)
                sp.dma_start(x_early[:], by_frame(k.xt)).then_inc(k.x_loaded.sem, 16)
                sp.wait_ge(k.loaded.sem, k.loaded.at(48))
                for s, n in k.tokens:
                    sp.sem_inc(s.sem, n)

            @block.vector
            def _(dve):
                dve.memset(k.ones[:, :], 1.0)
                dve.memset(k.eps[:, :], EPS)
                dve.memset(k.zero[:, :], 0.0)

        k.loaded.base += 48

        def norm(name, x, n, hi, lo, squares_at, work, rinv_at=None, out=None):
            return Norm(nc, k, k.norm, name, x, gain(n), hi, lo, work, T, THIRD, squares_at, rinv_at, out)

        work = r2 + big + 12 * KD * NMEM
        memory_phase(nc, k, Norm(nc, k, k.memory_norm, "nm", mem, gain(4), mh, ml, work + 16 * NMEM, NMEM, NMEM,
                                   r2 + big + 4 * KD * NMEM),
                     norm("n1", x_early, 0, xh1, xl1, r1, work + 16 * NMEM), mh, ml, work)
        work = r2 + big
        ffn_phase(nc, k, "f1", None, x_early, xh1, xl1, work, BiasRows(nc, k, work + 23 * T))
        attention_phase(nc, k, lambda work: norm("n2", x_early, 1, xh1, xl1, r1, work), xh1, xl1, x_early, k.x_dram, r2)
        delta_phase(nc, k, xh1, xl1, r2)
        merge_phase(nc, k, [(0, by_frame(k.ya_dram)), (4, by_frame(k.yb_dram))], xh1, xl1, xh2, xl2, r2 + 2 * big,
                    (r2, r2 + big))
        residual_phase(nc, k, x_late, xh2, xl2, x_from=k.x_dram)
        work = r1 + big
        cross_phase(nc, k, lambda work, rinv_at: norm("n3", x_late, 2, xh2, xl2, r2, work, rinv_at), xh2, xl2, work,
                    r2 + 2 * big)
        o = by_frame(k.o_dram)
        residual_phase(nc, k, x_late, xh2, xl2, sources=[(0, o[:, 0:4]), (4, o[:, 4:8])], work=work)
        ffn_phase(nc, k, "f2", norm("n4", x_late, 3, xh2, xl2, r2, r2 + 2 * big, work + 24 * T), x_late, xh2, xl2, work)
        last_norm_phase(nc, k, norm("n5", x_late, 5, None, None, r2, work, out=by_frame(k.y_out)))



def stationary(w):
    kk, m = w.shape
    return w.reshape(kk // P, P, m // P, P).transpose(2, 1, 0, 3).reshape(m // P, P, kk)


def weight_units(a):
    units = list(stationary(a["xattn_wk"])) + list(stationary(a["xattn_wv"]))

    def ffn(n):
        g, u, d = stationary(a[n + "_w_gate"]), stationary(a[n + "_w_up"]), a[n + "_w_down"].reshape(NFF, P, D)
        for i in range(0, NFF, 2):
            units.extend([g[i], u[i], g[i + 1], u[i + 1], d[i], d[i + 1]])

    ffn("ffn1")
    w_in = a["w_in"]
    wa, wb = 3 * HA * DHA, 4 * HB * DHB
    mixer_a = stationary(w_in[:, 0:wa])
    mixer_b = stationary(w_in[:, wa:wa + wb])
    for p in range(4):
        units.extend([mixer_a[4 * j + p] for j in range(3)] + [mixer_b[4 * j + p] for j in range(4)])
    units.extend(stationary(w_in[:, wa + wb + 2 * HB:]))
    units.extend(np.concatenate(pair, axis=1) for pair in zip(stationary(a["w_branch_a"]), stationary(a["w_branch_b"])))
    for n in ("w_mix_out", "xattn_wq", "xattn_wo"):
        units.extend(stationary(a[n]))
    ffn("ffn2")
    return np.stack(units)


def kernel(**inputs):
    import concourse.bacc as bacc
    from concourse.bass_utils import run_bass_kernel_spmd as run

    def features(x):
        return x.reshape(-1, D).T.reshape(KD, P, -1)

    a = {n: np.asarray(v) for n, v in inputs.items()}
    for n in a:
        if n not in ("x_prompt", "x_sample", "mem_prompt", "final_norm"):
            a[n] = a[n][0]
    wa, wb = 3 * HA * DHA, 4 * HB * DHB
    arrays = {
        "units": weight_units(a),
        "xt": np.concatenate([features(a["x_prompt"]), features(a["x_sample"])], axis=2),
        "memt": features(a["mem_prompt"]),
        "gains_dram": np.concatenate([a[n].reshape(KD, P).T for n in ("ffn1_norm", "mix_norm", "xattn_norm",
                                                                      "ffn2_norm", "mem_norm", "final_norm")], axis=1),
        "ident_dram": np.eye(P, dtype=np.float32),
        "table": a["a_rel_bias"][:, ::-1],
        "k_cache": a["cache_a_k"].reshape(DB, REACH, 4, P).transpose(2, 3, 0, 1),
        "v_cache": a["cache_a_v"].reshape(DB, 4, P, 4, P).transpose(3, 2, 0, 1, 4),
        "b_consts": delta_constants(),
        "w_beta_decay": a["w_in"][:, wa + wb:wa + wb + 2 * HB].reshape(KD, P, 2 * HB).transpose(1, 0, 2),
        "a_log": a["b_a_log"].reshape(HB), "dt_bias": a["b_dt_bias"].reshape(HB),
        "b_gain": a["b_out_norm"].reshape(P, 1),
        "conv_state": a["state_b_conv"].reshape(DB, CW - 1, 3, HB, P).transpose(3, 4, 2, 0, 1),
        "conv_w": a["b_conv_w"].reshape(CW, 3, HB, P).transpose(2, 3, 1, 0),
        "state_s": a["state_b_s"].transpose(1, 2, 0, 3),
        "mem_k": a["cache_mem_k"].reshape(DB, NMEM, HX, 2, P).transpose(2, 4, 3, 0, 1),
        "mem_v": a["cache_mem_v"].reshape(DB, 2, P, HX, DHX).transpose(3, 2, 0, 1, 4),
    }
    arrays = {n: np.ascontiguousarray(v) for n, v in arrays.items()}
    nc = bacc.Bacc("TRN2", target_bir_lowering=False, num_devices=1)
    io = {n: nc.dram_tensor(n, v.shape, F32, kind="ExternalInput").ap() for n, v in arrays.items()}
    for n, shape in OUTPUTS.items():
        io[n] = nc.dram_tensor(n, shape, F32, kind="ExternalOutput").ap()
    for n, shape in SCRATCH.items():
        io[n] = nc.dram_tensor(n, shape, F32, kind="Internal").ap()
    hybrid_layer(nc, io)
    r = run(nc, [arrays], core_ids=[0]).results[0]

    def frames(o):
        o = o.reshape(-1, T).T
        return o[:SEQ], o[SEQ:]

    yp, ys = frames(r["y_out"])
    kp, ks = frames(r["a_k_out"])
    vp, vs = frames(r["a_v_out"])
    conv = r["conv_out"].reshape(HB, P, 3, DB + 1, CW - 1).transpose(3, 4, 2, 0, 1).reshape(DB + 1, CW - 1, -1)
    mk, mv = (r["mem_out"][n * KD:(n + 1) * KD].reshape(D, NMEM).T.reshape(1, 1, NMEM, HX, DHX) for n in range(2))
    keep = min(REACH, SEQ)
    return (yp.reshape(1, SEQ, D), ys.reshape(DB, DS, D),
            kp[SEQ - keep:].reshape(1, 1, keep, HA, DHA), vp[SEQ - keep:].reshape(1, 1, keep, HA, DHA),
            conv[None, 0:1], r["p_s_out"][None, None], mk, mv,
            ks.reshape(1, DB, DS, HA, DHA), vs.reshape(1, DB, DS, HA, DHA),
            conv[None, 1:], r["s_s_out"].transpose(2, 0, 1, 3)[None])
```

```python
from contextlib import ExitStack

import numpy as np

import concourse.bass as bass
from concourse import mybir

F32 = mybir.dt.float32
F32R = mybir.dt.float32r
ALU = mybir.AluOpType
ACT = mybir.ActivationFunctionType
AX_X = mybir.AxisListType.X

P = 128
D = 1024
KD = D // P
SEQ = 1024
DB, DS = 8, 16
T = SEQ + DB * DS
NT_TILES = T // P
THIRD = T // 3
FF = 2816
NFF = FF // P
HA, DHA, REACH, REL = 8, 64, 512, 128
HB, DHB, CW = 4, 128, 4
HX, DHX, NMEM = 4, 256, 256
WIN = REACH + P
NBIAS = WIN + P
PADP, PADS = SEQ + CW - 1, DS + CW - 1
PADDED = PADP + DB * PADS
NEG = -1e30
EPS = 1e-6
SBUF_END = 229376
RING = 3
NPS = 4


class Counter:

    def __init__(self, nc, ctx, name):
        self.sem = ctx.enter_context(nc.semaphore(name))
        self.base = 0

    def at(self, k):
        return self.base + k



def slot(j, turn):
    return 1 if turn % RING == 1 and j == turn - 1 else j % RING


def sharing(j, turn):
    return [u for u in range(turn) if slot(u, turn) == slot(j, turn)]


def last_use(j, turn):
    same = sharing(j, turn)
    at = same.index(j)
    return (0, same[at - 1]) if at else (1, same[-1])


def load_units(sp, k, first, turns, turn, at_turn=None, then=None):
    def one(i, j):
        back, last = last_use(j, turn)
        if not (isinstance(i, int) and i < back):
            sp.wait_ge(k.unit_split.sem, k.unit_split.at(turn * i + (last + 1 - turn * back)))
        sp.dma_start(k.w_raw[slot(j, turn)][:, :], k.units[turn * i + (first + j)])\
            .then_inc(k.raw_landed[slot(j, turn)].sem, 16)
    for j in range(turn):
        if j >= k.ahead:
            one(0, j)
        if at_turn and j == 0:
            at_turn(0)
        if then and j == RING - 1:
            then()
    if turns > 1:
        with sp.Fori(1, turns) as i:
            if at_turn:
                at_turn(i)
            for j in range(turn):
                one(i, j)
    k.ahead = units_ahead(k)
    if k.ahead:
        sp.wait_ge(k.unit_split.sem, k.unit_split.at(turns * turn))
    for j in range(k.ahead):
        sp.dma_start(k.w_raw[j][:, :], k.units[first + turns * turn + j]).then_inc(k.raw_landed[j].sem, 16)


def units_ahead(k):
    return min(RING, k.turn_sizes[k.phase + 1]) if k.phase + 1 < len(k.turn_sizes) else 0


def split_units(pool, k, turns, jobs, norm=None):
    turn = len(jobs)

    def one(i, j):
        s, same = slot(j, turn), sharing(j, turn)
        back, last = last_use(j, turn)
        if not (isinstance(i, int) and i < back):
            pool.wait_ge(k.dense_done.sem, k.dense_done.at(jobs[-1] * i + (jobs[last] - jobs[-1] * back)))
        pool.wait_ge(k.raw_landed[s].sem, k.raw_landed[s].at(16 * len(same) * i + 16 * (same.index(j) + 1)))
        pool.tensor_tensor(k.w_hi[s][:, :], k.w_raw[s][:, :], k.zero[:, 0:1].to_broadcast([P, D]), ALU.add)\
            .then_inc(k.unit_hi.sem, 1)
        pool.wait_ge(k.unit_hi.sem, k.unit_hi.at(turn * i + (j + 1)))
        pool.tensor_tensor(k.w_lo[s][:, :], k.w_raw[s][:, :], k.w_hi[s][:, :].bitcast(F32),
                           ALU.subtract).then_inc(k.unit_split.sem, 1)

    for j in range(turn):
        if j or not k.split_ahead:
            one(0, j)
        if norm and j == 1:
            norm.gpsimd(pool)
    if turns > 1:
        with pool.Fori(1, turns) as i:
            for j in range(turn):
                one(i, j)
    k.split_ahead = units_ahead(k) > 0
    if k.split_ahead:
        users = sharing(0, turn)
        pool.wait_ge(k.dense_done.sem, k.dense_done.at(jobs[-1] * (turns - 1) + jobs[users[-1]]))
        pool.wait_ge(k.raw_landed[0].sem, k.raw_landed[0].at(16 * len(users) * turns + 16))
        pool.tensor_tensor(k.w_hi[0][:, :], k.w_raw[0][:, :], k.zero[:, 0:1].to_broadcast([P, D]), ALU.add)\
            .then_inc(k.unit_hi.sem, 1)
        pool.wait_ge(k.unit_hi.sem, k.unit_hi.at(turns * turn + 1))
        pool.tensor_tensor(k.w_lo[0][:, :], k.w_raw[0][:, :], k.w_hi[0][:, :].bitcast(F32),
                           ALU.subtract).then_inc(k.unit_split.sem, 1)


def product(pe, out, tiles, n0, n1):
    last = len(tiles) - 1
    for part in range(3):
        for i, (wh, wl, xh, xl) in enumerate(tiles):
            mm = pe.matmul(out, wl if part == 2 else wh, (xl if part == 1 else xh)[:, n0:n1],
                           start=(part == 0 and i == 0), stop=(part == 2 and i == last))
    return mm


def units_done(k, turns, turn):
    for u in range(turn):
        k.raw_landed[slot(u, turn)].base += 16 * turns
    for sig in (k.unit_hi, k.unit_split):
        sig.base += turns * turn
    k.next_unit += turns * turn
    k.phase += 1


class Filler:
    PIECES = 3 * KD

    def __init__(self, main, units, plan, ahead=0):
        self.main, self.units, self.plan, self.ahead = main, units, plan, ahead
        self.count = 3 * units
        assert sum(plan) == self.count * self.PIECES, sum(plan)

    def jobs(self):
        return tuple(3 * (u + 1) for u in range(self.main + self.units))

    def products(self, k, pe, i, place, xh, xl):
        turn, per_turn = self.main + self.units, 3 * (self.main + self.units)
        first = sum(self.plan[:place])
        for m in range(first, first + self.plan[place]):
            g, r = 3 * self.main + m // self.PIECES, m % self.PIECES
            u, n, part, c = g // 3, g % 3, r // KD, r % KD
            if r == 0:
                if n == 0:
                    pe.wait_ge(k.unit_split.sem, k.unit_split.at(turn * i + (turn * self.ahead + u + 1)))
                pe.wait_ge(k.evacuated.sem, k.evacuated.at(per_turn * i + (per_turn * self.ahead + g + 1)))
            w = (k.w_lo if part == 2 else k.w_hi)[slot(u, turn)]
            mm = pe.matmul(k.ps[g % 2][:, 0:THIRD], w[:, c * P:(c + 1) * P],
                           (xl if part == 1 else xh)[:, c, n * THIRD:(n + 1) * THIRD], start=(r == 0),
                           stop=(r == self.PIECES - 1))
            if r == self.PIECES - 1:
                mm.then_inc(k.dense_done.sem, 1)

    def finished(self, place, places=1):
        a = sum(self.plan[:place])
        b = sum(self.plan[:place + places])
        return [3 * self.main + g for g in range(self.count) if a < (g + 1) * self.PIECES <= b]


def ffn_phase(nc, k, name, norm, x, xh, xl, work, bias_rows=None):
    turns = NFF // 2
    h_hi = nc.alloc_sbuf_tensor_at(name + "_h_hi", [P, 2, T], F32R, offset=work)
    h_lo = nc.alloc_sbuf_tensor_at(name + "_h_lo", [P, 2, T], F32R, offset=work + 8 * T)
    gate = nc.alloc_sbuf_tensor_at(name + "_gate", [P, 3, THIRD], F32, offset=work + 16 * T)
    hid = nc.alloc_sbuf_tensor_at(name + "_hid", [P, 2, THIRD], F32, offset=work + 20 * T)
    JOBS = 36

    with nc.Block() as block:
        @block.sync
        def _(sp):
            load_units(sp, k, k.next_unit, turns, 6)

        @block.gpsimd
        def _(pool):
            split_units(pool, k, turns, (3, 6, 9, 12, 36, 36), norm)

        @block.tensor
        def _(pe):
            if norm:
                norm.tensor(pe)
            with pe.Fori(0, turns) as i:
                g = 0
                for u in range(4):
                    pe.wait_ge(k.unit_split.sem, k.unit_split.at(6 * i + (u + 1)))
                    for n in range(3):
                        if norm and u == 0:
                            pe.wait_ge(norm.s.nsplit[0].sem, norm.s.nsplit[0].at(n + 1))
                            pe.wait_ge(norm.s.nsplit[1].sem, norm.s.nsplit[1].at(n + 1))
                        if g < NPS:
                            pe.wait_ge(k.x_added.sem, k.x_added.at(24 * i + (g + 1)))
                        elif (g - NPS) % 6 < 3:
                            pe.wait_ge(k.gate_ready.sem, k.gate_ready.at(6 * i + ((g - NPS) // 6 * 3 + (g - NPS) % 6 + 1)))
                        else:
                            pe.wait_ge(k.gate_used.sem, k.gate_used.at(6 * i + ((g - NPS) // 6 * 3 + (g - NPS) % 6 - 3 + 1 + 3)))
                        tiles = [(k.w_hi[u % RING][:, c * P:(c + 1) * P], k.w_lo[u % RING][:, c * P:(c + 1) * P],
                                  xh[:, c, :], xl[:, c, :]) for c in range(KD)]
                        mm = product(pe, k.ps[g % NPS][:, 0:THIRD], tiles, n * THIRD, (n + 1) * THIRD)
                        mm.then_inc(k.dense_done.sem, 1)
                        g += 1
                pe.wait_ge(k.unit_split.sem, k.unit_split.at(6 * i + 6))
                for n in range(3):
                    pe.wait_ge(k.h_ready.sem, k.h_ready.at(6 * i + (3 + n + 1)))
                    for d in range(KD):
                        if g >= 12 + NPS:
                            pe.wait_ge(k.x_added.sem, k.x_added.at(24 * i + (g - 12 + 1)))
                        elif g == 12:
                            pe.wait_ge(k.gate_ready.sem, k.gate_ready.at(6 * i + 6))
                        else:
                            pe.wait_ge(k.gate_used.sem, k.gate_used.at(6 * i + (g - 13 + 4 + 3)))
                        tiles = [(k.w_hi[1 + c][:, d * P:(d + 1) * P], k.w_lo[1 + c][:, d * P:(d + 1) * P],
                                  h_hi[:, c, :], h_lo[:, c, :]) for c in range(2)]
                        mm = product(pe, k.ps[g % NPS][:, 0:THIRD], tiles, n * THIRD, (n + 1) * THIRD)
                        mm.then_inc(k.dense_done.sem, 1)
                        g += 1

        @block.scalar
        def _(act):
            if bias_rows:
                bias_rows.load(act)
            if norm:
                norm.scalar(act)
            if bias_rows:
                act.wait_ge(k.unit_split.sem, k.unit_split.at(3))
                bias_rows.store(act)
            with act.Fori(0, turns) as i:
                for c in range(2):
                    for n in range(3):
                        g = 6 * c + n
                        act.wait_ge(k.dense_done.sem, k.dense_done.at(JOBS * i + (g + 1)))
                        act.wait_ge(k.gate_used.sem, k.gate_used.at(6 * i + (3 * c + n + 1)))
                        act.activation(gate[:, n, :], k.ps[g % NPS][:, 0:THIRD], ACT.Silu)\
                            .then_inc(k.gate_ready.sem, 1)
            if bias_rows:
                bias_rows.stored(act)

        @block.vector
        def _(dve):
            if norm:
                norm.vector(dve)
            if bias_rows:
                bias_rows.spread(dve)
            with dve.Fori(0, turns) as i:
                for c in range(2):
                    for n in range(3):
                        g = 6 * c + 3 + n
                        j = 3 * c + n
                        cols = slice(n * THIRD, (n + 1) * THIRD)
                        dve.wait_ge(k.dense_done.sem, k.dense_done.at(JOBS * i + (g + 1)))
                        dve.wait_ge(k.gate_ready.sem, k.gate_ready.at(6 * i + (j + 1)))
                        up = k.ps[g % NPS][:, 0:THIRD]
                        dve.tensor_tensor(hid[:, j % 2, :], up, gate[:, n, :], ALU.mult).then_inc(k.hid_made.sem, 1)
                        dve.tensor_tensor(h_hi[:, c, cols], up, gate[:, n, :], ALU.mult)\
                            .then_inc(k.gate_used.sem, 1)
                        dve.wait_ge(k.hid_made.sem, k.hid_made.at(6 * i + (j + 1)))
                        dve.wait_ge(k.gate_used.sem, k.gate_used.at(6 * i + (j + 1 + 3)))
                        dve.tensor_tensor(h_lo[:, c, cols], hid[:, j % 2, :], h_hi[:, c, cols].bitcast(F32),
                                          ALU.subtract).then_inc(k.h_ready.sem, 1)
                g = 12
                for n in range(3):
                    for d in range(KD):
                        dve.wait_ge(k.dense_done.sem, k.dense_done.at(JOBS * i + (g + 1)))
                        xs = x[:, d, n * THIRD:(n + 1) * THIRD]
                        dve.scalar_tensor_tensor(out=xs, in0=k.ps[g % NPS][:, 0:THIRD], scalar=0.5, in1=xs,
                                                 op0=ALU.mult, op1=ALU.add).then_inc(k.x_added.sem, 1)
                        g += 1

    units_done(k, turns, 6)
    if norm:
        norm.done()
    k.dense_done.base += JOBS * turns
    k.x_added.base += 24 * turns
    for sig in (k.gate_used, k.gate_ready, k.hid_made, k.h_ready):
        sig.base += 6 * turns


class NormSignals:

    def __init__(self, k, name):
        self.nsq, self.ntotal = k.counter(name + "_squared"), k.counter(name + "_total")
        self.nln, self.nrinv = k.counter(name + "_ln"), k.counter(name + "_rinv")
        self.nscaled, self.nhi = k.counter(name + "_scaled"), k.counter(name + "_upper")
        self.nsplit = [k.counter(f"{name}_lower{h}") for h in range(2)]
        self.nout = [k.counter(f"{name}_stored{b}") for b in range(2)]


class Norm:

    def __init__(self, nc, k, signals, name, x, gains, hi, lo, work, width, cols, squares_at,
                 rinv_at=None, out=None):
        self.k, self.s, self.x, self.gains, self.hi, self.lo, self.out = k, signals, x, gains, hi, lo, out
        self.nb, self.width = width // cols, cols
        self.tmp = nc.alloc_sbuf_tensor_at(name + "_tmp", [P, 2, KD, cols], F32, offset=work)
        self.rinv = nc.alloc_sbuf_tensor_at(name + "_rinv", [P, 2, cols], F32,
                                            offset=work + 8 * KD * cols if rinv_at is None else rinv_at)
        self.squares = nc.alloc_sbuf_tensor_at(name + "_squares", [P, KD, width], F32, offset=squares_at)

    def cols(self, n):
        return slice(n * self.width, (n + 1) * self.width)

    def square(self, act, n):
        s = self.s
        for h in range(2):
            c = slice(4 * h, 4 * h + 4)
            act.activation(self.squares[:, c, self.cols(n)], self.x[:, c, self.cols(n)], ACT.Square)\
                .then_inc(s.nsq.sem, 1)

    def sums(self, pe, n):
        k, s = self.k, self.s
        for c in range(KD):
            if c % 4 == 0:
                pe.wait_ge(s.nsq.sem, s.nsq.at(2 * n + c // 4 + 1))
            mm = pe.matmul(k.ps[4 + n][:, 0:self.width], k.ones[:, :], self.squares[:, c, self.cols(n)],
                           start=(c == 0), stop=(c == KD - 1))
        mm.then_inc(s.ntotal.sem, 1)

    def root(self, act, n):
        k, s = self.k, self.s
        act.wait_ge(s.ntotal.sem, s.ntotal.at(n + 1))
        if n >= 2:
            act.wait_ge(s.nscaled.sem, s.nscaled.at(2 * (n - 1)))
        r = self.rinv[:, n % 2, :]
        act.activation(r, k.ps[4 + n][:, 0:self.width], ACT.Ln, bias=k.eps[:, 0:1], scale=1.0 / D)\
            .then_inc(s.nln.sem, 1)
        act.wait_ge(s.nln.sem, s.nln.at(n + 1))
        act.activation(r, r, ACT.Exp, scale=-0.5).then_inc(s.nrinv.sem, 1)

    def scale(self, dve, n):
        s, b = self.s, n % 2
        dve.wait_ge(s.nrinv.sem, s.nrinv.at(n + 1))
        if n >= 2 and self.out is None:
            dve.wait_ge(s.nsplit[0].sem, s.nsplit[0].at(n - 1))
            dve.wait_ge(s.nsplit[1].sem, s.nsplit[1].at(n - 1))
        elif n >= 2:
            dve.wait_ge(s.nout[b].sem, s.nout[b].at(16 * (n // 2)))
        for c in range(KD):
            mm = dve.scalar_tensor_tensor(out=self.tmp[:, b, c, :], in0=self.x[:, c, self.cols(n)],
                                          scalar=self.gains[:, c:c + 1], in1=self.rinv[:, b, :], op0=ALU.mult, op1=ALU.mult)
            if c % 4 == 3:
                mm.then_inc(s.nscaled.sem, 1)

    def upper(self, act, n):
        s = self.s
        for h in range(2):
            c = slice(4 * h, 4 * h + 4)
            act.wait_ge(s.nscaled.sem, s.nscaled.at(2 * n + h + 1))
            act.activation(self.hi[:, c, self.cols(n)], self.tmp[:, n % 2, c, :], ACT.Copy).then_inc(s.nhi.sem, 1)

    def lower(self, eng, n, h):
        s = self.s
        c = slice(4 * h, 4 * h + 4)
        eng.wait_ge(s.nhi.sem, s.nhi.at(2 * n + h + 1))
        eng.wait_ge(s.nscaled.sem, s.nscaled.at(2 * n + h + 1))
        eng.tensor_tensor(self.lo[:, c, self.cols(n)], self.tmp[:, n % 2, c, :], self.hi[:, c, self.cols(n)].bitcast(F32),
                          ALU.subtract).then_inc(s.nsplit[h].sem, 1)


    def tensor(self, pe):
        for n in range(self.nb):
            self.sums(pe, n)

    def scalar(self, act):
        act.preload_act_table_set("natural_log_exp_and_others")
        for n in range(self.nb):
            self.square(act, n)
        for n in range(self.nb):
            self.root(act, n)
            if self.out is None:
                self.upper(act, n)

    def vector(self, dve, both=False):
        for n in range(self.nb):
            self.scale(dve, n)
            if self.out is None:
                self.lower(dve, n, 0)
                if both:
                    self.lower(dve, n, 1)

    def gpsimd(self, pool):
        for n in range(self.nb):
            self.lower(pool, n, 1)

    def done(self):
        s, nb = self.s, self.nb
        for sig, n in ((s.nsq, 2), (s.ntotal, 1), (s.nln, 1), (s.nrinv, 1), (s.nscaled, 2)):
            sig.base += n * nb
        if self.out is None:
            for sig, n in ((s.nhi, 2), (s.nsplit[0], 1), (s.nsplit[1], 1)):
                sig.base += n * nb
        else:
            for b in range(2):
                s.nout[b].base += 16 * len(range(b, nb, 2))


def last_norm_phase(nc, k, norm):
    with nc.Block() as block:
        @block.tensor
        def _(pe):
            norm.tensor(pe)

        @block.scalar
        def _(act):
            norm.scalar(act)

        @block.vector
        def _(dve):
            norm.vector(dve)

        @block.sync
        def _(sp):
            for n in range(norm.nb):
                sp.wait_ge(norm.s.nscaled.sem, norm.s.nscaled.at(2 * n + 2))
                sp.dma_start(norm.out[:, :, norm.cols(n)], norm.tmp[:, n % 2]).then_inc(norm.s.nout[n % 2].sem, 16)
            for b in range(2):
                sp.wait_ge(norm.s.nout[b].sem, norm.s.nout[b].at(16 * len(range(b, norm.nb, 2))))

    norm.done()


class Core:

    def __init__(self, nc, ctx):
        self.nc, self.ctx, self.tokens, self.next_unit = nc, ctx, [], 0
        self.turn_sizes, self.phase, self.ahead, self.split_ahead = (2 * KD, 6, 7, 4, KD, KD, 2, KD, 6), 0, 0, False
        at = (nc.sbuf_base + 63) // 64 * 64
        self.ones = nc.alloc_sbuf_tensor_at("ones", [P, P], F32, offset=at)
        self.ident = nc.alloc_sbuf_tensor_at("ident", [P, P], F32, offset=at + 512)
        self.eps = nc.alloc_sbuf_tensor_at("eps", [P, 1], F32, offset=at + 1024)
        self.zero = nc.alloc_sbuf_tensor_at("zero", [P, 1], F32, offset=at + 1056)
        self.gains = nc.alloc_sbuf_tensor_at("gains", [P, 6 * KD], F32, offset=at + 1088)
        at += 1088 + 6 * KD * 4
        self.w_raw = [nc.alloc_sbuf_tensor_at(f"w_raw{s}", [P, D], F32, offset=at + 4096 * s) for s in range(RING)]
        self.w_hi = [nc.alloc_sbuf_tensor_at(f"w_hi{s}", [P, D], F32R, offset=at + 4096 * (RING + s))
                     for s in range(RING)]
        self.w_lo = [nc.alloc_sbuf_tensor_at(f"w_lo{s}", [P, D], F32R, offset=at + 4096 * (2 * RING + s))
                     for s in range(RING)]
        self.arena = at + 4096 * 3 * RING
        self.psum = ctx.enter_context(nc.psum_tensor("psum", [P, 8, 512], F32))
        self.ps = [self.psum[:, b, :] for b in range(8)]
        self.raw_landed = [self.counter(f"raw_landed{s}") for s in range(RING)]
        self.unit_hi, self.unit_split = self.counter("unit_hi"), self.counter("unit_split")
        self.dense_done, self.evacuated = self.counter("dense_done"), self.counter("evacuated", 2)
        self.gate_ready, self.gate_used = self.counter("gate_ready"), self.counter("gate_used", 3)
        self.hid_made, self.h_ready = self.counter("hid_made"), self.counter("h_ready")
        self.x_added = self.counter("x_added", NPS)
        self.norm, self.memory_norm = NormSignals(self, "norm"), NormSignals(self, "memory_norm")
        self.merged_hi, self.merged_split = self.counter("merged_hi"), self.counter("merged_split")
        self.x_loaded = self.counter("x_loaded")
        self.loaded = self.counter("loaded")
        self.table_loaded, self.rows_made = self.counter("table_loaded"), self.counter("rows_made")
        self.rows_stored = self.counter("rows_stored")
        self.v_turned, self.vn_ready = self.counter("v_turned"), self.counter("vn_ready")
        self.qbd_zero, self.qbd_ready, self.masked = self.counter("qbd_zero"), self.counter("qbd_ready"), self.counter("masked")
        self.scored, self.biased, self.maxed = self.counter("scored"), self.counter("biased"), self.counter("maxed")
        self.exped, self.inverted, self.normed = self.counter("exped"), self.counter("inverted"), self.counter("normed")
        self.turned, self.pt_ready = self.counter("turned"), self.counter("pt_ready")
        self.valued, self.o_read = self.counter("valued", 1), self.counter("o_read")
        self.a_loaded, self.kv_stored = self.counter("a_loaded"), self.counter("kv_stored", 32)
        self.ya_stored = self.counter("ya_stored", 16)

        self.kv_slot = [self.counter(f"slot_stored{b}", 32) for b in range(2)]
        self.score_read = self.counter("score_read", 2)
        self.merged, self.gated = self.counter("merged", 2), self.counter("gated")
        self.squared = self.counter("squared")
        self.lned = self.counter("lned")
        self.sq_summed = self.counter("sq_summed")
        self.rooted = self.counter("rooted")
        self.per_ready = self.counter("per_ready")
        self.decayed = self.counter("decayed")
        self.scaled = self.counter("scaled")
        self.rows_spread = self.counter("rows_spread")
        self.l2_done = self.counter("l2_done")
        self.grams = self.counter("grams")
        self.kv_turned = self.counter("kv_turned")
        self.y_started = self.counter("y_started")
        self.y_turned = self.counter("y_turned")
        self.x_started = self.counter("x_started")
        self.masked_level = self.counter("masked_level")
        self.p1_ready = self.counter("p1_ready")
        self.p1_done = self.counter("p1_done")
        self.level_done = self.counter("level_done")
        self.corrected = self.counter("corrected")
        self.w_ready = self.counter("w_ready")
        self.u_ready = self.counter("u_ready")
        self.wu_done = self.counter("wu_done")
        self.s_ready = self.counter("s_ready")
        self.ws_done = self.counter("ws_done")
        self.o_copied = self.counter("o_copied")
        self.qg_ready = self.counter("qg_ready")
        self.vw_ready = self.counter("vw_ready")
        self.o_done = self.counter("o_done")
        self.s_loaded = self.counter("s_loaded")
        self.wz_ready = self.counter("wz_ready")
        self.v8_ready = self.counter("v8_ready")
        self.pad_ready = self.counter("pad_ready")
        self.silued = self.counter("silued")
        self.convolved = self.counter("convolved")
        self.eg_ready = self.counter("eg_ready")
        self.dt_args = self.counter("dt_args")
        self.dt_ready = self.counter("dt_ready")
        self.s_final = self.counter("s_final")
        self.o_scaled = self.counter("o_scaled")
        self.o_normed = self.counter("o_normed")
        self.pad_landed = [self.counter(f"pad_landed{c}") for c in range(3)]
        self.z_landed, self.stash_clear = self.counter("z_landed"), self.counter("stash_clear")
        self.gate_sigmoid = self.counter("gate_sigmoid")
        self.third_landed = [[self.counter(f"third_landed{b}{h}") for h in range(2)] for b in range(2)]
        self.third_hi, self.third_split = self.counter("third_hi"), self.counter("third_split")
        self.x_landed = [self.counter(f"x_landed{c}") for c in range(KD)]
        self.q_moved, self.streams_loaded = self.counter("q_moved"), self.counter("streams_loaded")
        self.conv_loaded, self.conv_stored = self.counter("conv_loaded"), self.counter("conv_stored")
        self.tap = self.counter("tap")
        self.nt_made = self.counter("nt_made")
        self.first_mask = self.counter("first_mask")
        self.s_decayed = self.counter("s_decayed")
        self.pre_split, self.pre_third = self.counter("pre_split"), self.counter("pre_third")
        self.pre_copied = self.counter("pre_copied")
        self.pre = self.counter("pre")
        self.pre_pe = self.counter("pre_pe")
        self.pre_act = self.counter("pre_act")
        self.b_loaded = self.counter("b_loaded")
        self.kv_done, self.s_out, self.yb_stored = (self.counter("kv_done", 1), self.counter("s_out", 48),
                                                    self.counter("yb_stored", 16))

    def counter(self, name, tokens=0):
        s = Counter(self.nc, self.ctx, name)
        if tokens:
            self.tokens.append((s, tokens))
        return s



class BiasRows:

    def __init__(self, nc, k, work):
        self.k, self.far = k, NBIAS - (2 * REL + 1)
        self.rows = nc.alloc_sbuf_tensor_at("bias_rows", [P, HA, NBIAS], F32, offset=work)

    def load(self, act):
        act.dma_start(self.rows[:, :, self.far:], self.k.table.partition_broadcast(P))\
            .then_inc(self.k.table_loaded.sem, 16)

    def spread(self, dve):
        dve.wait_ge(self.k.table_loaded.sem, self.k.table_loaded.at(16))
        dve.tensor_copy(self.rows[:, :, 0:self.far], self.rows[:, :, self.far:self.far + 1]
                        .to_broadcast([P, HA, self.far])).then_inc(self.k.rows_made.sem, 1)

    def store(self, act):
        act.wait_ge(self.k.rows_made.sem, self.k.rows_made.at(1))
        act.dma_start(self.k.bias_dram[:, 0:HA * NBIAS], self.rows[:].rearrange("p h m -> p (h m)"))\
            .then_inc(self.k.rows_stored.sem, 16)

    def stored(self, act):
        act.wait_ge(self.k.rows_stored.sem, self.k.rows_stored.at(16))


def attention_phase(nc, k, make_norm, decay, xh, xl, x, x_to, work):
    at = [work]

    def sb(name, shape):
        t = nc.alloc_sbuf_tensor_at(name, shape, F32, offset=at[0])
        at[0] += (4 * int(np.prod(shape[1:])) + 31) // 32 * 32
        return t

    kc, vc = sb("a_kc", [P, DB, REACH]), sb("a_vc", [P, DB, 4, P])
    vns = sb("a_vns", [DS, DB, P])
    at[0] = work + 4 * KD * T
    q, kt, vt = sb("a_q", [P, T]), sb("a_k", [P, T]), sb("a_v", [P, T])
    qbd = sb("a_qbd", [P, DB, 32])
    bias, bias_s = sb("a_bias", [P, 2, WIN]), sb("a_bias_s", [P, REACH + DS])
    nmax, rsum, rinv = sb("a_nmax", [P, 2]), sb("a_rsum", [P, 2]), sb("a_rinv", [P, 2])
    decay.rows = q
    norm = make_norm(at[0])
    vn = sb("a_vn", [P, 8, P])
    sc, pt = sb("a_sc", [P, 2, WIN]), sb("a_pt", [P, 2, 5, P])
    ya = sb("a_y", [P, T])
    PAIRS, STEPS, ND = HA // 2, 18, 2
    stash = sb("a_stash", [P, 2, PADDED])
    filler = Filler(3, 4, [14] * 16 + [8] * 2 + [5] * 8 + [8])
    DONE = 9 + filler.count
    psS, psT = k.psum[:, 3:5, :].rearrange("p b c -> p (b c)"), k.psum[:, 5:7, :].rearrange("p b c -> p (b c)")
    obank = (7, 2)
    shifted = k.bias_dram_flat[P - 1:P - 1 + P * (k.bias_pitch - 1)].rearrange("(q m) -> q m", q=P)[:, 0:HA * NBIAS]\
        .rearrange("q (h m) -> h q m", h=HA)

    def window(t):
        n = min(5, t + 1)
        return t + 1 - n, n

    with nc.Block() as block:
        @block.sync
        def _(sp):
            decay.load(sp)

            def store_x():
                for c in range(KD):
                    sp.dma_start(x_to[c], x[:, c, :]).then_inc(k.loaded.sem, 16)

            load_units(sp, k, k.next_unit, PAIRS, 7, then=store_x)

        @block.gpsimd
        def _(pool):
            split_units(pool, k, PAIRS, filler.jobs(), norm)

        @block.tensor
        def _(pe):
            def scores(i, s):
                if s >= 1:
                    pe.wait_ge(k.biased.sem, k.biased.at(STEPS * i + s))
                if s < 16:
                    t, h = s // 2, s % 2
                    k0, n = window(t)
                    hp = slice(64 * h, 64 * h + 64)
                    for a, b in ((0, min(4, n)), (4, n)):
                        if b > a:
                            mm = pe.matmul(psS[:, a * P:b * P], q[hp, t * P:(t + 1) * P],
                                           kt[hp, (k0 + a) * P:(k0 + b) * P], start=True, stop=True)
                    mm.then_inc(k.scored.sem, 1)
                    return
                for b in range(4):
                    st = 4 * (s - 16) + b
                    pe.matmul(psS[32 * b:32 * b + 32, 0:REACH], qbd[:, st, :], kc[:, st, :], start=True, stop=True,
                              tile_position=(0, 32 * b))
                    mm = pe.matmul(psS[32 * b:32 * b + 32, REACH:REACH + DS], qbd[:, st, :],
                                   kt[:, SEQ + DS * st:SEQ + DS * (st + 1)], start=True, stop=True,
                                   tile_position=(0, 32 * b))
                mm.then_inc(k.scored.sem, 1)

            def turn_probs(i, s):
                pe.wait_ge(k.normed.sem, k.normed.at(STEPS * i + (s + 1)))
                if s >= 1:
                    pe.wait_ge(k.pt_ready.sem, k.pt_ready.at(STEPS * i + s))
                b = s % 2
                n = window(s // 2)[1] if s < 16 else 4
                for j in range(n):
                    mm = pe.transpose(psT[:, j * P:(j + 1) * P], sc[:, b, j * P:(j + 1) * P], k.ident[:, :])
                if s >= 16:
                    mm = pe.transpose(psT[0:DS, 4 * P:5 * P], sc[:, b, REACH:REACH + DS], k.ident[:, :])
                mm.then_inc(k.turned.sem, 1)

            def values(i, s):
                pe.wait_ge(k.pt_ready.sem, k.pt_ready.at(STEPS * i + (s + 1)))
                o = k.ps[obank[(s // 2) % 2 if s < 16 else s % 2]]
                b = s % 2
                if s < 16:
                    t, h = s // 2, s % 2
                    k0, n = window(t)
                    if h == 0 and t >= 2:
                        pe.wait_ge(k.o_read.sem, k.o_read.at(10 * i + (t - 1)))
                    for j in range(n):
                        mm = pe.matmul(o[64 * h:64 * h + 64, 0:P], vn[:, k0 + j, 64 * h:64 * h + 64], pt[:, b, j, :],
                                       start=(j == 0), stop=(j == n - 1), tile_position=(0, 64 * h))
                    mm.then_inc(k.valued.sem, 1)
                    return
                pe.wait_ge(k.o_read.sem, k.o_read.at(10 * i + (8 + (s - 16) - 1)))
                for c in range(4):
                    st = 4 * (s - 16) + c
                    out = o[:, 32 * c:32 * c + 32]
                    for j in range(4):
                        pe.matmul(out, vc[:, st, j, :], pt[:, b, j, 32 * c:32 * c + 32], start=(j == 0), stop=False)
                    mm = pe.matmul(out, vns[0:DS, st, :], pt[0:DS, b, 4, 32 * c:32 * c + 32], start=False, stop=True)
                    if c == 3:
                        mm.then_inc(k.valued.sem, 1)
                    filler.products(k, pe, i, 18 + 4 * (s - 16) + c, xh, xl)

            norm.tensor(pe)
            decay.products(pe, norm, xh, xl)
            with pe.Fori(0, PAIRS) as i:
                for u in range(3):
                    pe.wait_ge(k.unit_split.sem, k.unit_split.at(7 * i + (u + 1)))
                    for n in range(3):
                        g = 3 * u + n
                        pe.wait_ge(k.evacuated.sem, k.evacuated.at(DONE * i + max(g + 1, 2)))
                        tiles = [(k.w_hi[u][:, c * P:(c + 1) * P], k.w_lo[u][:, c * P:(c + 1) * P],
                                  xh[:, c, :], xl[:, c, :]) for c in range(KD)]
                        product(pe, k.ps[g % ND][:, 0:THIRD], tiles, n * THIRD, (n + 1) * THIRD)\
                            .then_inc(k.dense_done.sem, 1)
                pe.wait_ge(k.evacuated.sem, k.evacuated.at(DONE * i + (9 + ND)))
                for t in range(8):
                    mm = pe.transpose(psT[:, t * P:(t + 1) * P], vt[:, t * P:(t + 1) * P], k.ident[:, :])
                mm.then_inc(k.v_turned.sem, 1)
                for b in range(DB):
                    mm = pe.transpose(psS[0:DS, b * P:(b + 1) * P], vt[:, SEQ + DS * b:SEQ + DS * (b + 1)], k.ident[:, :])
                mm.then_inc(k.v_turned.sem, 1)
                pe.wait_ge(k.vn_ready.sem, k.vn_ready.at(2 * i + 2))
                for s in range(STEPS + 2):
                    if s == 16:
                        pe.wait_ge(k.a_loaded.sem, k.a_loaded.at(192 * i + 192))
                        pe.wait_ge(k.qbd_ready.sem, k.qbd_ready.at(2 * i + 2))
                    if s < STEPS:
                        scores(i, s)
                    if s >= 2:
                        values(i, s - 2)
                    if s < STEPS:
                        filler.products(k, pe, i, s, xh, xl)
                    if 1 <= s <= STEPS:
                        turn_probs(i, s - 1)
                filler.products(k, pe, i, 26, xh, xl)
            decay.block_sums(pe)

        @block.scalar
        def _(act):
            def evacuate(i, g):
                act.wait_ge(k.dense_done.sem, k.dense_done.at(DONE * i + (g + 1)))
                u, n = g // 3 - 3, g % 3
                row, src = stash[:, u % 2, :], k.ps[g % ND]
                if n == 0:
                    act.wait_ge(k.kv_slot[u % 2].sem, k.kv_slot[u % 2].at(32 * i + (16 * (u // 2) + 32)))
                if u == 3:
                    act.activation(row[:, n * THIRD:(n + 1) * THIRD], src[:, 0:THIRD], ACT.Copy)\
                        .then_inc(k.evacuated.sem, 1)
                elif n < 2:
                    act.activation(row[:, CW - 1 + n * THIRD:CW - 1 + (n + 1) * THIRD], src[:, 0:THIRD], ACT.Copy)\
                        .then_inc(k.evacuated.sem, 1)
                else:
                    act.activation(row[:, CW - 1 + 2 * THIRD:PADP], src[:, 0:THIRD - P], ACT.Copy)
                    act.activation(row[:, PADP:].rearrange("p (b c) -> p b c", c=PADS)[:, :, CW - 1:],
                                   src[:, THIRD - P:THIRD].rearrange("p (b c) -> p b c", c=DS), ACT.Copy)\
                        .then_inc(k.evacuated.sem, 1)
                if n == 2:
                    act.wait_ge(k.evacuated.sem, k.evacuated.at(DONE * i + (g + 1 + ND)))
                    act.dma_start(k.proj_dram[4 * i + u], row).then_inc(k.kv_slot[u % 2].sem, 16)

            norm.scalar(act)
            decay.scalar_before(act)
            act.wait_ge(k.stash_clear.sem, k.stash_clear.at(1))
            with act.Fori(0, PAIRS) as i:
                act.wait_ge(k.valued.sem, k.valued.at(STEPS * i + 1))
                loads = []
                for h in range(2):
                    loads.append((bias[:, h, :], shifted[2 * i + h][:, 0:WIN]))
                    for b in range(4):
                        r = 32 * b + 16 * h
                        loads.append((bias_s[r:r + 16, :], shifted[2 * i + h][0:16, 0:REACH + DS]))
                for dst, src in loads:
                    act.dma_start(dst, src).then_inc(k.a_loaded.sem, 16)
                for g in range(9):
                    if g == 3:
                        act.wait_ge(k.kv_stored.sem, k.kv_stored.at(32 * i + 32))
                    act.wait_ge(k.dense_done.sem, k.dense_done.at(DONE * i + (g + 1)))
                    dst = (q, kt, vt)[g // 3][:, (g % 3) * THIRD:(g % 3 + 1) * THIRD]
                    act.activation(dst, k.ps[g % ND][:, 0:THIRD], ACT.Copy,
                                   scale=DHA ** -0.5 if g < 3 else 1.0).then_inc(k.evacuated.sem, 1)
                    if g == 5:
                        act.wait_ge(norm.s.nscaled.sem, norm.s.nscaled.at(2 * norm.nb))
                        act.wait_ge(k.loaded.sem, k.loaded.at(16 * KD))
                        for dst, src in ((kc[:], k.k_cache[i]), (vc[:], k.v_cache[i])):
                            act.dma_start(dst, src).then_inc(k.a_loaded.sem, 16)
                act.wait_ge(k.evacuated.sem, k.evacuated.at(DONE * i + (9 + ND)))
                act.dma_start(k.a_k_out[i], kt[:, :]).then_inc(k.kv_stored.sem, 16)
                act.dma_start(k.a_v_out[i], vt[:, :]).then_inc(k.kv_stored.sem, 16)
                act.wait_ge(k.v_turned.sem, k.v_turned.at(2 * i + 1))
                act.activation(vn[:].rearrange("p t c -> p (t c)"), psT[:, :], ACT.Copy).then_inc(k.vn_ready.sem, 1)
                act.wait_ge(k.v_turned.sem, k.v_turned.at(2 * i + 2))
                act.activation(vns[:].rearrange("p t c -> p (t c)"), psS[0:DS, :], ACT.Copy).then_inc(k.vn_ready.sem, 1)

                def exps(s):
                    act.wait_ge(k.maxed.sem, k.maxed.at(STEPS * i + (s + 1)))
                    n = window(s // 2)[1] * P if s < 16 else REACH + DS
                    b = s % 2
                    act.activation(sc[:, b, 0:n], sc[:, b, 0:n], ACT.Exp, bias=nmax[:, b:b + 1],
                                   accum_out=rsum[:, b:b + 1]).then_inc(k.exped.sem, 1)

                def copy_turned(s):
                    act.wait_ge(k.turned.sem, k.turned.at(STEPS * i + (s + 1)))
                    if s >= 2:
                        act.wait_ge(k.valued.sem, k.valued.at(STEPS * i + (s - 1 + 1)))
                    n = window(s // 2)[1] if s < 16 else 4
                    b = s % 2
                    if s >= 16:
                        act.activation(pt[0:DS, b, 4, :], psT[0:DS, 4 * P:5 * P], ACT.Copy)
                    act.activation(pt[:, b, 0:n, :].rearrange("p t c -> p (t c)"), psT[:, 0:n * P], ACT.Copy)\
                        .then_inc(k.pt_ready.sem, 1)

                def copy_o(s):
                    act.wait_ge(k.valued.sem, k.valued.at(STEPS * i + (s + 1 + 1)))
                    if s == 1:
                        act.wait_ge(k.ya_stored.sem, k.ya_stored.at(16 * i + 16))
                    if s < 16:
                        t = s // 2
                        act.activation(ya[:, t * P:(t + 1) * P], k.ps[obank[t % 2]][:, 0:P], ACT.Copy)\
                            .then_inc(k.o_read.sem, 1)
                        return
                    o = k.ps[obank[s % 2]]
                    for h in range(2):
                        hp = slice(64 * h, 64 * h + 64)
                        c0 = SEQ + 64 * (s - 16)
                        a = act.activation(ya[hp, c0:c0 + 64].rearrange("p (b c) -> p b c", c=16),
                                           o[hp, 0:P].rearrange("p (b c) -> p b c", c=32)[:, :, 16 * h:16 * h + 16],
                                           ACT.Copy)
                    a.then_inc(k.o_read.sem, 1)

                for s in range(STEPS + 3):
                    if s >= 1:
                        for g in filler.finished(s - 1) if s <= STEPS else filler.finished(18 + 4 * (s - 19), 4):
                            evacuate(i, g)
                    if s < STEPS:
                        exps(s)
                    if 1 <= s <= STEPS:
                        copy_turned(s - 1)
                    if s >= 3 and ((s - 3) % 2 == 1 or s - 3 >= 16):
                        copy_o(s - 3)
                for g in filler.finished(26):
                    evacuate(i, g)
                act.wait_ge(k.o_read.sem, k.o_read.at(10 * i + 10))
                act.dma_start(k.ya_dram[i], ya[:, :]).then_inc(k.ya_stored.sem, 16)
            decay.scalar_behind(act)
            act.wait_ge(k.ya_stored.sem, k.ya_stored.at(16 * PAIRS + 16))
            act.wait_ge(k.kv_stored.sem, k.kv_stored.at(32 * PAIRS + 32))
            for b in range(2):
                act.wait_ge(k.kv_slot[b].sem, k.kv_slot[b].at(32 * PAIRS + 32))

        @block.vector
        def _(dve):
            decay.split_weights(dve)
            norm.vector(dve)
            decay.copy_rows(dve)
            decay.vector_before(dve)
            dve.wait_ge(norm.s.nsplit[1].sem, norm.s.nsplit[1].at(norm.nb))
            dve.memset(stash[:], 0.0).then_inc(k.stash_clear.sem, 1)
            dve.memset(qbd[:], 0.0).then_inc(k.qbd_zero.sem, 1)
            dve.wait_ge(k.qbd_zero.sem, k.qbd_zero.at(1))
            with dve.Fori(0, PAIRS) as i:
                dve.wait_ge(k.evacuated.sem, k.evacuated.at(DONE * i + (3 + ND)))
                for h in range(2):
                    hp = slice(64 * h, 64 * h + 64)
                    dve.tensor_copy(qbd[hp, :, 16 * h:16 * h + 16], q[hp, SEQ:T].rearrange("p (b c) -> p b c", c=DS))\
                        .then_inc(k.qbd_ready.sem, 1)
                dve.wait_ge(k.a_loaded.sem, k.a_loaded.at(192 * i + 192))
                for h in range(2):
                    dve.memset(bias[0:64, h, WIN - 64:WIN], NEG)
                    m = dve.memset(bias[64:P, h, 0:64], NEG)
                m.then_inc(k.masked.sem, 1)
                dve.wait_ge(k.masked.sem, k.masked.at(i + 1))

                def logits(s):
                    dve.wait_ge(k.scored.sem, k.scored.at(STEPS * i + (s + 1)))
                    if s >= 2:
                        dve.wait_ge(k.turned.sem, k.turned.at(STEPS * i + (s - 1)))
                    b = s % 2
                    if s < 16:
                        n = window(s // 2)[1] * P
                        add = bias[:, s % 2, WIN - n:WIN]
                    else:
                        n, add = REACH + DS, bias_s[:, :]
                    dve.tensor_tensor(sc[:, b, 0:n], psS[:, 0:n], add, ALU.add).then_inc(k.biased.sem, 1)
                    dve.wait_ge(k.biased.sem, k.biased.at(STEPS * i + (s + 1)))
                    dve.tensor_reduce(nmax[:, b:b + 1], sc[:, b, 0:n], AX_X, ALU.max, negate=True)\
                        .then_inc(k.maxed.sem, 1)

                def normalise(s):
                    b = s % 2
                    n = window(s // 2)[1] * P if s < 16 else REACH + DS
                    dve.wait_ge(k.exped.sem, k.exped.at(STEPS * i + (s + 1)))
                    dve.reciprocal(rinv[:, b:b + 1], rsum[:, b:b + 1]).then_inc(k.inverted.sem, 1)
                    dve.wait_ge(k.inverted.sem, k.inverted.at(STEPS * i + (s + 1)))
                    dve.tensor_scalar(sc[:, b, 0:n], sc[:, b, 0:n], rinv[:, b:b + 1], None, ALU.mult)\
                        .then_inc(k.normed.sem, 1)

                for s in range(STEPS + 1):
                    if s < STEPS:
                        logits(s)
                    if s >= 1:
                        normalise(s - 1)
            decay.vector_behind(dve)

    units_done(k, PAIRS, 7)
    k.qbd_zero.base += 1
    k.stash_clear.base += 1
    k.loaded.base += 16 * KD
    norm.done()
    decay.done()
    for b in range(2):
        k.kv_slot[b].base += 32 * PAIRS
    for s_, n in ((k.dense_done, DONE), (k.evacuated, DONE), (k.v_turned, 2), (k.vn_ready, 2), (k.scored, STEPS),
                  (k.biased, STEPS), (k.maxed, STEPS), (k.exped, STEPS), (k.inverted, STEPS), (k.normed, STEPS),
                  (k.turned, STEPS), (k.pt_ready, STEPS), (k.valued, STEPS), (k.o_read, 10), (k.a_loaded, 192),
                  (k.kv_stored, 32), (k.ya_stored, 16), (k.masked, 1), (k.qbd_ready, 2)):
        s_.base += n * PAIRS



MASKS = ("upto", "upto16", "future", "future16", "same16")


def delta_constants():
    j, i = np.arange(P)[:, None], np.arange(P)[None, :]
    same = j // DS == i // DS
    out = [j <= i, (j <= i) & same, np.where(j <= i, 0, NEG), np.where((j <= i) & same, 0, NEG), same]
    for level in range(7):
        half = 1 << level
        out.append((i // (2 * half) == j // (2 * half)) & (i % (2 * half) >= half) & (j % (2 * half) < half))
    streams = (j // DS) == np.arange(DB)[None, :]
    return np.concatenate([np.asarray(m, np.float32) for m in out + [streams]], axis=1)


PLAN_START, PLAN_NORM, PLAN_GROUP, PLAN_BEFORE, PLAN_LEVEL, PLAN_W, PLAN_STEP, PLAN_LAST = \
    82, 5, 16, 10, 2, 8, 5, 9
FIRST_TAP = 2


class Decay:

    def __init__(self, nc, k):
        NM = 12
        at = [SBUF_END - 4 * (NM * P + DB) - 3 * 4 * KD * 8 - 32 * 3 - 736 - 3 * 160]

        def sb(name, shape, dt=F32):
            t = nc.alloc_sbuf_tensor_at(name, shape, dt, offset=at[0])
            at[0] += (4 * int(np.prod(shape[1:])) + 31) // 32 * 32
            return t

        self.k, self.offset = k, at[0]
        self.consts = sb("b_consts", [P, NM * P + DB])

        def const(n):
            return self.consts[:, n * P:(n + 1) * P]

        self.upto, self.upto16, self.future, self.future16, self.same16 = (const(n) for n in range(5))
        self.level_mask = [const(5 + n) for n in range(7)]
        self.streams = self.consts[:, NM * P:NM * P + DB]
        self.w8, self.w8h, self.w8l = (sb("b_w8", [P, KD, 8]), sb("b_w8h", [P, KD, 8], F32R),
                                       sb("b_w8l", [P, KD, 8], F32R))
        self.rate, self.dtb, self.gn = sb("b_rate", [P, HB]), sb("b_dtb", [P, HB]), sb("b_gn", [P, 1])
        self.per = sb("b_per", [P, HB, 5, NT_TILES])
        self.t1, self.t2, self.t3 = (sb(n, [P, HB, NT_TILES]) for n in ("b_t1", "b_t2", "b_t3"))
        self.banks, self.raw, self.sums = (k.ps[7], k.ps[2], k.ps[3]), k.ps[7][:, 400:], k.ps[3]


    def load(self, sp):
        k = self.k
        for dst, src in ((self.consts[:], k.b_consts), (self.w8[:], k.w_beta_decay),
                         (self.rate[:], k.a_log.partition_broadcast(P)), (self.dtb[:], k.dt_bias.partition_broadcast(P)),
                         (self.gn[:], k.b_gain)):
            sp.dma_start(dst, src).then_inc(k.b_loaded.sem, 16)

    def products(self, pe, norm, xh, xl):
        k = self.k
        pe.wait_ge(k.pre_split.sem, k.pre_split.at(2))
        for n in range(3):
            for h in range(2):
                pe.wait_ge(norm.s.nsplit[h].sem, norm.s.nsplit[h].at(n + 1))
            tiles = [(self.w8h[:, c, :], self.w8l[:, c, :], xh[:, c, :], xl[:, c, :]) for c in range(KD)]
            product(pe, self.banks[n][0:8, 0:THIRD], tiles, n * THIRD, (n + 1) * THIRD).then_inc(k.pre_third.sem, 1)
        pe.wait_ge(k.pre_copied.sem, k.pre_copied.at(3))
        for t in range(NT_TILES):
            mm = pe.transpose(self.raw[:, 8 * t:8 * t + 8], self.rows[0:8, t * P:(t + 1) * P], k.ident[0:8, 0:8])
        mm.then_inc(k.pre_pe.sem, 1)

    def block_sums(self, pe):
        k = self.k
        pe.wait_ge(k.pre.sem, k.pre.at(8))
        for dst, m16, m in ((0, self.upto16, self.upto), (64, self.same16, k.ones[:, :])):
            pe.matmul(self.sums[:, dst:dst + 32], m, self.t1[:, :, 0:8], start=True, stop=True)
            mm = pe.matmul(self.sums[:, dst + 32:dst + 36], m16, self.t1[:, :, 8:9], start=True, stop=True)
        mm.then_inc(k.pre_pe.sem, 1)

    def scalar_before(self, act):
        k, t2, t3 = self.k, self.t2, self.t3
        act.wait_ge(k.b_loaded.sem, k.b_loaded.at(80))
        act.activation(self.rate[:, :], self.rate[:, :], ACT.Exp).then_inc(k.pre_act.sem, 1)
        act.wait_ge(k.pre.sem, k.pre.at(1))
        act.activation(t2[:], t2[:], ACT.Exp).then_inc(k.pre_act.sem, 1)
        act.wait_ge(k.pre.sem, k.pre.at(4))
        act.activation(t3[:], t3[:], ACT.Exp).then_inc(k.pre_act.sem, 1)
        act.wait_ge(k.pre_act.sem, k.pre_act.at(3))
        act.activation(t3[:], t3[:], ACT.Ln, bias=1.0).then_inc(k.pre_act.sem, 1)

    def scalar_behind(self, act):
        k, t2, t3 = self.k, self.t2, self.t3
        act.wait_ge(k.pre.sem, k.pre.at(10))
        act.activation(t2[:], t2[:], ACT.Exp).then_inc(k.pre_act.sem, 1)
        act.wait_ge(k.pre_act.sem, k.pre_act.at(5))
        act.wait_ge(k.pre.sem, k.pre.at(12))
        act.activation(self.per[:, :, 2, :], t3[:], ACT.Exp).then_inc(k.pre_act.sem, 1)

    def both(self, off):
        return self.raw[:, 0:8 * NT_TILES].rearrange("p (t c) -> p c t", c=8)[:, off:off + HB, :]

    def split_weights(self, dve):
        k = self.k
        dve.wait_ge(k.b_loaded.sem, k.b_loaded.at(80))
        dve.tensor_copy(self.w8h[:], self.w8[:]).then_inc(k.pre_split.sem, 1)
        dve.wait_ge(k.pre_split.sem, k.pre_split.at(1))
        dve.tensor_tensor(self.w8l[:], self.w8[:], self.w8h[:].bitcast(F32), ALU.subtract).then_inc(k.pre_split.sem, 1)

    def copy_rows(self, dve):
        k = self.k
        for n in range(3):
            dve.wait_ge(k.pre_third.sem, k.pre_third.at(n + 1))
            dve.tensor_copy(self.rows[0:8, n * THIRD:(n + 1) * THIRD], self.banks[n][0:8, 0:THIRD])\
                .then_inc(k.pre_copied.sem, 1)

    def vector_before(self, dve):
        k, t1, t2, t3 = self.k, self.t1, self.t2, self.t3
        wide = [P, HB, NT_TILES]
        dve.wait_ge(k.pre_pe.sem, k.pre_pe.at(1))
        dve.tensor_scalar(t2[:], self.both(0), -1.0, None, ALU.mult).then_inc(k.pre.sem, 1)
        dve.tensor_tensor(t1[:], self.both(HB), self.dtb[:, :].unsqueeze(2).to_broadcast(wide), ALU.add)\
            .then_inc(k.pre.sem, 1)
        dve.wait_ge(k.pre.sem, k.pre.at(2))
        dve.tensor_scalar(t3[:], t1[:], -1.0, None, ALU.mult).then_inc(k.pre.sem, 1)
        dve.wait_ge(k.pre.sem, k.pre.at(3))
        dve.tensor_tensor(t3[:], t1[:], t3[:], ALU.min).then_inc(k.pre.sem, 1)
        dve.wait_ge(k.pre_act.sem, k.pre_act.at(2))
        dve.tensor_scalar(t2[:], t2[:], 1.0, None, ALU.add).then_inc(k.pre.sem, 1)
        dve.wait_ge(k.pre.sem, k.pre.at(5))
        dve.reciprocal(self.per[:, :, 0, :], t2[:]).then_inc(k.pre.sem, 1)
        dve.wait_ge(k.pre_act.sem, k.pre_act.at(4))
        dve.scalar_tensor_tensor(out=t1[:], in0=t1[:], scalar=0.0, in1=t3[:], op0=ALU.max, op1=ALU.add)\
            .then_inc(k.pre.sem, 1)
        dve.wait_ge(k.pre.sem, k.pre.at(7))
        dve.scalar_tensor_tensor(out=t1[:], in0=t1[:], scalar=-1.0, in1=self.rate[:, :].unsqueeze(2).to_broadcast(wide),
                                 op0=ALU.mult, op1=ALU.mult).then_inc(k.pre.sem, 1)

    def vector_behind(self, dve):
        k, t1, t2, t3, per = self.k, self.t1, self.t2, self.t3, self.per
        dve.wait_ge(k.pre_pe.sem, k.pre_pe.at(2))
        gc8, gc1 = self.sums[:, 0:32].rearrange("p (h t) -> p h t", h=HB), self.sums[:, 32:36].unsqueeze(2)
        gl8, gl1 = self.sums[:, 64:96].rearrange("p (h t) -> p h t", h=HB), self.sums[:, 96:100].unsqueeze(2)
        dve.tensor_copy(t2[:, :, 0:8], gc8).then_inc(k.pre.sem, 1)
        dve.tensor_copy(t2[:, :, 8:9], gc1).then_inc(k.pre.sem, 1)
        dve.tensor_scalar(per[:, :, 3, 0:8], gc8, -1.0, None, ALU.mult)
        dve.tensor_scalar(per[:, :, 3, 8:9], gc1, -1.0, None, ALU.mult).then_inc(k.pre.sem, 1)
        dve.wait_ge(k.pre.sem, k.pre.at(11))
        dve.tensor_tensor(t3[:, :, 0:8], gl8, per[:, :, 3, 0:8], ALU.add)
        dve.tensor_tensor(t3[:, :, 8:9], gl1, per[:, :, 3, 8:9], ALU.add).then_inc(k.pre.sem, 1)
        dve.wait_ge(k.pre_act.sem, k.pre_act.at(6))
        dve.tensor_tensor(per[:, :, 1, :], per[:, :, 0, :], t2[:], ALU.mult)
        dve.tensor_copy(per[:, :, 4, :], t1[:]).then_inc(k.pre.sem, 1)

    def done(self):
        k = self.k
        k.pre.base += 13
        k.pre_pe.base += 2
        k.pre_split.base += 2
        k.pre_third.base += 3
        k.pre_copied.base += 3
        k.pre_act.base += 6
        k.b_loaded.base += 80


def delta_phase(nc, k, decay, xh, xl, work):
    at = [work]

    def sb(name, shape, dt=F32):
        t = nc.alloc_sbuf_tensor_at(name, shape, dt, offset=at[0])
        at[0] += (4 * int(np.prod(shape[1:])) + 31) // 32 * 32
        return t

    def alias(name, shape, offset):
        return nc.alloc_sbuf_tensor_at(name, shape, F32, offset=offset)

    upto, upto16, future, future16 = decay.upto, decay.upto16, decay.future, decay.future16
    level_mask, streams, gn, per = decay.level_mask, decay.streams, decay.gn, decay.per
    pad_at = at[0]
    pad = sb("b_pad", [P, 3, PADDED])
    X, Y, P1 = (alias(n, [P, T], pad_at + 4 * T * m) for m, n in enumerate(("b_X", "b_Y", "b_P1")))
    yq_at = at[0]
    y = sb("b_y", [P, 3, T])
    yq, yk, yv = y[:, 0, :], y[:, 1, :], y[:, 2, :]
    oT, MT = alias("b_oT", [P, T], yq_at + 4 * T), alias("b_MT", [P, T], yq_at + 8 * T)
    z = sb("b_z", [P, T])
    kbe, kd, vb = sb("b_kbe", [P, T]), sb("b_kd", [P, T]), sb("b_vb", [P, T])
    before_silu = (kbe[:, :], vb[:, :], yv)
    eg = sb("b_eg", [P, T])
    DT = sb("b_DT", [P, T])
    wT = alias("b_wT", [P, T], at[0] - 4 * T)
    NT = sb("b_NT", [P, T])
    u = alias("b_u", [P, T], at[0] - 4 * T)
    intra = sb("b_intra", [P, T])
    S = sb("b_S", [P, 2, P])
    Sb, v8 = sb("b_Sb", [P, DB, P]), sb("b_v8", [P, DB, P])
    wz = sb("b_wz", [P, DB * (P + DS)])[:]
    vw = sb("b_vw", [P, 2, P])
    sq = sb("b_sq", [P, 2, THIRD])
    rr = sb("b_rr", [P, 2, THIRD])
    cst, cout = sb("b_cst", [P, 3, DB, CW - 1]), sb("b_cout", [P, 3, (DB + 1) * (CW - 1)])
    cw = sb("b_cw", [P, 3, CW])
    stash = sb("b_stash", [P, 2, THIRD])
    sh = sb("b_sh", [P, 5, NT_TILES])
    assert at[0] <= decay.offset
    ND = 2
    LV = 18
    START, NORM, GROUP, BEFORE, LEVEL = 0, 1, 7, 10, 11
    W, STEP, END, LAST = LEVEL + LV, LEVEL + LV + 3, LEVEL + LV + 11, LEVEL + LV + 12
    plan = [PLAN_START] + [PLAN_NORM] * 6 + [PLAN_GROUP] * 3 + [PLAN_BEFORE] + [PLAN_LEVEL] * LV + [PLAN_W] * 3 + \
        [PLAN_STEP] * 8 + [0] + [PLAN_LAST] * 2
    plan[END] = 12 * Filler.PIECES - sum(plan)
    filler = Filler(0, 4, plan)

    def third(g):
        return slice(g * THIRD, (g + 1) * THIRD)

    def tile(t):
        return slice(t * P, (t + 1) * P)

    def by_tile(a):
        return a.rearrange("p (t c) -> p t c", c=P)

    def bank(a, b):
        return k.ps[a + b % 2]

    with nc.Block() as block:
        @block.sync
        def _(sp):
            def projections(i):
                if not isinstance(i, int):
                    sp.wait_ge(k.wu_done.sem, k.wu_done.at(3 * i))
                for dst, src in ((cst[:], k.conv_state[i]), (cw[:], k.conv_w[i])):
                    sp.dma_start(dst, src).then_inc(k.conv_loaded.sem, 16)
                for c in range(3):
                    sp.dma_start(pad[:, c, :], k.proj_dram[4 * i + c]).then_inc(k.pad_landed[c].sem, 16)
                sp.wait_ge(k.convolved.sem, k.convolved.at(3 * i + 1))
                sp.dma_start(pad[:, 0, 0:T], k.proj_dram[4 * i + 3][:, 0:T]).then_inc(k.z_landed.sem, 16)

            load_units(sp, k, k.next_unit, HB, 4, projections)

        @block.gpsimd
        def _(pool):
            split_units(pool, k, HB, (3, 6, 9, 12))

        def correct(pe, i, r):
            g = r % 3
            pe.wait_ge(k.p1_ready.sem, k.p1_ready.at(LV * i + (r + 1)))
            if r >= 2:
                pe.wait_ge(k.level_done.sem, k.level_done.at(LV * i + (r - 1)))
            if r < LV - 3:
                for t in range(3 * g, 3 * g + 3):
                    pe.matmul(bank(4, r)[:, tile(t % 3)], Y[:, tile(t)], P1[:, tile(t)], start=True, stop=True)
            for t in range(3 * g, 3 * g + 3):
                mm = pe.matmul(bank(6, r)[:, tile(t % 3)], P1[:, tile(t)], Y[:, tile(t)], start=True, stop=True)
            mm.then_inc(k.corrected.sem, 1)

        @block.tensor
        def _(pe):
            with pe.Fori(0, HB) as i:
                filler.products(k, pe, i, START, xh, xl)
                for r in range(6):
                    filler.products(k, pe, i, NORM + r, xh, xl)
                    pe.wait_ge(k.squared.sem, k.squared.at(9 * i + (r + 1)))
                    if r >= 2:
                        pe.wait_ge(k.lned.sem, k.lned.at(9 * i + (r - 1)))
                    pe.matmul(bank(2, r)[:, 0:THIRD], k.ones[:, :], sq[:, r % 2, :], start=True, stop=True)\
                        .then_inc(k.sq_summed.sem, 1)
                pe.wait_ge(k.per_ready.sem, k.per_ready.at(i + 1))
                pe.wait_ge(k.lned.sem, k.lned.at(9 * i + 6))
                for g in range(3):
                    tiles = range(3 * g, 3 * g + 3)
                    if g >= 1:
                        pe.wait_ge(k.decayed.sem, k.decayed.at(3 * i + g))
                        pe.wait_ge(k.scaled.sem, k.scaled.at(3 * i + g))
                    for t in tiles:
                        o = tile(t % 3)
                        pe.matmul(k.ps[2][:, o], sh[:, 4, t:t + 1].to_broadcast([P, P]), upto if t < 8 else upto16,
                                  start=True, stop=True)
                    for t in tiles:
                        mm = pe.matmul(k.ps[3][:, tile(t % 3)], sh[:, 0, t:t + 1].to_broadcast([P, P]), k.ident[:, :],
                                       start=True, stop=True)
                    mm.then_inc(k.rows_spread.sem, 1)
                    pe.wait_ge(k.l2_done.sem, k.l2_done.at(6 * i + (g + 4)))
                    for t in tiles:
                        pe.matmul(k.ps[4][:, tile(t % 3)], yk[:, tile(t)], yk[:, tile(t)], start=True, stop=True)
                    for t in tiles:
                        mm = pe.matmul(k.ps[5][:, tile(t % 3)], yk[:, tile(t)], yq[:, tile(t)], start=True, stop=True)
                    mm.then_inc(k.grams.sem, 1)
                    for t in tiles:
                        pe.transpose(k.ps[6][:, tile(t % 3)], yk[:, tile(t)], k.ident[:, :])
                    for t in tiles:
                        mm = pe.transpose(k.ps[7][:, tile(t % 3)], yv[:, tile(t)], k.ident[:, :])
                    mm.then_inc(k.kv_turned.sem, 1)
                    filler.products(k, pe, i, GROUP + g, xh, xl)
                filler.products(k, pe, i, BEFORE, xh, xl)
                pe.wait_ge(k.decayed.sem, k.decayed.at(3 * i + 3))
                pe.wait_ge(k.scaled.sem, k.scaled.at(3 * i + 3))
                for g in range(3):
                    pe.wait_ge(k.y_started.sem, k.y_started.at(3 * i + (g + 1)))
                    for t in range(3 * g, 3 * g + 3):
                        mm = pe.transpose(k.ps[2 + g][:, tile(t % 3)], Y[:, tile(t)], k.ident[:, :])
                    mm.then_inc(k.y_turned.sem, 1)
                pe.wait_ge(k.x_started.sem, k.x_started.at(3 * i + 3))
                for r in range(LV):
                    g = r % 3
                    pe.wait_ge(k.masked_level.sem, k.masked_level.at(LV * i + (r + 1)))
                    if r >= 2:
                        pe.wait_ge(k.p1_ready.sem, k.p1_ready.at(LV * i + (r - 1)))
                    for t in range(3 * g, 3 * g + 3):
                        mm = pe.matmul(bank(2, r)[:, tile(t % 3)], MT[:, tile(t)], X[:, tile(t)], start=True, stop=True)
                    mm.then_inc(k.p1_done.sem, 1)
                    filler.products(k, pe, i, LEVEL + r, xh, xl)
                    if r >= 1:
                        correct(pe, i, r - 1)
                correct(pe, i, LV - 1)
                pe.wait_ge(k.level_done.sem, k.level_done.at(LV * i + LV))
                for g in range(3):
                    if g >= 1:
                        pe.wait_ge(k.w_ready.sem, k.w_ready.at(3 * i + g))
                        pe.wait_ge(k.u_ready.sem, k.u_ready.at(3 * i + g))
                    for t in range(3 * g, 3 * g + 3):
                        pe.matmul(k.ps[2][:, tile(t % 3)], kbe[:, tile(t)], Y[:, tile(t)], start=True, stop=True)
                    for t in range(3 * g, 3 * g + 3):
                        mm = pe.matmul(k.ps[3][:, tile(t % 3)], Y[:, tile(t)], vb[:, tile(t)], start=True, stop=True)
                    mm.then_inc(k.wu_done.sem, 1)
                    filler.products(k, pe, i, W + g, xh, xl)
                pe.wait_ge(k.w_ready.sem, k.w_ready.at(3 * i + 3))
                pe.wait_ge(k.u_ready.sem, k.u_ready.at(3 * i + 3))
                for t in range(8):
                    s = S[:, t % 2, :]
                    pe.wait_ge(k.s_ready.sem, k.s_ready.at(9 * i + (t + 1)))
                    pe.matmul(bank(2, t)[:, 0:P], wT[:, tile(t)], s, start=True, stop=True).then_inc(k.ws_done.sem, 1)
                    filler.products(k, pe, i, STEP + t, xh, xl)
                    if t >= 2:
                        pe.wait_ge(k.o_copied.sem, k.o_copied.at(9 * i + (t - 1)))
                    pe.wait_ge(k.qg_ready.sem, k.qg_ready.at(3 * i + (t // 3 + 1)))
                    pe.matmul(bank(6, t)[:, 0:P], s, yq[:, tile(t)], start=True, stop=False)
                    pe.wait_ge(k.vw_ready.sem, k.vw_ready.at(9 * i + (t + 1)))
                    pe.matmul(bank(4, t)[:, 0:P], kd[:, tile(t)], vw[:, t % 2, :], start=True, stop=True)\
                        .then_inc(k.kv_done.sem, 1)
                    pe.matmul(bank(6, t)[:, 0:P], vw[:, t % 2, :], intra[:, tile(t)], start=False, stop=True)\
                        .then_inc(k.o_done.sem, 1)
                pe.wait_ge(k.s_loaded.sem, k.s_loaded.at(48 * i + 48))
                pe.wait_ge(k.wz_ready.sem, k.wz_ready.at(i + 1))
                pe.wait_ge(k.s_ready.sem, k.s_ready.at(9 * i + 9))
                for b in range(DB):
                    mm = pe.matmul(k.ps[2][:, 0:P], wz[:, tile(b)], Sb[:, b, :], start=(b == 0), stop=(b == DB - 1))
                mm.then_inc(k.ws_done.sem, 1)
                pe.wait_ge(k.o_copied.sem, k.o_copied.at(9 * i + 7))
                pe.wait_ge(k.vw_ready.sem, k.vw_ready.at(9 * i + 9))
                pe.matmul(k.ps[6][:, 0:P], vw[:, 0, :], intra[:, tile(8)], start=True, stop=False,
                          skip_group_check=True)
                for b in range(DB):
                    c = slice(b * DS, (b + 1) * DS)
                    mm = pe.matmul(k.ps[6][:, c], Sb[:, b, :], yq[:, SEQ + b * DS:SEQ + (b + 1) * DS],
                                   start=False, stop=(b == DB - 1), skip_group_check=True)
                mm.then_inc(k.o_done.sem, 1)
                pe.wait_ge(k.v8_ready.sem, k.v8_ready.at(i + 1))
                for h in range(2):
                    mm = pe.matmul(k.ps[4 + h][:, :], kd[:, tile(8)],
                                   v8[:, 4 * h:4 * h + 4, :].rearrange("p b c -> p (b c)"), start=True, stop=True)
                mm.then_inc(k.kv_done.sem, 1)
                filler.products(k, pe, i, END, xh, xl)
                for g in range(3):
                    pe.wait_ge(k.squared.sem, k.squared.at(9 * i + (6 + g + 1)))
                    if g == 2:
                        pe.wait_ge(k.lned.sem, k.lned.at(9 * i + 7))
                    pe.matmul(bank(2, g)[:, 0:THIRD], k.ones[:, :], sq[:, g % 2, :], start=True, stop=True)\
                        .then_inc(k.sq_summed.sem, 1)
                    if g < 2:
                        filler.products(k, pe, i, LAST + g, xh, xl)

        @block.scalar
        def _(act):
            def evacuate(i, place):
                evacuate_these(i, filler.finished(place))

            def evacuate_these(i, products):
                for g in products:
                    act.wait_ge(k.dense_done.sem, k.dense_done.at(12 * i + (g + 1)))
                    b = g % 2
                    act.wait_ge(k.kv_slot[b].sem, k.kv_slot[b].at(96 * i + (16 * (g // 2) + 32)))
                    act.activation(stash[:, b, :], k.ps[g % ND][:, 0:THIRD], ACT.Copy).then_inc(k.evacuated.sem, 1)
                    act.wait_ge(k.evacuated.sem, k.evacuated.at(12 * i + (g + 1 + ND)))
                    act.dma_start(k.gate_dram[4 * i + g // 3][:, third(g % 3)], stash[:, b, :])\
                        .then_inc(k.kv_slot[b].sem, 16)

            with act.Fori(0, HB) as i:
                first = filler.finished(START)
                for c in range(3):
                    act.wait_ge(k.convolved.sem, k.convolved.at(3 * i + (c + 1)))
                    if c == 1:
                        act.wait_ge(k.z_landed.sem, k.z_landed.at(16 * i + 16))
                        act.activation(z[:, :], pad[:, 0, 0:T], ACT.Silu).then_inc(k.silued.sem, 1)
                        evacuate_these(i, first[0:1])
                        act.wait_ge(k.yb_stored.sem, k.yb_stored.at(16 * i + 16))
                    act.activation(y[:, c, :], before_silu[c], ACT.Silu).then_inc(k.silued.sem, 1)
                act.dma_start(k.conv_out[i], cout[:]).then_inc(k.conv_stored.sem, 16)
                act.preload_act_table_set("natural_log_exp_and_others")
                evacuate_these(i, first[1:2])
                act.wait_ge(k.kv_done.sem, k.kv_done.at(9 * i + 1))
                act.wait_ge(k.s_out.sem, k.s_out.at(32 * i + 48))
                for b in range(3):
                    bb = slice(3 * b, min(DB, 3 * b + 3))
                    act.dma_start(Sb[:, bb, :], k.state_s[i][:, bb, :]).then_inc(k.s_loaded.sem, 16)
                act.wait_ge(k.silued.sem, k.silued.at(4 * i + 4))

                def square(r, src):
                    if r >= 2:
                        act.wait_ge(k.sq_summed.sem, k.sq_summed.at(9 * i + (r - 1)))
                    act.activation(sq[:, r % 2, :], src, ACT.Square).then_inc(k.squared.sem, 1)

                def root(r, scale):
                    act.wait_ge(k.sq_summed.sem, k.sq_summed.at(9 * i + (r + 1)))
                    if 2 <= r < 8:
                        act.wait_ge(k.l2_done.sem, k.l2_done.at(6 * i + min(r - 1, 6)))
                    elif r == 8:
                        act.wait_ge(k.o_normed.sem, k.o_normed.at(3 * i + 1))
                    b = k.ps[2 + r % 2] if r < 6 else k.ps[2 + (r - 6) % 2]
                    act.activation(rr[:, r % 2, :], b[:, 0:THIRD], ACT.Ln, bias=k.eps[:, 0:1], scale=scale)\
                        .then_inc(k.lned.sem, 1)
                    act.wait_ge(k.lned.sem, k.lned.at(9 * i + (r + 1)))
                    act.activation(rr[:, r % 2, :], rr[:, r % 2, :], ACT.Exp, scale=-0.5).then_inc(k.rooted.sem, 1)

                for r in range(7):
                    if r < 6:
                        square(r, y[:, r // 3, third(r % 3)])
                    if r == 1:
                        evacuate_these(i, first[2:])
                    if r >= 1:
                        root(r - 1, 1.0)
                        evacuate(i, NORM + r - 1)
                for g in range(3):
                    act.wait_ge(k.rows_spread.sem, k.rows_spread.at(3 * i + (g + 1)))
                    act.activation(eg[:, third(g)], k.ps[2][:, 0:THIRD], ACT.Exp).then_inc(k.eg_ready.sem, 1)
                    act.wait_ge(k.dt_args.sem, k.dt_args.at(3 * i + (g + 1)))
                    act.activation(DT[:, third(g)], DT[:, third(g)], ACT.Exp).then_inc(k.dt_ready.sem, 1)
                    if g >= 1:
                        evacuate(i, GROUP + g - 1)
                evacuate(i, GROUP + 2)
                evacuate(i, BEFORE)
                for g in range(3):
                    act.wait_ge(k.y_turned.sem, k.y_turned.at(3 * i + (g + 1)))
                    act.activation(X[:, third(g)], k.ps[2 + g][:, 0:THIRD], ACT.Copy).then_inc(k.x_started.sem, 1)
                for r in range(LV):
                    act.wait_ge(k.p1_done.sem, k.p1_done.at(LV * i + (r + 1)))
                    if r >= 3:
                        act.wait_ge(k.corrected.sem, k.corrected.at(LV * i + (r - 2)))
                    act.activation(P1[:, third(r % 3)], bank(2, r)[:, 0:THIRD], ACT.Copy).then_inc(k.p1_ready.sem, 1)
                    if r >= 1:
                        evacuate(i, LEVEL + r - 1)
                evacuate(i, LEVEL + LV - 1)
                for g in range(3):
                    act.wait_ge(k.wu_done.sem, k.wu_done.at(3 * i + (g + 1)))
                    act.activation(wT[:, third(g)], k.ps[2][:, 0:THIRD], ACT.Copy).then_inc(k.w_ready.sem, 1)
                    if g >= 1:
                        evacuate(i, W + g - 1)
                evacuate(i, W + 2)
                for t in range(9):
                    act.wait_ge(k.o_done.sem, k.o_done.at(9 * i + (t + 1)))
                    act.activation(oT[:, tile(t)], (bank(6, t) if t < 8 else k.ps[6])[:, 0:P], ACT.Copy)\
                        .then_inc(k.o_copied.sem, 1)
                    if 1 <= t <= 8:
                        evacuate(i, STEP + t - 1)
                act.wait_ge(k.o_copied.sem, k.o_copied.at(9 * i + 9))
                evacuate(i, END)
                for g in range(4):
                    if g < 3:
                        square(6 + g, oT[:, third(g)])
                    if g >= 1:
                        root(6 + g - 1, 1.0 / DHB)
                    if g >= 2:
                        evacuate(i, LAST + g - 2)
                act.wait_ge(k.s_final.sem, k.s_final.at(i + 1))
                act.dma_start(k.p_s_out[i], S[:, 0, :]).then_inc(k.s_out.sem, 16)
                act.dma_start(k.s_s_out[i], Sb[:]).then_inc(k.s_out.sem, 16)
                act.wait_ge(k.o_scaled.sem, k.o_scaled.at(3 * i + 3))
                act.dma_start(k.yb_dram[i], oT[:, :]).then_inc(k.yb_stored.sem, 16)
            act.wait_ge(k.yb_stored.sem, k.yb_stored.at(16 * HB + 16))
            act.wait_ge(k.s_out.sem, k.s_out.at(32 * HB + 48))
            act.wait_ge(k.conv_stored.sem, k.conv_stored.at(16 * HB))
            for b in range(2):
                act.wait_ge(k.kv_slot[b].sem, k.kv_slot[b].at(96 * HB + 32))

        @block.vector
        def _(dve):
            dve.memset(wz, 0.0)
            def convolution(i, ahead):
                def prepare(c):
                    if c == 0:
                        dve.wait_ge(k.conv_loaded.sem, k.conv_loaded.at(32 * i + (32 * ahead + 32)))
                        if ahead:
                            dve.wait_ge(k.conv_stored.sem, k.conv_stored.at(16 * i + 16))
                    dve.wait_ge(k.pad_landed[c].sem, k.pad_landed[c].at(16 * i + (16 * ahead + 16)))
                    dve.memset(pad[:, c, 0:CW - 1], 0.0)
                    dve.tensor_copy(pad[:, c, PADP:].rearrange("p (b c) -> p b c", c=PADS)[:, :, 0:CW - 1], cst[:, c])\
                        .then_inc(k.pad_ready.sem, 1)
                    dve.wait_ge(k.pad_ready.sem, k.pad_ready.at(3 * i + (3 * ahead + c + 1)))

                def tap(c, j):
                    pp, ss = pad[:, c, 0:PADP], pad[:, c, PADP:].rearrange("p (b c) -> p b c", c=PADS)
                    out = before_silu[c]
                    yp, ys = out[:, 0:SEQ], out[:, SEQ:T].rearrange("p (b c) -> p b c", c=DS)
                    w = cw[:, c, j:j + 1]
                    if j == 0:
                        prepare(c)
                        dve.tensor_scalar(yp, pp[:, 0:SEQ], w, None, ALU.mult)
                        m = dve.tensor_scalar(ys, ss[:, :, 0:DS], w, None, ALU.mult)
                        m.then_inc(k.tap.sem, 1)
                        return
                    dve.wait_ge(k.tap.sem, k.tap.at(9 * i + (9 * ahead + 3 * c + j)))
                    dve.scalar_tensor_tensor(out=yp, in0=pp[:, j:j + SEQ], scalar=w, in1=yp, op0=ALU.mult, op1=ALU.add)
                    m = dve.scalar_tensor_tensor(out=ys, in0=ss[:, :, j:j + DS], scalar=w, in1=ys,
                                                 op0=ALU.mult, op1=ALU.add)
                    if j < CW - 1:
                        m.then_inc(k.tap.sem, 1)
                        return
                    dve.tensor_copy(cout[:, c, 0:CW - 1], pp[:, SEQ:PADP])
                    m = dve.tensor_copy(cout[:, c, CW - 1:].rearrange("p (b c) -> p b c", c=CW - 1), ss[:, :, DS:PADS])
                    m.then_inc(k.convolved.sem, 1)

                return [(c, j) for c in range(3) for j in range(CW)], tap

            taps, tap = convolution(0, 0)
            for c, j in taps:
                tap(c, j)

            def turn(i, final):
                taps, tap = convolution(i, 1)

                def next_taps(n):
                    if not final:
                        for _ in range(n):
                            tap(*taps.pop(0))

                dve.tensor_copy(sh[:], per[:, i]).then_inc(k.per_ready.sem, 1)
                for r in range(6):
                    dve.wait_ge(k.rooted.sem, k.rooted.at(9 * i + (r + 1)))
                    a = y[:, r // 3, third(r % 3)]
                    dve.scalar_tensor_tensor(out=a, in0=a, scalar=DHB ** -0.5 if r < 3 else 1.0, in1=rr[:, r % 2, :],
                                             op0=ALU.mult, op1=ALU.mult).then_inc(k.l2_done.sem, 1)
                for g in range(3):
                    dve.wait_ge(k.eg_ready.sem, k.eg_ready.at(3 * i + (g + 1)))
                    for t in range(3 * g, 3 * g + 3):
                        m = dve.scalar_tensor_tensor(out=DT[:, tile(t)], in0=k.ps[2][:, tile(t % 3)],
                                                     scalar=sh[:, 3, t:t + 1], in1=future if t < 8 else future16,
                                                     op0=ALU.add, op1=ALU.add)
                    m.then_inc(k.dt_args.sem, 1)
                    dve.wait_ge(k.grams.sem, k.grams.at(3 * i + (g + 1)))
                    dve.wait_ge(k.dt_ready.sem, k.dt_ready.at(3 * i + (g + 1)))
                    dve.tensor_tensor(intra[:, third(g)], k.ps[5][:, 0:THIRD], DT[:, third(g)], ALU.mult)
                    dve.tensor_tensor(NT[:, third(g)], k.ps[4][:, 0:THIRD], DT[:, third(g)], ALU.mult)\
                        .then_inc(k.nt_made.sem, 1)
                    dve.tensor_tensor(yq[:, third(g)], yq[:, third(g)], eg[:, third(g)], ALU.mult)\
                        .then_inc(k.qg_ready.sem, 1)
                    dve.wait_ge(k.nt_made.sem, k.nt_made.at(3 * i + (g + 1)))
                    dve.tensor_tensor(NT[:, third(g)], k.ps[3][:, 0:THIRD], NT[:, third(g)], ALU.mult)\
                        .then_inc(k.decayed.sem, 1)
                    dve.wait_ge(k.kv_turned.sem, k.kv_turned.at(3 * i + (g + 1)))
                    for dst, src, n in ((kbe, 6, 1), (kd, 6, 2), (vb, 7, 0)):
                        m = dve.tensor_tensor(by_tile(dst[:, third(g)]), by_tile(k.ps[src][:, 0:THIRD]),
                                              sh[:, n, 3 * g:3 * g + 3].unsqueeze(2).to_broadcast([P, 3, P]), ALU.mult)
                    m.then_inc(k.scaled.sem, 1)
                dve.wait_ge(k.decayed.sem, k.decayed.at(3 * i + 3))

                def repeated(a):
                    return a.unsqueeze(1).to_broadcast([P, 3, P])

                for g in range(3):
                    dve.tensor_tensor(by_tile(MT[:, third(g)]), by_tile(NT[:, third(g)]), repeated(level_mask[0]),
                                      ALU.mult).then_inc(k.first_mask.sem, 1)
                    dve.wait_ge(k.first_mask.sem, k.first_mask.at(3 * i + (g + 1)))
                    dve.scalar_tensor_tensor(out=by_tile(Y[:, third(g)]), in0=by_tile(MT[:, third(g)]), scalar=-1.0,
                                             in1=repeated(k.ident[:, :]), op0=ALU.mult, op1=ALU.add)\
                        .then_inc(k.y_started.sem, 1)

                def mask_level(r):
                    if r >= 3:
                        dve.wait_ge(k.p1_done.sem, k.p1_done.at(LV * i + (r - 2)))
                    g = r % 3
                    dve.tensor_tensor(by_tile(MT[:, third(g)]), by_tile(NT[:, third(g)]),
                                      repeated(level_mask[1 + r // 3]), ALU.mult).then_inc(k.masked_level.sem, 1)

                dve.wait_ge(k.y_started.sem, k.y_started.at(3 * i + 3))
                dve.wait_ge(k.x_started.sem, k.x_started.at(3 * i + 3))
                for r in range(3):
                    mask_level(r)
                for r in range(LV):
                    g = r % 3
                    dve.wait_ge(k.corrected.sem, k.corrected.at(LV * i + (r + 1)))
                    if r < LV - 3:
                        dve.tensor_tensor(X[:, third(g)], X[:, third(g)], bank(4, r)[:, 0:THIRD], ALU.subtract)
                    dve.tensor_tensor(Y[:, third(g)], Y[:, third(g)], bank(6, r)[:, 0:THIRD], ALU.subtract)\
                        .then_inc(k.level_done.sem, 1)
                    if r + 3 < LV:
                        mask_level(r + 3)
                for g in range(3):
                    dve.wait_ge(k.wu_done.sem, k.wu_done.at(3 * i + (g + 1)))
                    dve.wait_ge(k.w_ready.sem, k.w_ready.at(3 * i + (g + 1)))
                    dve.tensor_copy(u[:, third(g)], k.ps[3][:, 0:THIRD]).then_inc(k.u_ready.sem, 1)
                dve.tensor_copy(wz.rearrange("p (b m) -> p b m", b=DB)[:, :, 0:DS],
                                wT[:, SEQ:T].rearrange("p (b c) -> p b c", c=DS)).then_inc(k.wz_ready.sem, 1)
                dve.memset(S[:, 0, :], 0.0).then_inc(k.s_ready.sem, 1)
                dve.wait_ge(k.s_ready.sem, k.s_ready.at(9 * i + 1))
                for t in range(8):
                    dve.wait_ge(k.ws_done.sem, k.ws_done.at(9 * i + (t + 1)))
                    if t >= 2:
                        dve.wait_ge(k.o_done.sem, k.o_done.at(9 * i + (t - 1)))
                    dve.tensor_tensor(vw[:, t % 2, :], u[:, tile(t)], bank(2, t)[:, 0:P], ALU.subtract)\
                        .then_inc(k.vw_ready.sem, 1)
                    if t >= FIRST_TAP:
                        next_taps(1)
                    dve.wait_ge(k.kv_done.sem, k.kv_done.at(9 * i + (t + 1 + 1)))
                    if t >= 1:
                        dve.wait_ge(k.o_done.sem, k.o_done.at(9 * i + t))
                    last = tile(t).stop - 1
                    dve.scalar_tensor_tensor(out=S[:, (t + 1) % 2, :], in0=S[:, t % 2, :], scalar=eg[:, last:last + 1],
                                             in1=bank(4, t)[:, 0:P], op0=ALU.mult, op1=ALU.add)\
                        .then_inc(k.s_ready.sem, 1)
                    dve.wait_ge(k.s_ready.sem, k.s_ready.at(9 * i + (t + 2)))
                dve.wait_ge(k.ws_done.sem, k.ws_done.at(9 * i + 9))
                dve.wait_ge(k.o_done.sem, k.o_done.at(9 * i + 7))
                dve.tensor_tensor(vw[:, 0, :], u[:, tile(8)], k.ps[2][:, 0:P], ALU.subtract).then_inc(k.vw_ready.sem, 1)
                dve.wait_ge(k.vw_ready.sem, k.vw_ready.at(9 * i + 9))
                dve.tensor_tensor(v8[:], vw[:, 0:1, :].to_broadcast([P, DB, P]),
                                  streams.unsqueeze(2).to_broadcast([P, DB, P]), ALU.mult).then_inc(k.v8_ready.sem, 1)
                next_taps(3)
                dve.wait_ge(k.o_done.sem, k.o_done.at(9 * i + 9))
                dve.tensor_tensor(Sb[:], Sb[:], eg[:, SEQ:T].rearrange("p (b c) -> p b c", c=DS)[:, :, DS - 1:DS]
                                  .to_broadcast([P, DB, P]), ALU.mult).then_inc(k.s_decayed.sem, 1)
                dve.wait_ge(k.kv_done.sem, k.kv_done.at(9 * i + 10))
                dve.wait_ge(k.s_decayed.sem, k.s_decayed.at(i + 1))
                dve.tensor_tensor(Sb[:, 0:4, :], Sb[:, 0:4, :], k.ps[4].rearrange("p (b c) -> p b c", c=P), ALU.add)
                dve.tensor_tensor(Sb[:, 4:8, :], Sb[:, 4:8, :], k.ps[5].rearrange("p (b c) -> p b c", c=P), ALU.add)\
                    .then_inc(k.s_final.sem, 1)
                next_taps(1)
                for g in range(3):
                    dve.wait_ge(k.rooted.sem, k.rooted.at(9 * i + (6 + g + 1)))
                    dve.scalar_tensor_tensor(out=oT[:, third(g)], in0=oT[:, third(g)], scalar=gn[:, 0:1],
                                             in1=rr[:, (6 + g) % 2, :], op0=ALU.mult, op1=ALU.mult)\
                        .then_inc(k.o_normed.sem, 1)
                    dve.wait_ge(k.o_normed.sem, k.o_normed.at(3 * i + (g + 1)))
                    dve.tensor_tensor(oT[:, third(g)], oT[:, third(g)], z[:, third(g)], ALU.mult)\
                        .then_inc(k.o_scaled.sem, 1)
                    next_taps(2 if g == 2 else 0)
                assert final or not taps

            with dve.Fori(0, HB - 1) as i:
                turn(i, False)
            turn(HB - 1, True)

    units_done(k, HB, 4)
    for b in range(2):
        k.kv_slot[b].base += 96 * HB
    for c in range(3):
        k.pad_landed[c].base += 16 * HB
    k.z_landed.base += 16 * HB
    for sig, n in ((k.evacuated, 12), (k.dense_done, 12), (k.squared, 9), (k.lned, 9), (k.sq_summed, 9), (k.rooted, 9),
                   (k.per_ready, 1), (k.decayed, 3), (k.scaled, 3), (k.rows_spread, 3), (k.l2_done, 6), (k.grams, 3),
                   (k.kv_turned, 3), (k.y_started, 3), (k.y_turned, 3), (k.x_started, 3), (k.masked_level, LV),
                   (k.p1_ready, LV), (k.p1_done, LV), (k.level_done, LV), (k.corrected, LV), (k.w_ready, 3),
                   (k.u_ready, 3), (k.wu_done, 3), (k.s_ready, 9), (k.ws_done, 9), (k.o_copied, 9), (k.qg_ready, 3),
                   (k.vw_ready, 9), (k.kv_done, 9), (k.o_done, 9), (k.s_loaded, 48), (k.wz_ready, 1), (k.v8_ready, 1),
                   (k.pad_ready, 3), (k.silued, 4), (k.convolved, 3), (k.eg_ready, 3), (k.dt_args, 3), (k.dt_ready, 3),
                   (k.s_final, 1), (k.s_out, 32), (k.conv_loaded, 32), (k.conv_stored, 16), (k.o_scaled, 3), (k.o_normed, 3), (k.yb_stored, 16), (k.tap, 9),
                   (k.nt_made, 3), (k.first_mask, 3), (k.s_decayed, 1)):
        sig.base += n * HB


def memory_phase(nc, k, own_norm, norm, xh, xl, work):
    kv = nc.alloc_sbuf_tensor_at("m_kv", [P, 2, NMEM], F32, offset=work)
    nat = nc.alloc_sbuf_tensor_at("m_nat", [P, 2, NMEM], F32, offset=work + 8 * NMEM)
    pe_norm = {3: [lambda pe: norm.sums(pe, 0)], 5: [lambda pe: norm.sums(pe, 1)], 7: [lambda pe: norm.sums(pe, 2)]}
    act_norm = {0: [lambda act: norm.square(act, 0)], 1: [lambda act: norm.square(act, 1)],
                2: [lambda act: norm.square(act, 2)], 4: [lambda act: norm.root(act, 0), lambda act: norm.upper(act, 0)],
                6: [lambda act: norm.root(act, 1), lambda act: norm.upper(act, 1)],
                8: [lambda act: norm.root(act, 2), lambda act: norm.upper(act, 2)]}
    UNITS = 2 * KD
    with nc.Block() as block:
        @block.sync
        def _(sp):
            load_units(sp, k, k.next_unit, 1, UNITS)

        @block.gpsimd
        def _(pool):
            for j in range(UNITS):
                s = slot(j, UNITS)
                pool.wait_ge(k.unit_hi.sem, k.unit_hi.at(j + 1))
                if j >= RING:
                    pool.wait_ge(k.dense_done.sem, k.dense_done.at(last_use(j, UNITS)[1] + 1))
                pool.tensor_tensor(k.w_lo[s][:, :], k.w_raw[s][:, :], k.w_hi[s][:, :].bitcast(F32), ALU.subtract)\
                    .then_inc(k.unit_split.sem, 1)

        @block.tensor
        def _(pe):
            own_norm.tensor(pe)
            for h in range(2):
                pe.wait_ge(own_norm.s.nsplit[h].sem, own_norm.s.nsplit[h].at(1))

            def turn(j):
                pe.wait_ge(k.evacuated.sem, k.evacuated.at(j + 1 + 2))
                for h in range(2):
                    mm = pe.transpose(k.ps[2 + j % 2][:, h * P:(h + 1) * P], kv[:, j % 2, h * P:(h + 1) * P],
                                      k.ident[:, :])
                mm.then_inc(k.turned.sem, 1)

            for j in range(UNITS):
                s = slot(j, UNITS)
                pe.wait_ge(k.unit_split.sem, k.unit_split.at(j + 1))
                pe.wait_ge(k.evacuated.sem, k.evacuated.at(j + 1))
                tiles = [(k.w_hi[s][:, c * P:(c + 1) * P], k.w_lo[s][:, c * P:(c + 1) * P], xh[:, c, :], xl[:, c, :])
                         for c in range(KD)]
                product(pe, k.ps[j % 2][:, 0:NMEM], tiles, 0, NMEM).then_inc(k.dense_done.sem, 1)
                if j >= 1:
                    turn(j - 1)
                for step in pe_norm.get(j, []):
                    step(pe)
            turn(UNITS - 1)

        @block.scalar
        def _(act):
            def unit_upper(j):
                s = slot(j, UNITS)
                act.wait_ge(k.raw_landed[s].sem, k.raw_landed[s].at(16 * (sharing(j, UNITS).index(j) + 1)))
                if j >= RING:
                    act.wait_ge(k.dense_done.sem, k.dense_done.at(last_use(j, UNITS)[1] + 1))
                act.activation(k.w_hi[s][:, :], k.w_raw[s][:, :], ACT.Copy).then_inc(k.unit_hi.sem, 1)

            own_norm.scalar(act)
            act.wait_ge(k.x_loaded.sem, k.x_loaded.at(16))
            for j in range(2):
                unit_upper(j)
            for j in range(UNITS + 1):
                if j + 2 < UNITS:
                    unit_upper(j + 2)
                if j < UNITS:
                    act.wait_ge(k.dense_done.sem, k.dense_done.at(j + 1))
                    act.wait_ge(k.kv_slot[j % 2].sem, k.kv_slot[j % 2].at(32 * (j // 2) + 32))
                    act.activation(kv[:, j % 2, :], k.ps[j % 2][:, 0:NMEM], ACT.Copy).then_inc(k.evacuated.sem, 1)
                    act.wait_ge(k.evacuated.sem, k.evacuated.at(j + 1 + 2))
                    act.dma_start(k.mem_out[j], kv[:, j % 2, :]).then_inc(k.kv_slot[j % 2].sem, 16)
                if j >= 1:
                    act.wait_ge(k.turned.sem, k.turned.at(j))
                    act.activation(nat[:, (j - 1) % 2, :], k.ps[2 + (j - 1) % 2][:, 0:NMEM], ACT.Copy)\
                        .then_inc(k.pt_ready.sem, 1)
                    act.wait_ge(k.pt_ready.sem, k.pt_ready.at(j))
                    act.dma_start(k.mem_turned[j - 1], nat[:, (j - 1) % 2, :]).then_inc(k.kv_slot[(j - 1) % 2].sem, 16)
                for step in act_norm.get(j, []):
                    step(act)
            for b in range(2):
                act.wait_ge(k.kv_slot[b].sem, k.kv_slot[b].at(32 * (UNITS // 2) + 32))

        @block.vector
        def _(dve):
            own_norm.vector(dve, both=True)
            dve.wait_ge(k.x_loaded.sem, k.x_loaded.at(16))
            norm.vector(dve, both=True)

    own_norm.done()
    norm.done()
    units_done(k, 1, UNITS)
    k.x_loaded.base += 16
    n = UNITS
    for sig in (k.dense_done, k.evacuated, k.turned, k.pt_ready):
        sig.base += n
    for b in range(2):
        k.kv_slot[b].base += 16 * n


def job_order(units):
    return [(u, n) for n in range(3) for u in range(RING)] + [(u, n) for u in range(RING, units) for n in range(3)]


def used_after(order, per_job):
    return tuple(per_job * (1 + max(j for j, (u, _) in enumerate(order) if u == m)) for m in range(KD))


def load_third(eng, k, st, sources, n):
    if n >= 2:
        eng.wait_ge(k.third_split.sem, k.third_split.at(2 * (n - 1)))
    for c, src in sources:
        eng.dma_start(st[n % 2][:, c:c + 4, :], src[:, :, n * THIRD:(n + 1) * THIRD])\
            .then_inc(k.third_landed[n % 2][c // 4].sem, 16)


def third_upper(act, k, st, hi, n):
    for h in range(2):
        c = slice(4 * h, 4 * h + 4)
        act.wait_ge(k.third_landed[n % 2][h].sem, k.third_landed[n % 2][h].at(16 * (n // 2 + 1)))
        act.activation(hi[:, c, n * THIRD:(n + 1) * THIRD], st[n % 2][:, c], ACT.Copy).then_inc(k.third_hi.sem, 1)


def third_lower(dve, k, st, hi, lo, n):
    for h in range(2):
        c = slice(4 * h, 4 * h + 4)
        dve.wait_ge(k.third_hi.sem, k.third_hi.at(2 * n + h + 1))
        dve.tensor_tensor(lo[:, c, n * THIRD:(n + 1) * THIRD], st[n % 2][:, c],
                          hi[:, c, n * THIRD:(n + 1) * THIRD].bitcast(F32), ALU.subtract).then_inc(k.third_split.sem, 1)


def thirds_done(k):
    k.third_hi.base += 6
    k.third_split.base += 6
    for b in range(2):
        for h in range(2):
            k.third_landed[b][h].base += 16 * (2 - b)


def merge_phase(nc, k, sources, yh, yl, hi, lo, work, stage):
    gt = nc.alloc_sbuf_tensor_at("e_gate", [P, 2, 2, THIRD], F32, offset=work)
    a1 = nc.alloc_sbuf_tensor_at("e_a", [P, 2, THIRD], F32, offset=work + 16 * THIRD)
    b1 = nc.alloc_sbuf_tensor_at("e_b", [P, 2, THIRD], F32, offset=work + 24 * THIRD)
    m1 = nc.alloc_sbuf_tensor_at("e_m", [P, 2, THIRD], F32, offset=work + 32 * THIRD)
    st = [nc.alloc_sbuf_tensor_at(f"e_st{b}", [P, KD, THIRD], F32, offset=at + RING * 4 * T) for b, at in enumerate(stage)]
    order = job_order(KD)
    JOBS = len(order)

    def chunk(a, j):
        m, n = order[j]
        return a[:, m, n * THIRD:(n + 1) * THIRD]

    with nc.Block() as block:
        @block.sync
        def _(sp):
            load_units(sp, k, k.next_unit, 1, KD, lambda _: load_third(sp, k, st, sources, 0),
                       lambda: load_third(sp, k, st, sources, 1))

        @block.gpsimd
        def _(pool):
            split_units(pool, k, 1, used_after(order, 2))

        @block.tensor
        def _(pe):
            for j, (m, n) in enumerate(order):
                if n == 0:
                    pe.wait_ge(k.unit_split.sem, k.unit_split.at(m + 1))
                pe.wait_ge(k.merged.sem, k.merged.at(j + 1))
                s = m % RING
                for ab in range(2):
                    if m < RING:
                        pe.wait_ge(k.third_split.sem, k.third_split.at(2 * n + ab + 1))
                    tiles = [(k.w_hi[s][:, c * P:(c + 1) * P], k.w_lo[s][:, c * P:(c + 1) * P], yh[:, c, :], yl[:, c, :])
                             for c in range(4 * ab, 4 * ab + 4)]
                    product(pe, k.ps[2 * (j % 2) + ab][:, 0:THIRD], tiles, n * THIRD, (n + 1) * THIRD)\
                        .then_inc(k.dense_done.sem, 1)

        @block.scalar
        def _(act):
            def load(j):
                m, n = order[j]
                for ab in range(2):
                    act.dma_start(gt[:, j % 2, ab, :], k.gate_dram[8 * ab + m][:, n * THIRD:(n + 1) * THIRD])\
                        .then_inc(k.kv_slot[j % 2].sem, 16)

            def gates(j):
                act.wait_ge(k.kv_slot[j % 2].sem, k.kv_slot[j % 2].at(32 * (j // 2) + 32 + 32))
                act.activation(gt[:, j % 2], gt[:, j % 2], ACT.Sigmoid).then_inc(k.gate_sigmoid.sem, 1)

            load(0)
            load(1)
            third_upper(act, k, st, yh, 0)
            gates(0)
            load_third(act, k, st, sources, 2)
            third_upper(act, k, st, yh, 1)
            for j in range(JOBS):
                if j == RING:
                    third_upper(act, k, st, yh, 2)
                if j + 1 < JOBS:
                    gates(j + 1)
                act.wait_ge(k.merged.sem, k.merged.at(j + 1 + 2))
                act.activation(chunk(hi, j), m1[:, j % 2, :], ACT.Copy).then_inc(k.merged_hi.sem, 1)
                if j + 2 < JOBS:
                    load(j + 2)

        @block.vector
        def _(dve):
            third_lower(dve, k, st, yh, yl, 0)
            third_lower(dve, k, st, yh, yl, 1)
            for j in range(JOBS):
                if j == RING:
                    third_lower(dve, k, st, yh, yl, 2)
                dve.wait_ge(k.dense_done.sem, k.dense_done.at(2 * j + 2))
                dve.wait_ge(k.gate_sigmoid.sem, k.gate_sigmoid.at(j + 1))
                dve.tensor_tensor(a1[:, j % 2, :], k.ps[2 * (j % 2)][:, 0:THIRD], gt[:, j % 2, 0, :], ALU.mult)
                dve.tensor_tensor(b1[:, j % 2, :], k.ps[2 * (j % 2) + 1][:, 0:THIRD], gt[:, j % 2, 1, :], ALU.mult)\
                    .then_inc(k.gated.sem, 1)
                dve.wait_ge(k.gated.sem, k.gated.at(j + 1))
                if j >= 2:
                    dve.wait_ge(k.merged_hi.sem, k.merged_hi.at(j - 1))
                dve.tensor_tensor(m1[:, j % 2, :], a1[:, j % 2, :], b1[:, j % 2, :], ALU.add).then_inc(k.merged.sem, 1)
                dve.wait_ge(k.merged_hi.sem, k.merged_hi.at(j + 1))
                dve.tensor_tensor(chunk(lo, j), m1[:, j % 2, :], chunk(hi, j).bitcast(F32), ALU.subtract)\
                    .then_inc(k.merged_split.sem, 1)

    units_done(k, 1, KD)
    thirds_done(k)
    k.dense_done.base += 2 * JOBS
    for sig in (k.merged, k.gated, k.gate_sigmoid, k.merged_hi, k.merged_split):
        sig.base += JOBS
    for b in range(2):
        k.kv_slot[b].base += 16 * JOBS


def residual_phase(nc, k, x, xh, xl, sources=None, work=None, x_from=None):
    order = job_order(KD)
    if sources:
        st = [nc.alloc_sbuf_tensor_at(f"r_st{b}", [P, KD, THIRD], F32, offset=work + 4 * KD * THIRD * b) for b in range(2)]

    with nc.Block() as block:
        @block.sync
        def _(sp):
            def third(n):
                if sources:
                    load_third(sp, k, st, sources, n)

            load_units(sp, k, k.next_unit, 1, KD, lambda _: third(0), lambda: third(1))

        @block.gpsimd
        def _(pool):
            split_units(pool, k, 1, used_after(order, 1))

        @block.tensor
        def _(pe):
            for j, (m, n) in enumerate(order):
                if n == 0:
                    pe.wait_ge(k.unit_split.sem, k.unit_split.at(m + 1))
                if sources and m < RING:
                    pe.wait_ge(k.third_split.sem, k.third_split.at(2 * n + 2))
                pe.wait_ge(k.x_added.sem, k.x_added.at(j + 1))
                s = m % RING
                tiles = [(k.w_hi[s][:, c * P:(c + 1) * P], k.w_lo[s][:, c * P:(c + 1) * P], xh[:, c, :], xl[:, c, :])
                         for c in range(KD)]
                product(pe, k.ps[j % NPS][:, 0:THIRD], tiles, n * THIRD, (n + 1) * THIRD).then_inc(k.dense_done.sem, 1)

        @block.scalar
        def _(act):
            if x_from is not None:
                act.wait_ge(k.unit_split.sem, k.unit_split.at(2))
                for c in range(KD):
                    act.dma_start(x[:, c, :], x_from[c]).then_inc(k.x_landed[c].sem, 16)
            if sources:
                third_upper(act, k, st, xh, 0)
                load_third(act, k, st, sources, 2)
                third_upper(act, k, st, xh, 1)
                third_upper(act, k, st, xh, 2)

        @block.vector
        def _(dve):
            if sources:
                third_lower(dve, k, st, xh, xl, 0)
                third_lower(dve, k, st, xh, xl, 1)
            for j, (m, n) in enumerate(order):
                if sources and j == RING:
                    third_lower(dve, k, st, xh, xl, 2)
                dve.wait_ge(k.dense_done.sem, k.dense_done.at(j + 1))
                if x_from is not None and n == 0:
                    dve.wait_ge(k.x_landed[m].sem, k.x_landed[m].at(16))
                xs = x[:, m, n * THIRD:(n + 1) * THIRD]
                dve.tensor_tensor(xs, xs, k.ps[j % NPS][:, 0:THIRD], ALU.add).then_inc(k.x_added.sem, 1)

    units_done(k, 1, KD)
    if sources:
        thirds_done(k)
    if x_from is not None:
        for c in range(KD):
            k.x_landed[c].base += 16
    for sig in (k.dense_done, k.x_added):
        sig.base += len(order)


def cross_phase(nc, k, make_norm, xh, xl, room1, room2):
    at = {1: room1, 2: room2}

    def sb(name, room, shape):
        t = nc.alloc_sbuf_tensor_at(name, shape, F32, offset=at[room])
        at[room] += (4 * int(np.prod(shape[1:])) + 31) // 32 * 32
        return t

    q, qn = sb("x_q", 1, [P, 2, T]), sb("x_q_next", 1, [P, 2, T])
    mk, mv = sb("x_mk", 1, [P, 2, NMEM]), sb("x_mv", 1, [P, 2, 2, P])
    qz = sb("x_qz", 1, [P, 2, DB, 32])
    sk = sb("x_sk", 2, [P, 2, DB, NMEM])
    sv = [sb("x_sv0", 1, [P, 4, 2, DHX]), sb("x_sv1", 2, [P, 4, 2, DHX])]
    sc, pt = sb("x_sc", 1, [P, 2, NMEM]), sb("x_pt", 1, [P, 2, 2, P])
    oc = sb("x_o", 2, [P, 2, 2, P])
    nmax, rsum, rinv = (sb(n, 2, [P, 2]) for n in ("x_nmax", "x_rsum", "x_rinv"))
    STEPS = 9
    filler = Filler(0, 2, [32] + [8] * 8 + [0, 8] + [4] * 8 + [8], ahead=1)
    norm = make_norm(room2, room1)

    def bank(a, b):
        return k.ps[a + b % 2]

    with nc.Block() as block:
        @block.sync
        def _(sp):
            load_units(sp, k, k.next_unit, HX, 2)

        @block.gpsimd
        def _(pool):
            split_units(pool, k, HX, (3, 6), norm)

        @block.tensor
        def _(pe):
            def scores(i, s):
                pe.wait_ge(k.score_read.sem, k.score_read.at(STEPS * i + (s + 1)))
                o = bank(2, s)
                if s < 8:
                    for c in range(2):
                        mm = pe.matmul(o[:, 0:NMEM], q[:, c, s * P:(s + 1) * P], mk[:, c, :], start=(c == 0),
                                       stop=(c == 1))
                else:
                    for b in range(DB):
                        r = 32 * (b // 2)
                        for c in range(2):
                            mm = pe.matmul(o[r:r + 32, 0:NMEM], qz[:, c, b, :], sk[:, c, b, :],
                                           start=(b % 2 == 0 and c == 0), stop=(b % 2 == 1 and c == 1),
                                           tile_position=(0, r))
                mm.then_inc(k.scored.sem, 1)

            def turn_probs(i, s):
                pe.wait_ge(k.normed.sem, k.normed.at(STEPS * i + (s + 1)))
                if s >= 2:
                    pe.wait_ge(k.pt_ready.sem, k.pt_ready.at(STEPS * i + (s - 1)))
                for j in range(2):
                    mm = pe.transpose(bank(4, s)[:, j * P:(j + 1) * P], sc[:, s % 2, j * P:(j + 1) * P], k.ident[:, :])
                mm.then_inc(k.turned.sem, 1)

            def values(i, s, fill):
                pe.wait_ge(k.pt_ready.sem, k.pt_ready.at(STEPS * i + (s + 1)))
                if s >= 2:
                    pe.wait_ge(k.o_read.sem, k.o_read.at(STEPS * i + (s - 1)))
                o = bank(6, s)
                for c in range(2):
                    if s < 8:
                        for j in range(2):
                            mm = pe.matmul(o[:, c * P:(c + 1) * P], mv[:, c, j, :], pt[:, s % 2, j, :],
                                           start=(j == 0), stop=(j == 1))
                        continue
                    for b in range(DB):
                        for j in range(2):
                            mm = pe.matmul(o[:, c * P + DS * b:c * P + DS * (b + 1)],
                                           sv[b // 4][:, b % 4, j, c * P:(c + 1) * P], pt[:, s % 2, j, DS * b:DS * (b + 1)],
                                           start=(j == 0), stop=(j == 1))
                        if c == 1 and b == DB - 1:
                            mm.then_inc(k.valued.sem, 1)
                        if fill and b % 2 == 1:
                            filler.products(k, pe, i, 11 + 4 * c + b // 2, xh, xl)
                if s < 8:
                    mm.then_inc(k.valued.sem, 1)

            norm.tensor(pe)
            for g in range(6):
                if g < 3:
                    pe.wait_ge(norm.s.nsplit[0].sem, norm.s.nsplit[0].at(g + 1))
                    pe.wait_ge(norm.s.nsplit[1].sem, norm.s.nsplit[1].at(g + 1))
                u, n = g // 3, g % 3
                if n == 0:
                    pe.wait_ge(k.unit_split.sem, k.unit_split.at(u + 1))
                pe.wait_ge(k.evacuated.sem, k.evacuated.at(g + 1))
                tiles = [(k.w_hi[u][:, c * P:(c + 1) * P], k.w_lo[u][:, c * P:(c + 1) * P], xh[:, c, :], xl[:, c, :])
                         for c in range(KD)]
                product(pe, k.ps[g % 2][:, 0:THIRD], tiles, n * THIRD, (n + 1) * THIRD).then_inc(k.dense_done.sem, 1)

            def turn(i, fill):
                if fill:
                    filler.products(k, pe, i, 0, xh, xl)
                pe.wait_ge(k.q_moved.sem, k.q_moved.at(2 * i + 2))
                pe.wait_ge(k.a_loaded.sem, k.a_loaded.at(32 * i + 32))
                for s in range(STEPS + 2):
                    if s == 8:
                        pe.wait_ge(k.streams_loaded.sem, k.streams_loaded.at(80 * i + 80))
                        pe.wait_ge(k.qbd_ready.sem, k.qbd_ready.at(i + 1))
                    if s < STEPS:
                        scores(i, s)
                    if s >= 2:
                        values(i, s - 2, fill)
                    if fill and s <= STEPS:
                        filler.products(k, pe, i, s + 1, xh, xl)
                    if 1 <= s <= STEPS:
                        turn_probs(i, s - 1)
                if fill:
                    filler.products(k, pe, i, 19, xh, xl)

            with pe.Fori(0, HX - 1) as i:
                turn(i, True)
            turn(HX - 1, False)

        @block.scalar
        def _(act):
            def evacuate(i, g, ahead):
                act.wait_ge(k.dense_done.sem, k.dense_done.at(6 * i + (6 * ahead + g + 1)))
                act.activation(qn[:, g // 3, g % 3 * THIRD:(g % 3 + 1) * THIRD], k.ps[g % 2][:, 0:THIRD], ACT.Copy,
                               scale=DHX ** -0.5).then_inc(k.evacuated.sem, 1)

            norm.scalar(act)
            for g in range(6):
                evacuate(0, g, 0)
            for h in range(2):
                act.wait_ge(norm.s.nsplit[h].sem, norm.s.nsplit[h].at(norm.nb))

            def turn(i, fill):
                act.wait_ge(k.valued.sem, k.valued.at(STEPS * i + 1))
                for dst, src in ((mk[:], k.mem_out[bass.ds(2 * i, 2)].rearrange("c p m -> p c m")),
                                 (mv[:].rearrange("p c j d -> p c (j d)"),
                                  k.mem_turned[bass.ds(2 * i + 8, 2)].rearrange("c p m -> p c m"))):
                    act.dma_start(dst, src).then_inc(k.a_loaded.sem, 16)
                act.wait_ge(k.evacuated.sem, k.evacuated.at(6 * i + 8))
                act.activation(q[:, 0, :], qn[:, 0, :], ACT.Copy).then_inc(k.q_moved.sem, 1)
                for dst, src in ((sk[:, 0], k.mem_k[i][:, 0]), (sk[:, 1], k.mem_k[i][:, 1]),
                                 (sv[0][:, 0:4], k.mem_v[i][:, 0:4]), (sv[1][:, 0:2], k.mem_v[i][:, 4:6]),
                                 (sv[1][:, 2:4], k.mem_v[i][:, 6:8])):
                    act.dma_start(dst, src).then_inc(k.streams_loaded.sem, 16)

                def exps(s):
                    act.wait_ge(k.maxed.sem, k.maxed.at(STEPS * i + (s + 1)))
                    if s >= 2:
                        act.wait_ge(k.turned.sem, k.turned.at(STEPS * i + (s - 1)))
                    b = s % 2
                    act.activation(sc[:, b, :], bank(2, s)[:, 0:NMEM], ACT.Exp, bias=nmax[:, b:b + 1],
                                   accum_out=rsum[:, b:b + 1]).then_inc(k.score_read.sem, 1)

                def copy_turned(s):
                    act.wait_ge(k.turned.sem, k.turned.at(STEPS * i + (s + 1)))
                    if s >= 2:
                        act.wait_ge(k.valued.sem, k.valued.at(STEPS * i + (s - 1 + 1)))
                    act.activation(pt[:, s % 2].rearrange("p j c -> p (j c)"), bank(4, s)[:, 0:NMEM], ACT.Copy)\
                        .then_inc(k.pt_ready.sem, 1)

                def copy_o(s):
                    b = s % 2
                    act.wait_ge(k.valued.sem, k.valued.at(STEPS * i + (s + 1 + 1)))
                    act.wait_ge(k.kv_slot[b].sem, k.kv_slot[b].at(16 * (5 - b) * i + (16 * (s // 2) + 32)))
                    act.activation(oc[:, b], bank(6, s)[:, 0:2 * P].rearrange("p (c t) -> p c t", c=2), ACT.Copy)\
                        .then_inc(k.o_read.sem, 1)
                    act.wait_ge(k.o_read.sem, k.o_read.at(STEPS * i + (s + 1)))
                    act.dma_start(k.o_dram[bass.ds(2 * i, 2), :, s * P:(s + 1) * P].rearrange("c p t -> p c t"), oc[:, b])\
                        .then_inc(k.kv_slot[b].sem, 16)

                for s in range(STEPS + 3):
                    if fill:
                        for g in filler.finished(s, 8 if s == 11 else 1):
                            act.wait_ge(k.q_moved.sem, k.q_moved.at(2 * i + 2))
                            evacuate(i, g, 1)
                    if s < STEPS:
                        exps(s)
                    if 1 <= s <= STEPS:
                        copy_turned(s - 1)
                    if s >= 3:
                        copy_o(s - 3)
                if fill:
                    for g in filler.finished(19):
                        evacuate(i, g, 1)

            with act.Fori(0, HX - 1) as i:
                turn(i, True)
            turn(HX - 1, False)
            for b in range(2):
                act.wait_ge(k.kv_slot[b].sem, k.kv_slot[b].at(16 * (5 - b) * HX + 32))

        @block.vector
        def _(dve):
            norm.vector(dve)
            dve.memset(qz[:], 0.0).then_inc(k.qbd_zero.sem, 1)
            dve.wait_ge(k.qbd_zero.sem, k.qbd_zero.at(1))
            with dve.Fori(0, HX) as i:
                dve.wait_ge(k.evacuated.sem, k.evacuated.at(6 * i + 8))
                dve.wait_ge(k.valued.sem, k.valued.at(STEPS * i + 1))
                dve.tensor_copy(q[:, 1, :], qn[:, 1, :]).then_inc(k.q_moved.sem, 1)
                dve.wait_ge(k.q_moved.sem, k.q_moved.at(2 * i + 2))
                for c in range(2):
                    qs = q[:, c, SEQ:T].rearrange("p (b w c) -> p w b c", w=2, c=DS)
                    for odd in range(2):
                        m = dve.tensor_copy(qz[:, c].rearrange("p (b w) c -> p w b c", w=2)[:, odd, :,
                                                                                              DS * odd:DS * (odd + 1)],
                                            qs[:, odd])
                m.then_inc(k.qbd_ready.sem, 1)

                def logits(s):
                    dve.wait_ge(k.scored.sem, k.scored.at(STEPS * i + (s + 1)))
                    if s >= 2:
                        dve.wait_ge(k.score_read.sem, k.score_read.at(STEPS * i + (s - 1 + 2)))
                    dve.tensor_reduce(nmax[:, s % 2:s % 2 + 1], bank(2, s)[:, 0:NMEM], AX_X, ALU.max, negate=True)\
                        .then_inc(k.maxed.sem, 1)

                def normalise(s):
                    b = s % 2
                    dve.wait_ge(k.score_read.sem, k.score_read.at(STEPS * i + (s + 1 + 2)))
                    dve.reciprocal(rinv[:, b:b + 1], rsum[:, b:b + 1]).then_inc(k.inverted.sem, 1)
                    dve.wait_ge(k.inverted.sem, k.inverted.at(STEPS * i + (s + 1)))
                    dve.tensor_scalar(sc[:, b, :], sc[:, b, :], rinv[:, b:b + 1], None, ALU.mult)\
                        .then_inc(k.normed.sem, 1)

                for s in range(STEPS + 1):
                    if s < STEPS:
                        logits(s)
                    if s >= 1:
                        normalise(s - 1)

    units_done(k, HX, 2)
    norm.done()
    k.qbd_zero.base += 1
    for sig, n in ((k.dense_done, 6), (k.evacuated, 6), (k.scored, STEPS), (k.maxed, STEPS), (k.score_read, STEPS),
                   (k.inverted, STEPS), (k.normed, STEPS), (k.turned, STEPS), (k.pt_ready, STEPS), (k.valued, STEPS),
                   (k.o_read, STEPS), (k.a_loaded, 32), (k.streams_loaded, 80), (k.qbd_ready, 1), (k.q_moved, 2),
                   (k.kv_slot[0], 80), (k.kv_slot[1], 64)):
        sig.base += n * HX




OUTPUTS = {"y_out": (KD, P, T), "a_k_out": (4, P, T), "a_v_out": (4, P, T), "conv_out": (HB, P, 3, (DB + 1) * (CW - 1)),
           "p_s_out": (HB, P, P), "s_s_out": (HB, P, DB, P), "mem_out": (2 * KD, P, NMEM)}
SCRATCH = {"bias_dram": (P, HA * NBIAS + 256), "ya_dram": (4, P, T), "yb_dram": (4, P, T), "x_dram": (KD, P, T),
           "proj_dram": (4 * HB, P, PADDED), "gate_dram": (2 * KD, P, T), "mem_turned": (2 * KD, P, NMEM), "o_dram": (KD, P, T)}


def by_frame(a):
    return a.rearrange("c p t -> p c t")


def hybrid_layer(nc, io):
    with ExitStack() as ctx:
        k = Core(nc, ctx)
        k.units, k.xt, k.memt, k.gains_dram, k.ident_dram = (io[n] for n in ("units", "xt", "memt", "gains_dram",
                                                                             "ident_dram"))
        k.table, k.k_cache, k.v_cache = io["table"], io["k_cache"], io["v_cache"]
        k.b_consts, k.w_beta_decay, k.a_log, k.dt_bias = (io[n] for n in ("b_consts", "w_beta_decay", "a_log", "dt_bias"))
        k.b_gain, k.conv_state, k.conv_w, k.state_s = io["b_gain"], io["conv_state"], io["conv_w"], io["state_s"]
        k.mem_k, k.mem_v = io["mem_k"], io["mem_v"]
        k.y_out, k.a_k_out, k.a_v_out, k.conv_out = io["y_out"], io["a_k_out"], io["a_v_out"], io["conv_out"]
        k.p_s_out, k.s_s_out, k.mem_out = io["p_s_out"], io["s_s_out"], io["mem_out"]
        k.bias_dram, k.ya_dram, k.yb_dram, k.x_dram = io["bias_dram"], io["ya_dram"], io["yb_dram"], io["x_dram"]
        k.proj_dram = io["proj_dram"]
        k.gate_dram, k.mem_turned, k.o_dram = io["gate_dram"], io["mem_turned"], io["o_dram"]
        k.bias_pitch = HA * NBIAS + 256
        k.bias_dram_flat = k.bias_dram.rearrange("p m -> (p m)")
        big = KD * T * 4
        r1 = k.arena
        r2 = r1 + 2 * big

        def split_pair(name, at):
            return (nc.alloc_sbuf_tensor_at(name + "_hi", [P, KD, T], F32R, offset=at),
                    nc.alloc_sbuf_tensor_at(name + "_lo", [P, KD, T], F32R, offset=at + big))

        xh1, xl1 = split_pair("x1", r1)
        xh2, xl2 = split_pair("x2", r2)
        x_early = nc.alloc_sbuf_tensor_at("x_early", [P, KD, T], F32, offset=r2)
        x_late = nc.alloc_sbuf_tensor_at("x_late", [P, KD, T], F32, offset=r1)
        mem = nc.alloc_sbuf_tensor_at("mem", [P, KD, NMEM], F32, offset=r2 + big)
        mh, ml = (nc.alloc_sbuf_tensor_at(n, [P, KD, NMEM], F32R, offset=r2 + big + 4 * KD * NMEM * (1 + j))
                  for j, n in enumerate(("mem_hi", "mem_lo")))

        def gain(n):
            return k.gains[:, n * KD:(n + 1) * KD]

        with nc.Block() as block:
            @block.sync
            def _(sp):
                for dst, src in ((mem[:], by_frame(k.memt)), (k.gains[:], k.gains_dram), (k.ident[:], k.ident_dram)):
                    sp.dma_start(dst, src).then_inc(k.loaded.sem, 16)
                sp.dma_start(x_early[:], by_frame(k.xt)).then_inc(k.x_loaded.sem, 16)
                sp.wait_ge(k.loaded.sem, k.loaded.at(48))
                for s, n in k.tokens:
                    sp.sem_inc(s.sem, n)

            @block.vector
            def _(dve):
                dve.memset(k.ones[:, :], 1.0)
                dve.memset(k.eps[:, :], EPS)
                dve.memset(k.zero[:, :], 0.0)

        k.loaded.base += 48

        def norm(name, x, n, hi, lo, squares_at, work, rinv_at=None, out=None):
            return Norm(nc, k, k.norm, name, x, gain(n), hi, lo, work, T, THIRD, squares_at, rinv_at, out)

        work = r2 + big + 12 * KD * NMEM
        memory_phase(nc, k, Norm(nc, k, k.memory_norm, "nm", mem, gain(4), mh, ml, work + 16 * NMEM, NMEM, NMEM,
                                   r2 + big + 4 * KD * NMEM),
                     norm("n1", x_early, 0, xh1, xl1, r1, work + 16 * NMEM), mh, ml, work)
        work = r2 + big
        ffn_phase(nc, k, "f1", None, x_early, xh1, xl1, work, BiasRows(nc, k, work + 23 * T))
        decay = Decay(nc, k)
        attention_phase(nc, k, lambda work: norm("n2", x_early, 1, xh1, xl1, r1, work), decay, xh1, xl1, x_early, k.x_dram, r2)
        delta_phase(nc, k, decay, xh1, xl1, r2)
        merge_phase(nc, k, [(0, by_frame(k.ya_dram)), (4, by_frame(k.yb_dram))], xh1, xl1, xh2, xl2, r2 + 2 * big,
                    (r2, r2 + big))
        residual_phase(nc, k, x_late, xh2, xl2, x_from=k.x_dram)
        work = r1 + big
        cross_phase(nc, k, lambda work, rinv_at: norm("n3", x_late, 2, xh2, xl2, r2, work, rinv_at), xh2, xl2, work,
                    r2 + 2 * big)
        o = by_frame(k.o_dram)
        residual_phase(nc, k, x_late, xh2, xl2, sources=[(0, o[:, 0:4]), (4, o[:, 4:8])], work=work)
        ffn_phase(nc, k, "f2", norm("n4", x_late, 3, xh2, xl2, r2, r2 + 2 * big, work + 24 * T), x_late, xh2, xl2, work)
        last_norm_phase(nc, k, norm("n5", x_late, 5, None, None, r2, work, out=by_frame(k.y_out)))



def stationary(w):
    kk, m = w.shape
    return w.reshape(kk // P, P, m // P, P).transpose(2, 1, 0, 3).reshape(m // P, P, kk)


def weight_units(a):
    units = list(stationary(a["xattn_wk"])) + list(stationary(a["xattn_wv"]))

    def ffn(n):
        g, u, d = stationary(a[n + "_w_gate"]), stationary(a[n + "_w_up"]), a[n + "_w_down"].reshape(NFF, P, D)
        for i in range(0, NFF, 2):
            units.extend([g[i], u[i], g[i + 1], u[i + 1], d[i], d[i + 1]])

    ffn("ffn1")
    w_in = a["w_in"]
    wa, wb = 3 * HA * DHA, 4 * HB * DHB
    mixer_a = stationary(w_in[:, 0:wa])
    mixer_b = stationary(w_in[:, wa:wa + wb])
    for p in range(4):
        units.extend([mixer_a[4 * j + p] for j in range(3)] + [mixer_b[4 * j + p] for j in range(4)])
    units.extend(stationary(w_in[:, wa + wb + 2 * HB:]))
    units.extend(np.concatenate(pair, axis=1) for pair in zip(stationary(a["w_branch_a"]), stationary(a["w_branch_b"])))
    for n in ("w_mix_out", "xattn_wq", "xattn_wo"):
        units.extend(stationary(a[n]))
    ffn("ffn2")
    return np.stack(units)


def kernel(**inputs):
    import concourse.bacc as bacc
    from concourse.bass_utils import run_bass_kernel_spmd as run

    def features(x):
        return x.reshape(-1, D).T.reshape(KD, P, -1)

    a = {n: np.asarray(v) for n, v in inputs.items()}
    for n in a:
        if n not in ("x_prompt", "x_sample", "mem_prompt", "final_norm"):
            a[n] = a[n][0]
    wa, wb = 3 * HA * DHA, 4 * HB * DHB
    arrays = {
        "units": weight_units(a),
        "xt": np.concatenate([features(a["x_prompt"]), features(a["x_sample"])], axis=2),
        "memt": features(a["mem_prompt"]),
        "gains_dram": np.concatenate([a[n].reshape(KD, P).T for n in ("ffn1_norm", "mix_norm", "xattn_norm",
                                                                      "ffn2_norm", "mem_norm", "final_norm")], axis=1),
        "ident_dram": np.eye(P, dtype=np.float32),
        "table": a["a_rel_bias"][:, ::-1],
        "k_cache": a["cache_a_k"].reshape(DB, REACH, 4, P).transpose(2, 3, 0, 1),
        "v_cache": a["cache_a_v"].reshape(DB, 4, P, 4, P).transpose(3, 2, 0, 1, 4),
        "b_consts": delta_constants(),
        "w_beta_decay": a["w_in"][:, wa + wb:wa + wb + 2 * HB].reshape(KD, P, 2 * HB).transpose(1, 0, 2),
        "a_log": a["b_a_log"].reshape(HB), "dt_bias": a["b_dt_bias"].reshape(HB),
        "b_gain": a["b_out_norm"].reshape(P, 1),
        "conv_state": a["state_b_conv"].reshape(DB, CW - 1, 3, HB, P).transpose(3, 4, 2, 0, 1),
        "conv_w": a["b_conv_w"].reshape(CW, 3, HB, P).transpose(2, 3, 1, 0),
        "state_s": a["state_b_s"].transpose(1, 2, 0, 3),
        "mem_k": a["cache_mem_k"].reshape(DB, NMEM, HX, 2, P).transpose(2, 4, 3, 0, 1),
        "mem_v": a["cache_mem_v"].reshape(DB, 2, P, HX, DHX).transpose(3, 2, 0, 1, 4),
    }
    arrays = {n: np.ascontiguousarray(v) for n, v in arrays.items()}
    nc = bacc.Bacc("TRN2", target_bir_lowering=False, num_devices=1)
    io = {n: nc.dram_tensor(n, v.shape, F32, kind="ExternalInput").ap() for n, v in arrays.items()}
    for n, shape in OUTPUTS.items():
        io[n] = nc.dram_tensor(n, shape, F32, kind="ExternalOutput").ap()
    for n, shape in SCRATCH.items():
        io[n] = nc.dram_tensor(n, shape, F32, kind="Internal").ap()
    hybrid_layer(nc, io)
    r = run(nc, [arrays], core_ids=[0]).results[0]

    def frames(o):
        o = o.reshape(-1, T).T
        return o[:SEQ], o[SEQ:]

    yp, ys = frames(r["y_out"])
    kp, ks = frames(r["a_k_out"])
    vp, vs = frames(r["a_v_out"])
    conv = r["conv_out"].reshape(HB, P, 3, DB + 1, CW - 1).transpose(3, 4, 2, 0, 1).reshape(DB + 1, CW - 1, -1)
    mk, mv = (r["mem_out"][n * KD:(n + 1) * KD].reshape(D, NMEM).T.reshape(1, 1, NMEM, HX, DHX) for n in range(2))
    keep = min(REACH, SEQ)
    return (yp.reshape(1, SEQ, D), ys.reshape(DB, DS, D),
            kp[SEQ - keep:].reshape(1, 1, keep, HA, DHA), vp[SEQ - keep:].reshape(1, 1, keep, HA, DHA),
            conv[None, 0:1], r["p_s_out"][None, None], mk, mv,
            ks.reshape(1, DB, DS, HA, DHA), vs.reshape(1, DB, DS, HA, DHA),
            conv[None, 1:], r["s_s_out"].transpose(2, 0, 1, 3)[None])
```
